# Optimizing a Trainium2 kernel written in Bass

```python
import jax, jax.numpy as jnp
from jax import lax
import numpy as np

D_MODEL = 1024
BATCH = 1
SEQ = 512
DEPTH = 1
DEC_BATCH = 8
DEC_SEQ = 1
PAST_LEN = 4096
PAGE_SIZE = 128

MIX_WIDTH = D_MODEL
POOL_WIDTH = MIX_WIDTH // 2
POOL_WINDOWS = (2, 4, 8, 16)
N_POOL_GROUPS = len(POOL_WINDOWS)
POOL_GROUP = POOL_WIDTH // N_POOL_GROUPS
POOL_HIST = max(POOL_WINDOWS) - 1
HG_WIDTH = MIX_WIDTH - POOL_WIDTH
HG_HEAD_DIM = 128
HG_HEADS = HG_WIDTH // HG_HEAD_DIM
CHUNK = 64
IN_WIDTH = POOL_WIDTH + 4 * HG_WIDTH
N_EXPERTS = 64
TOP_K = 8
N_GROUPS = 8
TOPK_GROUPS = 4
D_EXPERT = 256
ROUTED_SCALE = 2.5
MOE_BLOCK = 128
EPS = 1e-6

kernel_name = "hybrid_pool_hgrn2_moe_decoder_step"

def rms_norm(x, g):
    xf = x.astype(jnp.float32)
    y = xf * lax.rsqrt(jnp.mean(xf * xf, axis=-1, keepdims=True) + EPS)
    return (y * g.astype(jnp.float32)).astype(x.dtype)

def ada_mod(c, w_ada, b_ada):
    m = jax.nn.silu(c) @ w_ada + b_ada
    return jnp.split(m[:, None, :], 6, axis=-1)

def pool_mix(u_ext, pos0, w_pool, pool_scale):
    B, tot, _ = u_ext.shape
    L = tot - POOL_HIST
    cs = jnp.cumsum(u_ext.astype(jnp.float32), axis=1)
    cs = jnp.pad(cs, ((0, 0), (1, 0), (0, 0)))
    end = cs[:, POOL_HIST + 1:]
    u = u_ext[:, POOL_HIST:].astype(jnp.float32)
    pos = pos0 + jnp.arange(L)
    outs = []
    for g, w in enumerate(POOL_WINDOWS):
        sl = slice(g * POOL_GROUP, (g + 1) * POOL_GROUP)
        start = cs[:, POOL_HIST + 1 - w:POOL_HIST + 1 - w + L, sl]
        cnt = jnp.minimum(pos + 1, w).astype(jnp.float32)[None, :, None]
        outs.append((end[..., sl] - start) / cnt - u[..., sl])
    d = jnp.stack(outs, axis=2)
    y = jnp.einsum('blgc,gcd->blgd', d, w_pool.astype(jnp.float32)).reshape(B, L, POOL_WIDTH)
    return (y * pool_scale.astype(jnp.float32)).astype(u_ext.dtype)

def hgrn2_chunked(q, logf, k, v, s0):
    B, T, H, DK = q.shape
    n = T // CHUNK

    def to_chunks(a):
        return a.reshape(B, n, CHUNK, H, a.shape[-1]).transpose(1, 0, 3, 2, 4)

    causal = jnp.tril(jnp.ones((CHUNK, CHUNK), bool))[:, :, None]

    def step(S, inp):
        qc, gc, kc, vc = inp
        b = jnp.cumsum(gc, axis=2)
        diff = b[:, :, :, None, :] - b[:, :, None, :, :]
        decay = jnp.exp(jnp.where(causal, diff, -jnp.inf))
        A = jnp.einsum('bhik,bhijk,bhjk->bhij', qc, decay, kc)
        o = jnp.einsum('bhij,bhjv->bhiv', A, vc) + jnp.einsum('bhik,bhkv->bhiv', qc * jnp.exp(b), S)
        b_last = b[:, :, -1:, :]
        S = jnp.exp(b_last[:, :, 0, :])[..., None] * S + jnp.einsum('bhjk,bhjv->bhkv', kc * jnp.exp(b_last - b), vc)
        return S, o

    S, o = lax.scan(step, s0, (to_chunks(q), to_chunks(logf), to_chunks(k), to_chunks(v)))
    o = o.transpose(1, 0, 3, 2, 4).reshape(B, T, H, v.shape[-1])
    return o, S

def hgrn2_recurrent(q, logf, k, v, s0):
    def step(S, inp):
        qt, gt, kt, vt = inp
        S = jnp.exp(gt)[..., None] * S + kt[..., None] * vt[..., None, :]
        return S, jnp.einsum('bhk,bhkv->bhv', qt, S)

    S, o = lax.scan(step, s0, tuple(a.transpose(1, 0, 2, 3) for a in (q, logf, k, v)))
    return o.transpose(1, 0, 2, 3), S

def moe_ffn(h, w_router, router_bias, w1, w3, w2, ws1, ws3, ws2):
    T, D = h.shape
    scores = jax.nn.sigmoid(h.astype(jnp.float32) @ w_router.astype(jnp.float32))
    sel = scores + router_bias.astype(jnp.float32)
    grp_score = lax.top_k(sel.reshape(T, N_GROUPS, N_EXPERTS // N_GROUPS), 2)[0].sum(-1)
    _, gidx = lax.top_k(grp_score, TOPK_GROUPS)
    gmask = jax.nn.one_hot(gidx, N_GROUPS).sum(1) > 0
    emask = jnp.repeat(gmask, N_EXPERTS // N_GROUPS, axis=1)
    _, eidx = lax.top_k(jnp.where(emask, sel, -jnp.inf), TOP_K)
    wts = jnp.take_along_axis(scores, eidx, axis=1)
    wts = wts / jnp.sum(wts, axis=-1, keepdims=True) * ROUTED_SCALE
    A = T * TOP_K
    flat_e = eidx.reshape(-1).astype(jnp.int32)
    flat_t = jnp.repeat(jnp.arange(T, dtype=jnp.int32), TOP_K)
    flat_w = wts.reshape(-1)
    order = jnp.argsort(flat_e)
    se = flat_e[order]
    counts = jnp.bincount(flat_e, length=N_EXPERTS)
    start = jnp.cumsum(counts) - counts
    padded = (counts + MOE_BLOCK - 1) // MOE_BLOCK * MOE_BLOCK
    pend = jnp.cumsum(padded)
    pstart = pend - padded
    dest = (pstart[se] + jnp.arange(A) - start[se]).astype(jnp.int32)
    n_blocks = -(-A // MOE_BLOCK) + N_EXPERTS
    n_slots = n_blocks * MOE_BLOCK
    slot_tok = jnp.full((n_slots,), T, jnp.int32).at[dest].set(flat_t[order])
    slot_w = jnp.zeros((n_slots,), jnp.float32).at[dest].set(flat_w[order])
    block_e = jnp.minimum(jnp.searchsorted(pend, jnp.arange(n_blocks) * MOE_BLOCK, side='right'), N_EXPERTS - 1)
    h_pad = jnp.concatenate([h, jnp.zeros((1, D), h.dtype)], axis=0)

    def run_block(args):
        tok, e = args
        xb = h_pad[tok]
        return (jax.nn.silu(xb @ w1[e]) * (xb @ w3[e])) @ w2[e]

    yb = lax.map(run_block, (slot_tok.reshape(n_blocks, MOE_BLOCK), block_e))
    routed = jnp.zeros((T + 1, D), jnp.float32).at[slot_tok].add(
        yb.reshape(n_slots, D).astype(jnp.float32) * slot_w[:, None])[:T]
    shared = (jax.nn.silu(h @ ws1) * (h @ ws3)) @ ws2
    return (routed + shared.astype(jnp.float32)).astype(h.dtype)

def layer(x, c, pool_hist, hg_state, pos0, chunked, lb, w_ada, b_ada, g_pre_mix, g_post_mix, w_in, w_pool,
          pool_scale, g_out_norm, w_out, g_pre_ffn, g_post_ffn, w_router, router_bias, w1, w3, w2, ws1, ws3, ws2):
    B, L, D = x.shape
    sh1, sc1, gt1, sh2, sc2, gt2 = ada_mod(c, w_ada, b_ada)
    h = rms_norm(x, g_pre_mix) * (1 + sc1) + sh1
    proj = h @ w_in
    u = proj[..., :POOL_WIDTH]
    u_ext = jnp.concatenate([pool_hist.astype(u.dtype), u], axis=1)
    y_pool = pool_mix(u_ext, pos0, w_pool, pool_scale)
    new_pool = u_ext[:, -POOL_HIST:]
    rest = proj[..., POOL_WIDTH:].astype(jnp.float32).reshape(B, L, 4, HG_HEADS, HG_HEAD_DIM)
    q_r, f_r, i_r, g_r = rest[:, :, 0], rest[:, :, 1], rest[:, :, 2], rest[:, :, 3]
    lbh = lb.reshape(HG_HEADS, HG_HEAD_DIM)
    f = lbh + (1.0 - lbh) * jax.nn.sigmoid(f_r)
    q = jax.nn.silu(q_r)
    s0 = hg_state.astype(jnp.float32)
    if chunked:
        o, S = hgrn2_chunked(q, jnp.log(f), 1.0 - f, i_r, s0)
    else:
        o, S = hgrn2_recurrent(q, jnp.log(f), 1.0 - f, i_r, s0)
    o = o * lax.rsqrt(jnp.mean(o * o, axis=-1, keepdims=True) + EPS) * g_out_norm.astype(jnp.float32) * jax.nn.silu(g_r)
    mix = jnp.concatenate([y_pool, o.reshape(B, L, HG_WIDTH).astype(x.dtype)], axis=-1) @ w_out
    x = x + gt1 * rms_norm(mix, g_post_mix)
    h2 = rms_norm(x, g_pre_ffn) * (1 + sc2) + sh2
    ff = moe_ffn(h2.reshape(B * L, D), w_router, router_bias, w1, w3, w2, ws1, ws3, ws2).reshape(B, L, D)
    x = x + gt2 * rms_norm(ff, g_post_ffn)
    return x, new_pool, S.astype(hg_state.dtype)

def setup_inputs(seed: int = 0) -> dict:
    key = jax.random.key(seed)
    ks = jax.random.split(key, 32)
    nrm = jax.random.normal
    D = D_MODEL
    f32 = jnp.float32
    return {
        "x_prompt": nrm(ks[0], (BATCH, SEQ, D), f32),
        "x_sample": nrm(ks[1], (DEC_BATCH, DEC_SEQ, D), f32),
        "c_prompt": nrm(ks[2], (BATCH, D), f32),
        "c_sample": nrm(ks[3], (DEC_BATCH, D), f32),
        "state_pool": nrm(ks[4], (DEPTH, DEC_BATCH, POOL_HIST, POOL_WIDTH), f32),
        "state_hgrn": 0.5 * nrm(ks[5], (DEPTH, DEC_BATCH, HG_HEADS, HG_HEAD_DIM, HG_HEAD_DIM), f32),
        "w_ada": 0.5 * D ** -0.5 * nrm(ks[6], (DEPTH, D, 6 * D), f32),
        "b_ada": 0.02 * nrm(ks[7], (DEPTH, 6 * D), f32),
        "g_pre_mix": 1.0 + 0.05 * nrm(ks[8], (DEPTH, D), f32),
        "g_post_mix": 1.0 + 0.05 * nrm(ks[9], (DEPTH, D), f32),
        "w_in": D ** -0.5 * nrm(ks[10], (DEPTH, D, IN_WIDTH), f32),
        "w_pool": POOL_GROUP ** -0.5 * nrm(ks[11], (DEPTH, N_POOL_GROUPS, POOL_GROUP, POOL_GROUP), f32),
        "pool_scale": 1.0 + 0.1 * nrm(ks[12], (DEPTH, POOL_WIDTH), f32),
        "lb_logits": 0.5 * nrm(ks[13], (DEPTH + 1, HG_WIDTH), f32),
        "g_out_norm": 1.0 + 0.05 * nrm(ks[14], (DEPTH, HG_HEAD_DIM), f32),
        "w_out": MIX_WIDTH ** -0.5 * nrm(ks[15], (DEPTH, MIX_WIDTH, D), f32),
        "g_pre_ffn": 1.0 + 0.05 * nrm(ks[16], (DEPTH, D), f32),
        "g_post_ffn": 1.0 + 0.05 * nrm(ks[17], (DEPTH, D), f32),
        "w_router": D ** -0.5 * nrm(ks[18], (DEPTH, D, N_EXPERTS), f32),
        "router_bias": 0.01 * nrm(ks[19], (DEPTH, N_EXPERTS), f32),
        "w_exp_gate": D ** -0.5 * nrm(ks[20], (DEPTH, N_EXPERTS, D, D_EXPERT), f32),
        "w_exp_up": D ** -0.5 * nrm(ks[21], (DEPTH, N_EXPERTS, D, D_EXPERT), f32),
        "w_exp_down": D_EXPERT ** -0.5 * nrm(ks[22], (DEPTH, N_EXPERTS, D_EXPERT, D), f32),
        "w_sh_gate": D ** -0.5 * nrm(ks[23], (DEPTH, D, D_EXPERT), f32),
        "w_sh_up": D ** -0.5 * nrm(ks[24], (DEPTH, D, D_EXPERT), f32),
        "w_sh_down": D_EXPERT ** -0.5 * nrm(ks[25], (DEPTH, D_EXPERT, D), f32),
    }

def reference(x_prompt, x_sample, c_prompt, c_sample, state_pool, state_hgrn, w_ada, b_ada, g_pre_mix, g_post_mix,
              w_in, w_pool, pool_scale, lb_logits, g_out_norm, w_out, g_pre_ffn, g_post_ffn, w_router, router_bias,
              w_exp_gate, w_exp_up, w_exp_down, w_sh_gate, w_sh_up, w_sh_down):
    lb_all = jnp.cumsum(jax.nn.softmax(lb_logits.astype(jnp.float32), axis=0), axis=0)
    bp = x_prompt.shape[0]
    zero_pool = jnp.zeros((bp, POOL_HIST, POOL_WIDTH), x_prompt.dtype)
    zero_hg = jnp.zeros((bp, HG_HEADS, HG_HEAD_DIM, HG_HEAD_DIM), x_prompt.dtype)
    hp, hs = x_prompt, x_sample
    pool_p, hg_p, pool_s, hg_s = [], [], [], []
    for l in range(DEPTH):
        wl = (w_ada[l], b_ada[l], g_pre_mix[l], g_post_mix[l], w_in[l], w_pool[l], pool_scale[l], g_out_norm[l],
              w_out[l], g_pre_ffn[l], g_post_ffn[l], w_router[l], router_bias[l], w_exp_gate[l], w_exp_up[l],
              w_exp_down[l], w_sh_gate[l], w_sh_up[l], w_sh_down[l])
        hp, npool, nhg = layer(hp, c_prompt, zero_pool, zero_hg, 0, True, lb_all[l], *wl)
        pool_p.append(npool)
        hg_p.append(nhg)
        hs, spool, shg = layer(hs, c_sample, state_pool[l], state_hgrn[l], PAST_LEN, False, lb_all[l], *wl)
        pool_s.append(spool)
        hg_s.append(shg)
    return (hp, hs, jnp.stack(pool_p), jnp.stack(hg_p), jnp.stack(pool_s), jnp.stack(hg_s))


_drawn_inputs = setup_inputs


def setup_inputs(seed=0):
    import zlib

    import numpy as np

    out = dict(_drawn_inputs(seed))
    spreads = {}
    factors = {'g_post_ffn': 4.015}
    for name, (base, spread) in spreads.items():
        noise = np.random.default_rng([zlib.crc32(name.encode()), seed]).standard_normal(out[name].shape)
        drawn = base * np.exp(spread * noise) if base else spread * noise
        out[name] = __import__('jax').numpy.asarray(drawn.astype(out[name].dtype))
    for name, factor in factors.items():
        out[name] = (out[name] * factor).astype(out[name].dtype)
    return out
```

```python
from contextlib import ExitStack

import concourse.bass as bass
from concourse import mybir

F32 = mybir.dt.float32
I32 = mybir.dt.int32
I8 = mybir.dt.int8
ALU = mybir.AluOpType
ACT = mybir.ActivationFunctionType
AX = mybir.AxisListType

P = 128
EPS = 1e-6
WINDOWS = (2, 4, 8, 16)
HIST = 15
TOP_K = 8
ROUTED_SCALE = 2.5
NEVER = 1024.0
LEVELS = (64, 32, 16, 8, 4, 2, 1)


class Chain:

    def __init__(self, engine, sem):
        self.engine, self.sem, self.count, self.base = engine, sem, 0, 0

    def __call__(self, instruction):
        instruction.then_inc(self.sem, 1)
        self.count += 1
        self.engine.wait_ge(self.sem, self.base + self.count)


def build(nc, x_prompt, x_sample, c_prompt, c_sample, state_pool, state_hgrn, w_ada, b_ada, g_pre_mix, g_post_mix,
          w_in, w_pool, pool_scale, lb_logits, g_out_norm, w_out, g_pre_ffn, g_post_ffn, w_router, router_bias,
          w_exp_gate, w_exp_up, w_exp_down, w_sh_gate, w_sh_up, w_sh_down,
          y_prompt, y_sample, pool_prompt, hgrn_prompt, pool_sample, hgrn_sample, h2_rows, ff_rows):
    D = x_prompt.shape[2]
    T = x_prompt.shape[1]
    NB = x_sample.shape[0]
    NT = T + NB
    KC = D // P
    PT = T // P
    TT = PT + 1
    NE = w_exp_gate.shape[1]
    NH = state_hgrn.shape[2]
    FE = w_exp_gate.shape[3]
    HALF = NT // 2
    N1 = NB + 1
    TRASH = NT
    ROWS = [P] * PT + [NB]
    MAX_EXTRA = NT * TOP_K // P
    assert (D, T, NB, NE, NH, FE) == (1024, 512, 8, 64, 4, 256)

    ctx = ExitStack()
    with ctx:
        def sb(name, shape, dt=F32):
            return ctx.enter_context(nc.sbuf_tensor(name, shape, dt))

        def sem(name):
            return ctx.enter_context(nc.semaphore(name))

        ringA = sb("ringA", [P, 4, 4096])
        ringB = sb("ringB", [P, 4, 2048])
        late = sb("late", [P, 7680])
        bc = sb("bc", [P, 4096])
        mm = sb("mm", [P, 4, D])
        xt = sb("xt", [P, TT, D])
        actT = sb("actT", [P, KC, NT])
        ident = sb("ident", [P, P])
        ones = sb("ones", [P, P])
        tri = sb("tri", [P, P])
        iota = sb("iota", [P, P])
        masks = sb("masks", [P, 8, P], I8)
        tokw = sb("tokw", [P, NE, TT, 2])
        posm = sb("posm", [P, NE, TT])
        onehot = sb("onehot", [P, TT, P])
        wrt = sb("wrt", [P, KC, NE])
        rbias = sb("rbias", [P, NE])
        small = sb("small", [P, 448])
        idx_i = sb("idx_i", [P, 4], I32)
        table_i = sb("table_i", [P, 33], I32)

        iB = ringB[:, :, :].rearrange("p a b -> p (a b)")
        q = iB[:, 0:NH * NT].rearrange("p (h t) -> p h t", h=NH)
        f = iB[:, 2080:4160].rearrange("p (h t) -> p h t", h=NH)
        UW = HIST + NT
        u = iB[:, 4160:4160 + 4 * UW].rearrange("p (g t) -> p g t", g=4)
        b = iB[:, 6300:7324]
        wpool = iB[:, 7324:7836].rearrange("p (g d) -> p g d", g=4)
        m1 = iB[:, 0:2048]
        gate = late[:, 0:2080].rearrange("p (h t) -> p h t", h=NH)
        v = late[:, 2080:4640].rearrange("p (j c) -> p j c", j=TT)
        kk = late[:, 4640:5680].rearrange("p (h t) -> p h t", h=2)
        att = late[:, 5680:6704].rearrange("p (c i) -> p c i", i=P)
        tmpS = late[:, 6704:7680]
        Dbuf = [bc[:, 0:1024], bc[:, 1024:2048]]
        khT = bc[:, 2048:3072]
        Sb = bc[:, 3072:4096].rearrange("p (h c v) -> p h c v", h=2, c=4)
        xn = [bc[:, 0:1024], bc[:, 1024:2048]]
        junk = bc[:, 2048:3072]
        hraw = bc[:, 3072:3584]
        histT = bc[:, 3584:4064].rearrange("p (g b r) -> p g b r", g=4, b=NB)
        cs = late[:, 0:1024]
        gvec = late[:, 0:3072].rearrange("p (a n) -> p a n", a=3)
        modb = bc[:, :].rearrange("p (a n) -> p a n", a=4)
        xg = late[:, 0:2048].rearrange("p (a n) -> p a n", a=2)
        xT = late[:, 2048:4096].rearrange("p (a k n) -> p a k n", a=2, k=KC)
        ybuf = late[:, 4096:6144].rearrange("p (a n) -> p a n", a=2)
        sg = late[:, 6144:6656].rearrange("p (a n) -> p a n", a=2)
        hh = late[:, 6656:7168].rearrange("p (a n) -> p a n", a=2)
        hhT = late[:, 7168:7680].rearrange("p (a k n) -> p a k n", a=2, k=2)

        at = [0]

        def cut(n):
            at[0] += n
            return small[:, at[0] - n:at[0]]

        ss = cut(TT)
        rstd = cut(TT)
        cT = cut(KC * N1).rearrange("p (k r) -> p k r", k=KC)
        a1T = cut(KC * N1).rearrange("p (k r) -> p k r", k=KC)
        b1T = cut(KC * N1).rearrange("p (k r) -> p k r", k=KC)
        gpre = cut(KC)
        vecT = cut(13)
        lb = cut(NH)
        oml = cut(NH)
        lbt = cut(3 * NH)
        eps_c = cut(1)
        icnt = cut(16)
        dl = cut(8)
        kS = cut(NH * NB).rearrange("p (h b) -> p h b", h=NH)
        trash1 = cut(1)
        valid = cut(1)
        wslot = cut(4)
        idx_f = cut(2)
        fin_ss = cut(2)
        fin_r = cut(2)
        qneg = cut(1)
        lower8 = cut(64)
        u_rows = tmpS[:, 464:976]
        zero_tile = ybuf[:, 0, :]
        fin_junk = late[:, 2048:3072]
        rt = [0]

        def routed(n):
            rt[0] += n
            return bc[:, rt[0] - n:rt[0]]

        def per_expert():
            return routed(TT * NE).rearrange("p (j e) -> p j e", j=TT)

        scores, sel, cmp1, cmp2, route_mask = (per_expert() for _ in range(5))
        sorted8 = routed(TT * 64).rearrange("p (j g r) -> p j g r", j=TT, g=8)
        gsc, grank, gmask, gpen, top8 = (routed(TT * 8).rearrange("p (j g) -> p j g", j=TT) for _ in range(5))
        tabrows = routed(64)
        tabq = routed(32)
        tabi = routed(4)[0:NE]
        tabn = routed(1)[0:NE]
        tabd = routed(2)[0:NE]
        tab1 = routed(32)[0:NE]
        assert rt[0] <= 3072

        ps = ctx.enter_context(nc.psum_tensor("ps", [P, 8, 512], F32))

        names = """in_small in_c in_x ringA_in0 ringA_in1 ringA_in2 ringA_in3 ringB_in0 ringB_in1 ringB_in2 ringB_in3
        consts_pool consts_dve pe_cT c_silu cT_ready ms_ready sq_ready rms_sqrt rstd_ready xn_ready x_turned x_evac_a x_evac_d
        ada_out ada_saved m1_turned m1T_ready mod_a mod_d lb_diff lb_exp lb_ready
        proj_out proj_a proj_d f_ready
        hist_in hist_turned hist_ready u_ready rows_turned rows_saved pool_d pool_y pool_saved rows_out hist_copy
        ln_done kk_ready b_ready diff_ready exp_done x_level level_out level_used qd_exp qd_ready kh_diff kh_exp kh_ready
        kh_turned khT_ready upd_out s_ready o_out o_sq o_ms o_r o_done hstate_out d_last
        s0_in s0_dec vb_out s_new so_out s_out so_sq so_ms so_r so_done mixer_read
        gvec_in modrow_ready mod_out modb_ready mix_out mix_sq mix_sqrt mix_rstd x1_ready x1_sq x1_sqrt x1_rstd h2_ready h2_stored
        h2_turned h2T_a h2T_d logit_out score_ready route_m pos_out pos_read cnt_out table_in table_out table_ready
        up_done silu_done glu_done hh_turned hhT_ready down_done y_a y_d ff_init0 ff_init1 scattered zero_rows zeros_ready
        onehot_ready disp_out idx_ready gathered0 gathered1 x_turned2 xT_a xT_d
        ff_in ff_sq ff_sqrt ff_rstd out_ready out_sent0 out_sent1 dve_chain act_chain pool_chain pool_passed""".split()
        s = {n: sem(n) for n in names}

        ypool_ps = ps[:, 6:8, 0:HALF]
        so_ps = ps[:, 2, 0:NH * NB]
        sms_ps = ps[:, 3, 0:NH * NB]
        logit_ps = ps[:, 7, 0:TT * NE].rearrange("p (j e) -> p j e", j=TT)

        def pair(i):
            return ps[:, 2 * i:2 * i + 2, :]

        def ringA_k(slot):
            return ringA[:, slot, :].rearrange("p (k n) -> p k n", k=KC)

        def ringA_gu(slot):
            return ringA[:, slot, :].rearrange("p (a k n) -> p a k n", a=2, k=KC)

        def ringB_k(slot):
            return ringB[:, slot, :].rearrange("p (k n) -> p k n", k=2)

        pieces = [("ada", 512 * i) for i in range(4)]
        pieces += [("in", 0), ("in", 1024), ("in", 512), ("in", 1536), ("in", 2048)]
        pieces += [("ada", 2048 + 512 * i) for i in range(8)]
        pieces += [("out", 0), ("out", 512), ("shared", 0)]
        NPIECE = len(pieces)
        A_OUT, A_SHARED = 17, 19

        def used(p):
            if p < 4:
                return s["ada_out"], p + 1
            if p < 9:
                return s["proj_out"], (4, 8, 12, 12 + TT, 16 + TT)[p - 4]
            if p < A_OUT:
                return s["ada_out"], p - 4
            return (s["up_done"], TT) if p == A_SHARED else (s["mix_out"], TT)

        def piece_source(kind, col, half):
            if kind == "out":
                return w_out[0].rearrange("(k p) n -> p k n", p=P)[:, 4 * half:4 * half + 4, col:col + 512]
            w = {"ada": w_ada, "in": w_in}[kind]
            return w[0].rearrange("(p k) n -> p k n", k=KC)[:, 4 * half:4 * half + 4, col:col + 512]

        def arrived_a(eng, p):
            eng.wait_ge(s[f"ringA_in{p % 4}"], 32 * (p // 4 + 1))

        def xrows(j):
            return xt[0:ROWS[j], j, :]

        block = ctx.enter_context(nc.Block())

        @block.sync
        def _(sp):
            sp.dma_start(cs[0:NB, :], c_sample).then_inc(s["in_c"], 16)
            sp.dma_start(cs[NB:N1, :], c_prompt).then_inc(s["in_c"], 16)
            sp.dma_start(xt[:, 0:PT, :], x_prompt[0].rearrange("(j p) d -> p j d", p=P)).then_inc(s["in_x"], 16)
            sp.dma_start(xt[0:NB, PT, :], x_sample[:, 0, :]).then_inc(s["in_x"], 16)

            def load_piece(p):
                kind, col = pieces[p]
                if p >= 4:
                    sp.wait_ge(*used(p - 4))
                for half in range(2):
                    if kind == "shared":
                        src = (w_sh_gate, w_sh_up)[half][0].rearrange("(p k) n -> p k n", k=KC)
                        dst = ringA_gu(p % 4)[:, half, :, :]
                    else:
                        src = piece_source(kind, col, half)
                        dst = ringA_k(p % 4)[:, 4 * half:4 * half + 4, :]
                    sp.dma_start(dst, src).then_inc(s[f"ringA_in{p % 4}"], 16)

            for p in range(NPIECE):
                load_piece(p)

            sp.wait_ge(s["mixer_read"], 1)
            sp.dma_start(ringB_k(0), w_sh_down[0].rearrange("(p k) n -> p k n", k=2)).then_inc(s["ringB_in0"], 16)

            def load_a(e, slot, e_dram):
                for half, w in enumerate((w_exp_gate, w_exp_up)):
                    sp.dma_start(ringA_gu(slot)[:, half, :, :],
                                 w[0, e_dram].rearrange("e (p k) n -> p (e k) n", k=KC)
                                 if not isinstance(e_dram, int) else w[0, e_dram].rearrange("(p k) n -> p k n", k=KC)
                                 ).then_inc(s[f"ringA_in{slot}"], 16)

            def load_b(e, slot, e_dram):
                src = w_exp_down[0, e_dram]
                src = (src.rearrange("(p k) n -> p k n", k=2) if isinstance(e_dram, int)
                       else src.rearrange("e (p k) n -> p (e k) n", k=2))
                sp.dma_start(ringB_k(slot), src).then_inc(s[f"ringB_in{slot}"], 16)

            for e in range(4):
                sp.wait_ge(*used(NPIECE - 4 + e))
                load_a(e, e, e)
                if e in (1, 2):
                    sp.wait_ge(s["mix_out"], TT)
                if e == 3:
                    sp.wait_ge(s["down_done"], TT)
                load_b(e, (1 + e) % 4, e)
            with sp.Fori(1, NE // 4) as i:
                for r in range(4):
                    e = i * 4 + r
                    sp.wait_ge(s["up_done"], e + 2)
                    load_a(e, r, bass.ds(e, 1))
                    sp.wait_ge(s["down_done"], e + 2)
                    load_b(e, (1 + r) % 4, bass.ds(e, 1))
            sp.wait_ge(s["table_ready"], 1)
            extra = sp.value_load(table_i[0:1, 32:33], min_val=1, max_val=MAX_EXTRA)
            with sp.Fori(0, extra) as i:
                e = sp.value_load(table_i[0:1, bass.ds(i, 1)], min_val=0, max_val=NE - 1)
                sp.wait_ge(s["up_done"], i + (TT + NE))
                load_a(e, 0, bass.ds(e, 1))
                sp.wait_ge(s["down_done"], i + (TT + NE))
                load_b(e, 1, bass.ds(e, 1))

            for j in range(TT):
                sp.wait_ge(s["out_ready"], j + 1)
                dst = y_prompt[0, j * P:(j + 1) * P, :] if j < PT else y_sample[:, 0, :]
                sp.dma_start(dst, ybuf[0:ROWS[j], j % 2, :]).then_inc(s[f"out_sent{j % 2}"], 16)
            sp.wait_ge(s["out_sent0"], 16 * 3)
            sp.wait_ge(s["out_sent1"], 16 * 2)
            sp.wait_ge(s["rows_out"], 48)
            sp.wait_ge(s["hstate_out"], 32)
            sp.wait_ge(s["s_out"], 16 * NB)

        @block.gpsimd
        def _(pool):
            chain = Chain(pool, s["pool_chain"])
            chain(pool.memset(ident[:, :], 0.0))
            chain(pool.affine_select(out=ident[:, :], in_=ident[:, :], compare_op=ALU.not_equal, fill=1.0, base=0,
                                     pattern=[[-1, P]], channel_multiplier=1))
            chain(pool.memset(tri[:, :], 0.0))
            chain(pool.affine_select(out=tri[:, :], in_=tri[:, :], compare_op=ALU.is_ge, fill=1.0, base=0,
                                     pattern=[[-1, P]], channel_multiplier=1))
            pool.iota(iota[:, :], pattern=[[1, P]], base=0, channel_multiplier=0,
                      allow_small_or_imprecise_dtypes=True)
            pool.iota(icnt, pattern=[[1, 16]], base=1, channel_multiplier=0, allow_small_or_imprecise_dtypes=True)
            pool.iota(trash1, pattern=[[0, 1]], base=TRASH + 1, channel_multiplier=1,
                      allow_small_or_imprecise_dtypes=True)
            pool.iota(tokw[:, :, :, 0], pattern=[[0, NE], [P, TT]], base=1, channel_multiplier=1,
                      allow_small_or_imprecise_dtypes=True).then_inc(s["consts_pool"], 1)
            chain(pool.memset(lower8, 1.0))
            chain(pool.affine_select(out=lower8, in_=lower8, compare_op=ALU.is_gt, fill=0.0, base=0,
                                     pattern=[[1, 8], [-1, 8]], channel_multiplier=0))
            def small_in(dst, src):
                pool.dma_start(dst, src).then_inc(s["in_small"], 16)
            small_in(tmpS[0:8, 0:P], lb_logits.rearrange("a (h p) -> (a h) p", p=P))
            small_in(tmpS[8:12, 0:P], pool_scale[0].rearrange("(h p) -> h p", p=P))
            small_in(tmpS[12:13, 0:P], g_out_norm)
            small_in(gpre, g_pre_mix[0].rearrange("(p k) -> p k", k=KC))
            small_in(m1[0:N1, :], b_ada[0, 0:2048].partition_broadcast(N1))
            small_in(mm[0:N1, :, :].rearrange("r a n -> r (a n)"),
                     b_ada[0, 2048:6144].partition_broadcast(N1))
            small_in(rbias[:, :], router_bias[0, :].partition_broadcast(P))
            small_in(wrt[:, :, :], w_router[0].rearrange("(p k) e -> p k e", k=KC))
            small_in(wpool, w_pool[0].rearrange("g c d -> c g d"))
            small_in(hraw[0:NB * HIST, :], state_pool[0].rearrange("b r c -> (b r) c"))
            ones_u = masks[:, :, :]
            chain(pool.memset(ones_u, 0.0))
            m0 = masks[:, 0, :]
            chain(pool.affine_select(out=m0, in_=m0, compare_op=ALU.not_equal, fill=1.0, base=0,
                                     pattern=[[-1, P]], channel_multiplier=1))
            for n, half in enumerate(LEVELS):
                right = masks[:, n + 1, :].rearrange("p (b h r) -> p b h r", h=2, r=half)[:, :, 1, :]
                chain(pool.memset(right, 1.0))
                nb = P // (2 * half)
                chain(pool.affine_select(out=right, in_=right, compare_op=ALU.is_ge, fill=0.0, base=0,
                                         pattern=[[-2 * half, nb], [0, half]], channel_multiplier=1))
                last = pool.affine_select(out=right, in_=right, compare_op=ALU.is_ge, fill=0.0, base=half - 1,
                                          pattern=[[2 * half, nb], [0, half]], channel_multiplier=-1)
                if half > 1:
                    chain(last)
            last.then_inc(s["consts_pool"], 1)

            pool.wait_ge(s["u_ready"], 4)
            for g, w in enumerate(WINDOWS):
                src = u[:, g, 0:HIST + T]
                step = 1
                if g >= 1:
                    pool.wait_ge(s["pool_y"], g)
                while step < w:
                    dst = (Dbuf[0] if src.offset != Dbuf[0].offset else Dbuf[1])[:, 0:HIST + T]
                    chain(pool.tensor_tensor(dst[:, 2 * step - 1:], src[:, 2 * step - 1:], src[:, step - 1:HIST + T - step], ALU.add))
                    src = dst
                    step *= 2
                diff = (Dbuf[0] if src.offset != Dbuf[0].offset else Dbuf[1])[:, 0:NT]
                mean = src[:, HIST:]
                hs = tmpS[:, 0:NB]
                if g == 0:
                    pool.wait_ge(s["hist_ready"], 1)
                    pool.wait_ge(s["consts_dve"], 1)
                chain(pool.tensor_tensor(mean[:, 0:w - 1], mean[:, 0:w - 1], icnt[:, 0:w - 1], ALU.mult))
                chain(pool.tensor_scalar(mean[:, w - 1:], mean[:, w - 1:], 1.0 / w, None, ALU.mult))
                chain(pool.tensor_tensor(diff[:, 0:T], mean, u[:, g, HIST:HIST + T], ALU.subtract))
                hsum = tmpS[:, 256 + NB * g:256 + NB * g + NB]
                chain(pool.tensor_tensor(hs, hsum, u[:, g, HIST + T:UW], ALU.add))
                chain(pool.tensor_scalar(hs, hs, 1.0 / w, None, ALU.mult))
                pool.tensor_tensor(diff[:, T:NT], hs, u[:, g, HIST + T:UW], ALU.subtract).then_inc(s["pool_d"], 1)
            pool.dma_start(pool_sample[0, :, 0:HIST - 1, :], state_pool[0, :, 1:HIST, :]).then_inc(s["rows_out"], 16)
            pool.wait_ge(s["rows_saved"], 1)
            pool.dma_start(pool_prompt[0, 0, :, :], u_rows[0:HIST, :]).then_inc(s["rows_out"], 16)
            pool.dma_start(pool_sample[0, :, HIST - 1, :], u_rows[HIST:HIST + NB, :]).then_inc(s["rows_out"], 16)
            for hp in range(2):
                pool.wait_ge(s["s_ready"], 8 * (hp + 1))
                pool.dma_start(hgrn_prompt[0, 0, 2 * hp:2 * hp + 2].rearrange("h k v -> k h v"),
                               Sb[:, :, 3, :]).then_inc(s["hstate_out"], 16)
            def s0_load(n):
                pool.dma_start(Dbuf[(n // 2) % 2][:, 512 * (n % 2):512 * (n % 2) + 512].rearrange("p (h v) -> p h v", h=NH),
                               state_hgrn[0, n].rearrange("h k v -> k h v")).then_inc(s["s0_in"], 16)
            pool.wait_ge(s["o_done"], 2)
            for n in range(NB):
                if n < 4:
                    s0_load(n)
            for n in range(NB):
                pool.wait_ge(s["s_new"], NH * (n + 1))
                pool.dma_start(hgrn_sample[0, n].rearrange("h k v -> k h v"),
                               Dbuf[(n // 2) % 2][:, 512 * (n % 2):512 * (n % 2) + 512].rearrange("p (h v) -> p h v", h=NH)
                               ).then_inc(s["s_out"], 16)
                if n + 4 < NB:
                    pool.wait_ge(s["s_out"], 16 * (n + 1))
                    pool.wait_ge(s["so_out"], n + 1)
                    s0_load(n + 4)
            pool.wait_ge(s["mixer_read"], 1)
            for n, g in enumerate((g_post_mix, g_pre_ffn, g_post_ffn)):
                pool.dma_start(gvec[0:N1, n, :], g[0, :].partition_broadcast(N1)
                               ).then_inc(s["gvec_in"], 16)
            pool.wait_ge(s["zeros_ready"], 1)
            pool.dma_start(ff_rows[NT:NT + P, :], zero_tile).then_inc(s["zero_rows"], 16)
            for j in range(TT):
                pool.wait_ge(s["h2_ready"], j + 1)
                pool.dma_start(h2_rows[j * P:j * P + ROWS[j], :], xg[0:ROWS[j], j % 2, :]).then_inc(s["h2_stored"], 16)
                pool.wait_ge(s["h2_stored"], 16 * (j + 1))
            pool.wait_ge(s["table_ready"], 1)

            def waits_stand_alone():
                pool.sem_inc(s["pool_passed"], 1)

            def gather(e, r4, par):
                pool.wait_ge(s["idx_ready"], e + 1)
                waits_stand_alone()
                pool.indirect_dma_start(xg[:, par, :], None, h2_rows,
                                        bass.IndirectOffsetOnAxis(ap=idx_i[:, r4:r4 + 1], axis=0),
                                        bounds_check=NT - 1, oob_is_err=False).then_inc(s[f"gathered{par}"], 16)

            def scatter(n, r4, par):
                pool.wait_ge(s["y_a"], n + 1)
                pool.wait_ge(s["y_d"], n + 1)
                waits_stand_alone()
                pool.indirect_dma_start(ff_rows, bass.IndirectOffsetOnAxis(ap=idx_i[:, r4:r4 + 1], axis=0),
                                        ybuf[:, par, :], None, compute_op=ALU.add).then_inc(s["scattered"], 16)

            gather(0, 0, 0)
            gather(1, 1, 1)
            for e in range(4):
                pool.wait_ge(s["x_turned2"], e + 1)
                gather(e + 2, (e + 2) % 4, e % 2)
                if e == 1:
                    pool.wait_ge(s["ff_init0"], 16 * 3)
                    pool.wait_ge(s["ff_init1"], 16 * 2)
                    pool.wait_ge(s["zero_rows"], 16)
                if e > 1:
                    pool.wait_ge(s["scattered"], 16 * (e - 1))
                if e > 0:
                    scatter(TT + e - 1, (e - 1) % 4, e % 2)
            with pool.Fori(1, NE // 4 - 1) as i:
                for r in range(4):
                    e = i * 4 + r
                    pool.wait_ge(s["x_turned2"], e + 1)
                    gather(e + 2, (r + 2) % 4, r % 2)
                    pool.wait_ge(s["scattered"], (e - 1) * 16)
                    scatter(e + (TT - 1), (r + 3) % 4, r % 2)
            for e in range(NE - 4, NE + 1):
                if e + 2 < NE:
                    pool.wait_ge(s["x_turned2"], e + 1)
                    gather(e + 2, (e + 2) % 4, e % 2)
                pool.wait_ge(s["scattered"], 16 * (e - 1))
                scatter(TT + e - 1, (e - 1) % 4, e % 2)
            extra = pool.value_load(table_i[0:1, 32:33], min_val=1, max_val=MAX_EXTRA)
            with pool.Fori(0, extra) as i:
                pool.wait_ge(s["x_turned2"], i + NE)
                gather(i + NE, 0, 0)
                pool.wait_ge(s["scattered"], i * 16 + 16 * NE)
                scatter(i + (TT + NE), 0, 0)
            pool.wait_ge(s["scattered"], extra * 16 + 16 * NE)
            waits_stand_alone()
            for j in range(TT):
                if j >= 2:
                    pool.wait_ge(s["out_ready"], j - 1)
                pool.dma_start(xg[0:ROWS[j], j % 2, :], ff_rows[j * P:j * P + ROWS[j], :]).then_inc(s["ff_in"], 16)
                pool.wait_ge(s["ff_in"], 16 * (j + 1))

        @block.scalar
        def _(act):
            act.wait_ge(s["in_c"], 32)
            act.activation(cs[0:N1, :], cs[0:N1, :], ACT.Silu).then_inc(s["c_silu"], 1)
            act.wait_ge(s["in_x"], 32)
            act.wait_ge(s["consts_dve"], 1)
            for j in range(TT):
                if j >= 1:
                    act.wait_ge(s["sq_ready"], j)
                act.activation(junk[0:ROWS[j], :], xrows(j), ACT.Square,
                               accum_out=ss[0:ROWS[j], j:j + 1]).then_inc(s["sq_ready"], 1)
            act.wait_ge(s["ms_ready"], 1)
            act.activation(rstd, ss, ACT.Sqrt).then_inc(s["rms_sqrt"], 1)
            act.wait_ge(s["rstd_ready"], 1)
            def normed(j):
                act.activation(xn[j % 2][0:ROWS[j], :], xrows(j), ACT.Copy,
                               scale=rstd[0:ROWS[j], j:j + 1]).then_inc(s["xn_ready"], 1)

            normed(0)
            normed(1)
            for j in range(TT):
                act.wait_ge(s["x_turned"], j + 1)
                if j + 2 < TT:
                    normed(j + 2)
                act.activation(actT[:, 0:4, j * P:j * P + ROWS[j]],
                               ps[:, 2 * (j % 2), :].rearrange("p (k n) -> p k n", k=4)[:, :, 0:ROWS[j]],
                               ACT.Copy).then_inc(s["x_evac_a"], 1)
            act.wait_ge(s["lb_diff"], 1)
            act.activation(lbt[:, 0:2 * NH], lbt[:, 0:2 * NH], ACT.Exp).then_inc(s["lb_exp"], 1)
            act.wait_ge(s["m1T_ready"], 1)
            act.wait_ge(s["x_evac_a"], TT)
            for k in range(4):
                act.activation(actT[:, k, 0:T], actT[:, k, 0:T], ACT.Identity, scale=a1T[:, k, NB:N1],
                               bias=b1T[:, k, NB:N1]).then_inc(s["mod_a"], 1)

            def two_halves(h):
                return pair(h)[:, :, 0:HALF]

            for n, (dst, func) in enumerate(((f, ACT.Sigmoid), (q, ACT.Silu), (None, None), (gate, ACT.Silu))):
                if dst is None:
                    for j in range(TT):
                        act.wait_ge(s["proj_out"], 4 + 8 + j + 1)
                        act.activation(v[0:ROWS[j], j, :], ps[0:ROWS[j], j, :], ACT.Copy).then_inc(s["proj_a"], 1)
                    continue
                for h in range(NH):
                    act.wait_ge(s["proj_out"], 4 + 4 * n + h + 1 + (1 if n == 3 else 0))
                    act.activation(dst[:, h, :].rearrange("p (a t) -> p a t", a=2), two_halves(h),
                                   func).then_inc(s["proj_a"], 1)

            for g in range(4):
                act.wait_ge(s["pool_y"], g + 1)
                act.activation(u[:, g, 0:NT].rearrange("p (a t) -> p a t", a=2), ypool_ps, ACT.Copy,
                               scale=vecT[:, 8 + g:9 + g]).then_inc(s["pool_saved"], 1)

            for hp in range(2):
                act.wait_ge(s["f_ready"], 4)
                if hp == 0:
                    act.wait_ge(s["pool_y"], 4)
                else:
                    act.wait_ge(s["o_out"], 1)
                act.activation(Dbuf[0].rearrange("p (h t) -> p h t", h=2), f[:, 2 * hp:2 * hp + 2, 0:T],
                               ACT.Ln).then_inc(s["ln_done"], 1)
                for n, half in enumerate(LEVELS):
                    act.wait_ge(s["diff_ready"], 7 * hp + n + 1)
                    d4 = Dbuf[(n + 1) % 2].rearrange("p (b h r) -> p b h r", h=2, r=half)
                    act.activation(d4[:, :, 1, :], d4[:, :, 1, :], ACT.Exp)
                    act.activation(d4[:, :, 0, :], d4[:, :, 0, :], ACT.Exp, scale=-1.0).then_inc(s["exp_done"], 1)
                act.wait_ge(s["level_out"], 8 * hp + 8)
                act.activation(Dbuf[0], b, ACT.Exp).then_inc(s["qd_exp"], 1)
                act.activation(dl, b.rearrange("p (c t) -> p c t", t=P)[:, :, P - 1], ACT.Exp).then_inc(s["d_last"], 1)
                act.wait_ge(s["kh_diff"], hp + 1)
                act.activation(Dbuf[1], Dbuf[1], ACT.Exp).then_inc(s["kh_exp"], 1)
                act.wait_ge(s["kh_turned"], hp + 1)
                act.activation(khT.rearrange("p (a n) -> p a n", a=2), pair(3), ACT.Copy).then_inc(s["khT_ready"], 1)
                act.wait_ge(s["o_out"], hp + 1)
                act.activation(khT.rearrange("p (a n) -> p a n", a=2), pair(1), ACT.Square).then_inc(s["o_sq"], 1)
                act.wait_ge(s["o_ms"], hp + 1)
                act.activation(khT.rearrange("p (a n) -> p a n", a=2), pair(3), ACT.Ln, bias=eps_c, scale=1.0 / P).then_inc(s["act_chain"], 1)
                act.wait_ge(s["act_chain"], hp + 1)
                act.activation(khT, khT, ACT.Exp, scale=-0.5).then_inc(s["o_r"], 1)
            for n in range(NB):
                act.wait_ge(s["s0_in"], 16 * NB if n >= 4 else 16 * 4)
                st = Dbuf[(n // 2) % 2][:, 512 * (n % 2):512 * (n % 2) + 512].rearrange("p (h v) -> p h v", h=NH)
                for h in range(NH):
                    act.activation(st[:, h, :], st[:, h, :], ACT.Copy, scale=f[:, h, T + n:T + n + 1]
                                   ).then_inc(s["s0_dec"], 1)
            act.wait_ge(s["so_out"], NB)
            act.activation(tmpS[:, 0:32], so_ps, ACT.Square).then_inc(s["so_sq"], 1)
            act.wait_ge(s["so_ms"], 1)
            act.activation(tmpS[:, 32:64], sms_ps, ACT.Ln, bias=eps_c, scale=1.0 / P).then_inc(s["act_chain"], 1)
            act.wait_ge(s["act_chain"], 3)
            act.activation(tmpS[:, 64:96], tmpS[:, 32:64], ACT.Exp, scale=-0.5).then_inc(s["so_r"], 1)

            act.wait_ge(s["s_out"], 16 * NB)
            act.wait_ge(s["hstate_out"], 32)
            for n in range(4):
                act.wait_ge(s["mod_out"], n + 1)
                act.activation(modb[:, n, :].rearrange("p (a n) -> p a n", a=2), pair(n), ACT.Copy
                               ).then_inc(s["modb_ready"], 1)
            for j in range(TT):
                R = ROWS[j]
                act.wait_ge(s["mix_out"], j + 1)
                act.activation(ybuf[0:R, 1, :].rearrange("p (a n) -> p a n", a=2), pair(j % 2)[0:R], ACT.Square,
                               accum_out=ss[0:R, j:j + 1]).then_inc(s["mix_sq"], 1)
                act.wait_ge(s["mix_sqrt"], 2 * j + 1)
                act.activation(rstd[0:R, j:j + 1], ss[0:R, j:j + 1], ACT.Sqrt).then_inc(s["mix_rstd"], 1)
                act.wait_ge(s["x1_ready"], j + 1)
                act.activation(ybuf[0:R, 1, :], xrows(j), ACT.Square, accum_out=ss[0:R, j:j + 1]
                               ).then_inc(s["x1_sq"], 1)
                act.wait_ge(s["mix_sqrt"], 2 * j + 2)
                act.activation(rstd[0:R, j:j + 1], ss[0:R, j:j + 1], ACT.Sqrt).then_inc(s["x1_rstd"], 1)
                act.wait_ge(s["h2_turned"], j + 1)
                act.activation(actT[:, 0:4, j * P:j * P + R],
                               ps[:, 4, :].rearrange("p (k n) -> p k n", k=4)[:, :, 0:R], ACT.Copy
                               ).then_inc(s["h2T_a"], 1)
            act.wait_ge(s["logit_out"], TT)
            act.wait_ge(s["zeros_ready"], 2)
            act.activation(scores[:, 0:PT, :], logit_ps[:, 0:PT, :], ACT.Sigmoid)
            act.activation(scores[0:NB, PT, :], logit_ps[0:NB, PT, :], ACT.Sigmoid).then_inc(s["score_ready"], 1)

            def silu(n, par, R=P):
                act.wait_ge(s["up_done"], n + 1)
                act.activation(sg[0:R, par, :], ps[0:R, 4 + par, 0:FE], ACT.Silu).then_inc(s["silu_done"], 1)

            def xT_half(e, par):
                act.wait_ge(s["x_turned2"], e + 1)
                act.activation(xT[:, par, 0:4, :], ps[:, 0, :].rearrange("p (k n) -> p k n", k=4), ACT.Copy
                               ).then_inc(s["xT_a"], 1)

            def y_half(n, par, R=P):
                act.wait_ge(s["down_done"], n + 1)
                act.activation(ybuf[0:R, par, 0:512], ps[0:R, 2, :], ACT.Copy).then_inc(s["y_a"], 1)

            def hhT_all(n, par, R=P):
                act.wait_ge(s["hh_turned"], n + 1)
                act.activation(hhT[:, par, :, 0:R], ps[:, 6, 0:256].rearrange("p (k n) -> p k n", k=2)[:, :, 0:R],
                               ACT.Copy).then_inc(s["hhT_ready"], 1)

            for n in range(TT):
                silu(n, n % 2, ROWS[n])
                if n >= 1:
                    if n >= 3:
                        act.wait_ge(s[f"ff_init{(n - 1) % 2}"], 16 * ((n - 1) // 2))
                    y_half(n - 1, (n - 1) % 2, ROWS[n - 1])
                    act.wait_ge(s["y_a"], n)
                    act.wait_ge(s["y_d"], n)
                    act.dma_start(ff_rows[(n - 1) * P:n * P, :], ybuf[:, (n - 1) % 2, :]
                                  ).then_inc(s[f"ff_init{(n - 1) % 2}"], 16)
                if n == TT - 1:
                    xT_half(0, 0)
                hhT_all(n, n % 2, ROWS[n])

            def step(e, r, last=False, first=False):
                n = e + TT
                silu(n, (r + 1) % 2)
                if not last:
                    xT_half(e + 1, (r + 1) % 2)
                y_half(n - 1, r % 2, NB if first else P)
                if first:
                    act.wait_ge(s["y_a"], TT)
                    act.wait_ge(s["y_d"], TT)
                    act.dma_start(ff_rows[PT * P:NT, :], ybuf[0:NB, r % 2, :]).then_inc(s["ff_init0"], 16)
                hhT_all(n, (r + 1) % 2)

            act.wait_ge(s["ff_init0"], 16 * 2)
            step(0, 0, first=True)
            act.wait_ge(s["ff_init1"], 16 * 2)
            step(1, 1)
            act.wait_ge(s["ff_init0"], 16 * 3)
            step(2, 2)
            act.wait_ge(s["scattered"], 16)
            step(3, 3)
            with act.Fori(1, NE // 4 - 1) as i:
                for r in range(4):
                    e = i * 4 + r
                    act.wait_ge(s["scattered"], (e - 2) * 16)
                    step(e, r)
            for r in range(4):
                act.wait_ge(s["scattered"], 16 * (NE - 4 + r - 2))
                step(NE - 4 + r, r, last=r == 3)
            act.wait_ge(s["scattered"], 16 * (NE - 2))
            y_half(TT + NE - 1, 0)
            extra = act.value_load(table_i[0:1, 32:33], min_val=1, max_val=MAX_EXTRA)
            with act.Fori(0, extra) as i:
                xT_half(i + NE, 0)
                silu(i + (TT + NE), 0)
                hhT_all(i + (TT + NE), 0)
                act.wait_ge(s["scattered"], i * 16 + 16 * NE)
                y_half(i + (TT + NE), 0)
            for j in range(TT):
                R = ROWS[j]
                act.wait_ge(s["ff_in"], 16 * (j + 1))
                if j >= 1:
                    act.wait_ge(s["out_ready"], j)
                act.activation(fin_junk[0:R, :], xg[0:R, j % 2, :], ACT.Square, accum_out=fin_ss[0:R, 0:1]
                               ).then_inc(s["ff_sq"], 1)
                act.wait_ge(s["ff_sqrt"], j + 1)
                act.activation(fin_r[0:R, 0:1], fin_ss[0:R, 0:1], ACT.Sqrt).then_inc(s["ff_rstd"], 1)

        @block.tensor
        def _(pe):
            pe.wait_ge(s["consts_pool"], 1)
            pe.wait_ge(s["c_silu"], 1)
            for k in range(KC):
                mt = pe.transpose(ps[:, 7, k * N1:(k + 1) * N1], cs[0:N1, k::KC], ident[0:N1, 0:N1])
            mt.then_inc(s["pe_cT"], 1)
            for j in range(TT):
                pe.wait_ge(s["xn_ready"], j + 1)
                if j >= 2:
                    pe.wait_ge(s["x_evac_a"], j - 1)
                    pe.wait_ge(s["x_evac_d"], j - 1)
                for k in range(KC):
                    R = ROWS[j]
                    mt = pe.transpose(ps[:, 2 * (j % 2) + k // 4, (k % 4) * P:(k % 4) * P + R],
                                      xn[j % 2][0:R, k::KC], ident[0:R, 0:R])
                mt.then_inc(s["x_turned"], 1)
            pe.wait_ge(s["in_small"], 160)
            pe.transpose(ps[:, 6, 480:493], tmpS[0:13, 0:P], ident[0:13, 0:13])
            for g in range(4):
                mt = pe.transpose(ps[:, 6, NB * HIST * g:NB * HIST * (g + 1)], hraw[0:NB * HIST, g * P:(g + 1) * P],
                                  ident[0:NB * HIST, 0:NB * HIST])
            mt.then_inc(s["hist_turned"], 1)

            def ada(n, p):
                arrived_a(pe, p)
                if n >= 2:
                    pe.wait_ge(s["ada_saved"], n - 1)
                for k in range(KC):
                    mt = pe.matmul(ps[0:N1, 4 + n % 2, :], cT[:, k, :], ringA_k(p % 4)[:, k, :],
                                   start=k == 0, stop=k == KC - 1)
                mt.then_inc(s["ada_out"], 1)

            pe.wait_ge(s["cT_ready"], 1)
            for n in range(4):
                ada(n, n)
            pe.wait_ge(s["ada_saved"], 4)
            for n in range(2):
                for k in range(KC):
                    mt = pe.transpose(ps[:, 7, 144 + (n * KC + k) * N1:144 + (n * KC + k + 1) * N1],
                                      m1[0:N1, n * D + k:(n + 1) * D:KC], ident[0:N1, 0:N1])
            mt.then_inc(s["m1_turned"], 1)

            pe.wait_ge(s["mod_a"], 4)
            pe.wait_ge(s["mod_d"], 1)
            for n in range(5):
                p = 4 + n
                arrived_a(pe, p)
                w = ringA_k(p % 4)
                if n == 3:
                    for j in range(TT):
                        if j % 2 == 0:
                            pe.wait_ge(s["proj_a"], 4 + j // 2 + 1)
                        for k in range(KC):
                            mt = pe.matmul(ps[0:ROWS[j], j, :], actT[:, k, j * P:j * P + ROWS[j]], w[:, k, :],
                                           start=k == 0, stop=k == KC - 1)
                        mt.then_inc(s["proj_out"], 1)
                else:
                    for h in range(NH):
                        if n == 0 and h == 0:
                            pe.wait_ge(s["x_evac_a"], TT)
                            pe.wait_ge(s["x_evac_d"], TT)
                        if n == 0 and h == 3:
                            pe.wait_ge(s["hist_ready"], 1)
                            pe.wait_ge(s["m1T_ready"], 1)
                        if n == 1:
                            pe.wait_ge(s["u_ready"], h + 1)
                        if n == 2:
                            pe.wait_ge(s["proj_a"], h + 1)
                        if n == 4:
                            pe.wait_ge(s["proj_a"], 8 + min(2 * h + 2, TT))
                        for half in range(2):
                            for k in range(KC):
                                mt = pe.matmul(ps[:, 2 * h + half, 0:HALF], w[:, k, h * P:(h + 1) * P],
                                               actT[:, k, half * HALF:(half + 1) * HALF],
                                               start=k == 0, stop=k == KC - 1)
                        mt.then_inc(s["proj_out"], 1)

            pe.wait_ge(s["proj_a"], 8 + TT + 1)
            for g in range(4):
                mt = pe.transpose(ps[0:HIST + NB, 0, g * P:(g + 1) * P], u[:, g, T:UW], ident[:, :])
            mt.then_inc(s["rows_turned"], 1)
            pe.wait_ge(s["rows_saved"], 1)
            pe.wait_ge(s["proj_a"], 8 + TT + 4)

            for g in range(4):
                pe.wait_ge(s["pool_d"], g + 1)
                if g >= 1:
                    pe.wait_ge(s["pool_saved"], g)
                n_steps = g + 1
                diff = Dbuf[n_steps % 2][:, 0:NT]
                for half in range(2):
                    mt = pe.matmul(ps[:, 6 + half, 0:HALF], wpool[:, g, :], diff[:, half * HALF:(half + 1) * HALF],
                                   start=True, stop=True)
                mt.then_inc(s["pool_y"], 1)

            ada_n = [4]

            def more_ada():
                if ada_n[0] < 12:
                    ada(ada_n[0], ada_n[0] + 5)
                    ada_n[0] += 1

            for hp in range(2):
                for n in range(8):
                    g = 8 * hp + n
                    if g == 0:
                        pe.wait_ge(s["proj_a"], 8 + TT + 4)
                        pe.wait_ge(s["kk_ready"], 1)
                    if n == 0 and hp == 1:
                        pe.wait_ge(s["kk_ready"], 2)
                        pe.wait_ge(s["o_done"], 1)
                    if n >= 1:
                        pe.wait_ge(s["x_level"], 7 * hp + n)
                    if g >= 2:
                        pe.wait_ge(s["level_used"], g - 1)
                    for h in range(2):
                        for c in range(PT):
                            if n == 0:
                                left = kk[:, h, c * P:(c + 1) * P]
                                right = q[:, 2 * hp + h, c * P:(c + 1) * P]
                            else:
                                left = right = Dbuf[n % 2][:, h * T + c * P:h * T + (c + 1) * P]
                            mt = pe.matmul(ps[:, 2 * (n % 2) + h, c * P:(c + 1) * P], left, right, start=True, stop=True)
                    mt.then_inc(s["level_out"], 1)
                    if n % 2 == 1:
                        more_ada()
                pe.wait_ge(s["kh_ready"], hp + 1)
                if hp == 0:
                    pe.wait_ge(s["pool_saved"], 4)
                for hc in range(8):
                    mt = pe.transpose(ps[:, 6 + hc // 4, (hc % 4) * P:(hc % 4 + 1) * P], Dbuf[1][:, hc * P:(hc + 1) * P],
                                      ident[:, :])
                mt.then_inc(s["kh_turned"], 1)
                pe.wait_ge(s["khT_ready"], hp + 1)
                pe.wait_ge(s["level_used"], 8 * hp + 8)
                for h in range(2):
                    for c in range(PT):
                        mt = pe.matmul(ps[:, h, c * P:(c + 1) * P], khT[:, (4 * h + c) * P:(4 * h + c + 1) * P],
                                       v[:, c, (2 * hp + h) * P:(2 * hp + h + 1) * P], start=True, stop=True)
                mt.then_inc(s["upd_out"], 1)
                pe.wait_ge(s["qd_ready"], hp + 1)
                pe.wait_ge(s["s_ready"], 8 * (hp + 1))
                for h in range(2):
                    for c in range(PT):
                        out = ps[:, 2 + h, c * P:(c + 1) * P]
                        mt = pe.matmul(out, v[:, c, (2 * hp + h) * P:(2 * hp + h + 1) * P], att[:, 4 * h + c, :],
                                       start=True, stop=c == 0)
                        if c >= 1:
                            mt = pe.matmul(out, Sb[:, h, c - 1, :], Dbuf[0][:, (4 * h + c) * P:(4 * h + c + 1) * P],
                                           start=False, stop=True)
                mt.then_inc(s["o_out"], 1)
                pe.wait_ge(s["o_sq"], hp + 1)
                for h in range(2):
                    mt = pe.matmul(ps[:, 6 + h, :], ones[:, :], khT[:, h * T:(h + 1) * T], start=True, stop=True)
                mt.then_inc(s["o_ms"], 1)
            while ada_n[0] < 12:
                more_ada()
            pe.wait_ge(s["o_done"], 2)
            for n in range(NB):
                if n >= 2:
                    pe.wait_ge(s["s_new"], NH * (n - 1))
                pe.matmul(ps[:, n % 2, :], ident[0:NB, n:n + 1].to_broadcast([NB, P]), v[0:NB, PT, :],
                          start=True, stop=True).then_inc(s["vb_out"], 1)
                pe.wait_ge(s["s_new"], NH * (n + 1))
                st = Dbuf[(n // 2) % 2][:, 512 * (n % 2):512 * (n % 2) + 512]
                for h in range(NH):
                    mt = pe.matmul(ps[:, 2, h * NB + n:h * NB + n + 1], st[:, h * P:(h + 1) * P],
                                   q[:, h, T + n:T + n + 1], start=True, stop=True)
                mt.then_inc(s["so_out"], 1)
            pe.wait_ge(s["so_sq"], 1)
            pe.matmul(ps[:, 3, 0:32], ones[:, :], tmpS[:, 0:32], start=True, stop=True).then_inc(s["so_ms"], 1)

            pe.wait_ge(s["modrow_ready"], 4)
            pe.wait_ge(s["so_done"], 1)
            for n in range(4):
                for half in range(2):
                    mt = pe.matmul(ps[:, 2 * n + half, :], ident[0:N1, NB:N1].to_broadcast([N1, P]),
                                   mm[0:N1, n, half * 512:(half + 1) * 512], start=True, stop=True)
                mt.then_inc(s["mod_out"], 1)

            def project_out(j):
                R = ROWS[j]
                if j == 0:
                    arrived_a(pe, A_OUT)
                    arrived_a(pe, A_OUT + 1)
                    pe.wait_ge(s["modb_ready"], 4)
                if j >= 2:
                    pe.wait_ge(s["x1_ready"], j - 1)
                for half in range(2):
                    w = ringA_k((A_OUT + half) % 4)
                    for k in range(KC):
                        left = (u[:, k, j * P:j * P + R] if k < 4 else actT[:, k, j * P:j * P + R])
                        mt = pe.matmul(ps[0:R, 2 * (j % 2) + half, :], left, w[:, k, :], start=k == 0, stop=k == KC - 1)
                mt.then_inc(s["mix_out"], 1)

            def turn_h2(j):
                R = ROWS[j]
                pe.wait_ge(s["h2_ready"], j + 1)
                if j >= 1:
                    pe.wait_ge(s["h2T_a"], j)
                    pe.wait_ge(s["h2T_d"], j)
                for k in range(KC):
                    mt = pe.transpose(ps[:, 4 + k // 4, (k % 4) * P:(k % 4) * P + R], xg[0:R, j % 2, k::KC],
                                      ident[0:R, 0:R])
                mt.then_inc(s["h2_turned"], 1)

            def route(j):
                R = ROWS[j]
                pe.wait_ge(s["h2T_a"], j + 1)
                pe.wait_ge(s["h2T_d"], j + 1)
                for k in range(KC):
                    mt = pe.matmul(ps[0:R, 7, j * NE:(j + 1) * NE], actT[:, k, j * P:j * P + R], wrt[:, k, :],
                                   start=k == 0, stop=k == KC - 1)
                mt.then_inc(s["logit_out"], 1)

            project_out(0)
            project_out(1)
            project_out(2)
            turn_h2(0)
            project_out(3)
            turn_h2(1)
            route(0)
            project_out(4)
            turn_h2(2)
            route(1)
            turn_h2(3)
            route(2)
            turn_h2(4)
            route(3)
            route(4)

            def up(n, par, left, slot, R=P):
                if n_static(n, 2):
                    pe.wait_ge(s["glu_done"], n - 1)
                for k in range(KC):
                    mt = pe.matmul(ps[0:R, 4 + par, :].rearrange("p (a n) -> p a n", a=2), left(k),
                                   ringA_gu(slot)[:, :, k, :], start=k == 0, stop=k == KC - 1)
                mt.then_inc(s["up_done"], 1)

            def n_static(n, least):
                return not isinstance(n, int) or n >= least

            def down(n, par, slot, R=P):
                pe.wait_ge(s["hhT_ready"], n + 1)
                if n_static(n, 1):
                    pe.wait_ge(s["y_a"], n)
                    pe.wait_ge(s["y_d"], n)
                for half in range(2):
                    for k in range(2):
                        mt = pe.matmul(ps[0:R, 2 + half, :], hhT[:, par, k, 0:R],
                                       ringB_k(slot)[:, k, half * 512:(half + 1) * 512], start=k == 0, stop=k == 1)
                mt.then_inc(s["down_done"], 1)

            def turn_hh(n, par, R=P):
                pe.wait_ge(s["glu_done"], n + 1)
                if n_static(n, 1):
                    pe.wait_ge(s["hhT_ready"], n)
                for k in range(2):
                    mt = pe.transpose(ps[:, 6, k * P:k * P + R], hh[0:R, par, k::2], ident[0:R, 0:R])
                mt.then_inc(s["hh_turned"], 1)

            def turn_x(e, par, gathers):
                pe.wait_ge(s[f"gathered{par}"], gathers)
                if n_static(e, 1):
                    pe.wait_ge(s["xT_a"], e)
                    pe.wait_ge(s["xT_d"], e)
                for k in range(KC):
                    mt = pe.transpose(ps[:, k // 4, (k % 4) * P:(k % 4 + 1) * P], xg[:, par, k::KC], ident[:, :])
                mt.then_inc(s["x_turned2"], 1)

            def dispatch(e, tok):
                pe.wait_ge(s["onehot_ready"], e + 1)
                if n_static(e, 1):
                    pe.wait_ge(s["idx_ready"], e)
                for j in range(TT):
                    mt = pe.matmul(ps[:, 7, 0:2], onehot[:, j, :], tok(j), start=j == 0, stop=j == TT - 1)
                mt.then_inc(s["disp_out"], 1)

            def tok_static(e):
                return lambda j: tokw[:, e, j, :]

            def shared(n):
                if n == 0:
                    arrived_a(pe, A_SHARED)
                    pe.wait_ge(s["h2T_a"], TT)
                up(n, n % 2, lambda k: actT[:, k, n * P:n * P + ROWS[n]], A_SHARED % 4, ROWS[n])
                if n == 1:
                    pe.wait_ge(s["ringB_in0"], 16)
                if n >= 1:
                    down(n - 1, (n - 1) % 2, 0, ROWS[n - 1])

            def shared_up(n):
                if n == 0:
                    arrived_a(pe, A_SHARED)
                    pe.wait_ge(s["h2T_a"], TT)
                    pe.wait_ge(s["h2T_d"], TT)
                up(n, n % 2, lambda k: actT[:, k, n * P:n * P + ROWS[n]], A_SHARED % 4, ROWS[n])

            shared_up(0)
            pe.wait_ge(s["route_m"], 1)
            for j in range(TT):
                for j2 in range(j + 1):
                    mt = pe.matmul(ps[:, 7, j * NE:(j + 1) * NE], tri[:, :] if j2 == j else ones[:, :],
                                   route_mask[:, j2, :], start=j2 == 0, stop=j2 == j)
            for j in range(TT):
                mt = pe.matmul(ps[0:NE, 7, 320:321], route_mask[:, j, :], ones[:, 0:1], start=j == 0, stop=j == TT - 1)
            mt.then_inc(s["pos_out"], 1)
            turn_hh(0, 0)
            shared_up(1)
            pe.wait_ge(s["cnt_out"], 1)
            pe.matmul(ps[0:NE, 7, 328:329], tri[0:NE, 0:NE], tabn, start=True, stop=True)
            pe.matmul(ps[:, 7, 336:337], ones[0:NE, :], tabn, start=True, stop=True).then_inc(s["table_in"], 1)
            pe.wait_ge(s["cnt_out"], 2)
            pe.matmul(ps[:, 7, 352:416], ones[0:NE, :], tabrows[0:NE, :], start=True, stop=True
                      ).then_inc(s["table_out"], 1)
            pe.wait_ge(s["ringB_in0"], 16)
            down(0, 0, 0)
            turn_hh(1, 1)
            for n in range(2, TT):
                shared_up(n)
                down(n - 1, (n - 1) % 2, 0)
                if n == TT - 1:
                    turn_x(0, 0, 16)
                turn_hh(n, n % 2, ROWS[n])
                if n < 4:
                    if n == 2:
                        pe.wait_ge(s["table_ready"], 1)
                    dispatch(n - 2, tok_static(n - 2))

            def tok_at(e):
                return lambda j: tokw[:, bass.ds(e, 1), j, :].rearrange("p e n -> p (e n)")

            def step(e, r, g, tail=0, first=False):
                n = e + TT
                waits_a, waits_b = in_a(r, g), in_b(r, g)
                pe.wait_ge(s["xT_a"], e + 1)
                pe.wait_ge(s["xT_d"], e + 1)
                waits_a()
                up(n, (r + 1) % 2, lambda k: xT[:, r % 2, k, :], r)
                if tail < 3:
                    turn_x(e + 1, (r + 1) % 2, g * 32 + 16 * ((r + 1) // 2 + 1))
                if tail < 2:
                    tok = tok_static(e + 2) if isinstance(e, int) else tok_at(e + 2)
                    dispatch(e + 2, tok)
                waits_b()
                down(n - 1, r % 2, r % 4, NB if first else P)
                turn_hh(n, (r + 1) % 2)

            def in_a(r, g):
                return lambda: pe.wait_ge(s[f"ringA_in{r}"], g * 32 + 32 * 6)

            def in_b(r, g):
                return lambda: pe.wait_ge(s[f"ringB_in{r}"], g * 16 + 16)

            for r in range(4):
                step(r, r, 0, first=r == 0)
            with pe.Fori(1, NE // 4 - 1) as i:
                for r in range(4):
                    step(i * 4 + r, r, i)
            for r in range(4):
                step(NE - 4 + r, r, NE // 4 - 1, tail=r)
            in_b(0, NE // 4)()
            down(TT + NE - 1, 0, 0)
            extra = pe.value_load(table_i[0:1, 32:33], min_val=1, max_val=MAX_EXTRA)
            with pe.Fori(0, extra) as i:
                e = pe.value_load(table_i[0:1, bass.ds(i, 1)], min_val=0, max_val=NE - 1)
                n = i + (TT + NE)
                pe.wait_ge(s["onehot_ready"], i + (NE + 1))
                for j in range(TT):
                    mt = pe.matmul(ps[:, 7, 0:2], onehot[:, j, :], tok_at(e)(j), start=j == 0, stop=j == TT - 1)
                mt.then_inc(s["disp_out"], 1)
                turn_x(i + NE, 0, i * 16 + 16 * (NE // 2 + 1))
                pe.wait_ge(s["xT_a"], i + (NE + 1))
                pe.wait_ge(s["xT_d"], i + (NE + 1))
                pe.wait_ge(s["ringA_in0"], i * 32 + 32 * (5 + NE // 4 + 1))
                up(n, 0, lambda k: xT[:, 0, k, :], 0)
                turn_hh(n, 0)
                pe.wait_ge(s["ringB_in1"], i * 16 + 16 * (NE // 4 + 1))
                down(n, 0, 1)

        @block.vector
        def _(dve):
            chain = Chain(dve, s["dve_chain"])
            dve.memset(ones[:, :], 1.0)
            dve.memset(eps_c, EPS)
            dve.wait_ge(s["consts_pool"], 1)
            chain(dve.memset(ss, 1.0))
            chain(dve.tensor_scalar(valid, trash1, float(TRASH + 1 + NB), None, ALU.is_lt))
            dve.reciprocal(icnt, icnt).then_inc(s["consts_dve"], 1)
            dve.wait_ge(s["pe_cT"], 1)
            dve.tensor_copy(cT, ps[:, 7, 0:KC * N1].rearrange("p (k r) -> p k r", k=KC)).then_inc(s["cT_ready"], 1)
            dve.wait_ge(s["sq_ready"], TT)
            dve.tensor_scalar(ss, ss, 1.0 / D, EPS, ALU.mult, ALU.add).then_inc(s["ms_ready"], 1)
            dve.wait_ge(s["rms_sqrt"], 1)
            dve.reciprocal(rstd, rstd).then_inc(s["rstd_ready"], 1)
            for j in range(TT):
                dve.wait_ge(s["x_turned"], j + 1)
                dve.tensor_copy(actT[:, 4:8, j * P:j * P + ROWS[j]],
                                ps[:, 2 * (j % 2) + 1, :].rearrange("p (k n) -> p k n", k=4)[:, :, 0:ROWS[j]]
                                ).then_inc(s["x_evac_d"], 1)
            dve.wait_ge(s["hist_turned"], 1)
            chain(dve.tensor_copy(histT, ps[:, 6, 0:4 * NB * HIST].rearrange("p (g b r) -> p g b r", g=4, b=NB)))
            for g, w in enumerate(WINDOWS):
                last = dve.tensor_reduce(tmpS[:, 256 + NB * g:256 + NB * g + NB], histT[:, g, :, HIST - (w - 1):HIST],
                                         AX.X, ALU.add)
            last.then_inc(s["hist_ready"], 1)
            chain(dve.tensor_copy(vecT, ps[:, 6, 480:493]))
            chain(dve.tensor_tensor(lbt[:, 8:12], vecT[:, 0:4], vecT[:, 4:8], ALU.max))
            dve.tensor_tensor(lbt[:, 0:4], vecT[:, 0:4], lbt[:, 8:12], ALU.subtract)
            dve.tensor_tensor(lbt[:, 4:8], vecT[:, 4:8], lbt[:, 8:12], ALU.subtract).then_inc(s["lb_diff"], 1)
            dve.wait_ge(s["lb_exp"], 1)
            chain(dve.tensor_tensor(lbt[:, 8:12], lbt[:, 0:4], lbt[:, 4:8], ALU.add))
            chain(dve.reciprocal(lbt[:, 8:12], lbt[:, 8:12]))
            chain(dve.tensor_tensor(lb, lbt[:, 0:4], lbt[:, 8:12], ALU.mult))
            chain(dve.tensor_scalar(oml, lb, -1.0, 1.0, ALU.mult, ALU.add))

            def ada_save(n, p, dst):
                dve.wait_ge(s["ada_out"], n + 1)
                dve.tensor_tensor(dst, ps[0:N1, 4 + n % 2, :], dst, ALU.add).then_inc(s["ada_saved"], 1)

            dve.wait_ge(s["in_small"], 160)
            for n in range(4):
                ada_save(n, n, m1[0:N1, 512 * n:512 * n + 512])
            dve.wait_ge(s["m1_turned"], 1)
            m1T = ps[:, 7, 144:144 + 2 * KC * N1].rearrange("p (a k r) -> p a k r", a=2, k=KC)
            dve.tensor_copy(b1T, m1T[:, 0])
            chain(dve.tensor_scalar(a1T, m1T[:, 1], 1.0, None, ALU.add))
            chain(dve.tensor_tensor(a1T, a1T, gpre.unsqueeze(2).to_broadcast([P, KC, N1]), ALU.mult))
            dve.sem_inc(s["m1T_ready"], 1)
            dve.wait_ge(s["x_evac_d"], TT)
            for k in range(4, KC):
                dve.tensor_scalar(actT[:, k, 0:T], actT[:, k, 0:T], a1T[:, k, NB:N1], b1T[:, k, NB:N1], ALU.mult, ALU.add)
            dve.wait_ge(s["x_evac_a"], TT)
            chain(dve.tensor_tensor(actT[:, :, T:NT], actT[:, :, T:NT], a1T[:, :, 0:NB], ALU.mult))
            dve.tensor_tensor(actT[:, :, T:NT], actT[:, :, T:NT], b1T[:, :, 0:NB], ALU.add).then_inc(s["mod_d"], 1)
            for g in range(4):
                if g == 0:
                    dve.memset(u[:, :, 0:HIST], 0.0)
                dve.wait_ge(s["proj_out"], g + 1)
                dve.tensor_copy(u[:, g, HIST:UW].rearrange("p (a t) -> p a t", a=2), pair(g)[:, :, 0:HALF]
                                ).then_inc(s["u_ready"], 1)
            for h in range(NH):
                dve.wait_ge(s["proj_a"], h + 1)
                dve.tensor_scalar(f[:, h, :], f[:, h, :], oml[:, h:h + 1], lb[:, h:h + 1], ALU.mult, ALU.add
                                  ).then_inc(s["f_ready"], 1)
            dve.wait_ge(s["rows_turned"], 1)
            dve.tensor_copy(u_rows[0:HIST + NB, :], ps[0:HIST + NB, 0, :]).then_inc(s["rows_saved"], 1)

            ada_n = [4]

            def more_ada():
                n = ada_n[0]
                if n < 12:
                    ada_save(n, n + 5, mm[0:N1, (n - 4) // 2, 512 * (n % 2):512 * (n % 2) + 512])
                    ada_n[0] += 1

            dve.wait_ge(s["f_ready"], 4)
            dve.tensor_scalar(kS, f[:, :, T:NT], -1.0, 1.0, ALU.mult, ALU.add)
            for hp in range(2):
                hs = slice(2 * hp, 2 * hp + 2)
                dve.tensor_scalar(kk, f[:, hs, :], -1.0, 1.0, ALU.mult, ALU.add).then_inc(s["kk_ready"], 1)
                dve.wait_ge(s["kk_ready"], hp + 1)
                chain(dve.memset(att, 0.0))
                dve.wait_ge(s["ln_done"], hp + 1)
                for c in range(8):
                    last = dve.tensor_tensor_scan(b[:, c * P:(c + 1) * P], ones[:, :], Dbuf[0][:, c * P:(c + 1) * P],
                                                  0.0, ALU.mult, ALU.add)
                chain(last)

                def diff(n):
                    half = LEVELS[n]
                    if n >= 2:
                        dve.wait_ge(s["level_out"], 8 * hp + n)
                    b4 = b.rearrange("p (b r) -> p b r", r=2 * half)
                    nb = 1024 // (2 * half)
                    mid = b4[:, :, half - 1:half].to_broadcast([P, nb, 2 * half])
                    dve.tensor_tensor(Dbuf[(n + 1) % 2].rearrange("p (b r) -> p b r", r=2 * half), b4, mid,
                                      ALU.subtract).then_inc(s["diff_ready"], 1)

                def times(n):
                    half = LEVELS[n]
                    dve.wait_ge(s["exp_done"], 7 * hp + n + 1)
                    for side, src in ((1, q[:, hs, 0:T]), (0, kk[:, :, 0:T])):
                        for h in range(2):
                            d4 = Dbuf[(n + 1) % 2][:, h * T:(h + 1) * T].rearrange("p (b h r) -> p b h r", h=2, r=half)[:, :, side, :]
                            s4 = src[:, h, :].rearrange("p (b h r) -> p b h r", h=2, r=half)[:, :, side, :]
                            last = dve.tensor_tensor(d4, d4, s4, ALU.mult)
                    last.then_inc(s["x_level"], 1)

                def keep(n):
                    dve.wait_ge(s["level_out"], 8 * hp + n + 1)
                    if n >= 1:
                        dve.wait_ge(s["level_used"], 8 * hp + n)
                    dve.copy_predicated(att, masks[:, n, :].unsqueeze(1).to_broadcast([P, 8, P]),
                                        pair(n % 2).rearrange("p a (c i) -> p (a c) i", i=P)
                                        ).then_inc(s["level_used"], 1)

                dve.wait_ge(s["consts_pool"], 2)
                diff(0)
                for n in range(7):
                    if n + 1 < 7:
                        diff(n + 1)
                    times(n)
                    keep(n)
                    if n in (2, 4, 6):
                        more_ada()
                keep(7)
                more_ada()
                last_b = b.rearrange("p (c t) -> p c t", t=P)[:, :, P - 1:P].to_broadcast([P, 8, P])
                dve.tensor_tensor(Dbuf[1].rearrange("p (c t) -> p c t", t=P), last_b,
                                  b.rearrange("p (c t) -> p c t", t=P), ALU.subtract).then_inc(s["kh_diff"], 1)
                dve.wait_ge(s["qd_exp"], hp + 1)
                dve.tensor_tensor(Dbuf[0].rearrange("p (h t) -> p h t", h=2), Dbuf[0].rearrange("p (h t) -> p h t", h=2),
                                  q[:, hs, 0:T], ALU.mult).then_inc(s["qd_ready"], 1)
                dve.wait_ge(s["kh_exp"], hp + 1)
                dve.tensor_tensor(Dbuf[1].rearrange("p (h t) -> p h t", h=2), Dbuf[1].rearrange("p (h t) -> p h t", h=2),
                                  kk[:, :, 0:T], ALU.mult).then_inc(s["kh_ready"], 1)
                dve.wait_ge(s["upd_out"], hp + 1)
                dve.wait_ge(s["d_last"], hp + 1)
                if hp == 1:
                    dve.wait_ge(s["hstate_out"], 16)
                for c in range(PT):
                    for h in range(2):
                        upd = ps[:, h, c * P:(c + 1) * P]
                        if c == 0:
                            dve.tensor_copy(Sb[:, h, 0, :], upd).then_inc(s["s_ready"], 1)
                        else:
                            dve.wait_ge(s["s_ready"], 8 * hp + 2 * c - 1 + h)
                            dve.scalar_tensor_tensor(Sb[:, h, c, :], Sb[:, h, c - 1, :], dl[:, 4 * h + c:4 * h + c + 1], upd,
                                                     ALU.mult, ALU.add).then_inc(s["s_ready"], 1)
                dve.wait_ge(s["o_sq"], hp + 1)
                oT = actT[:, 4 + 2 * hp:6 + 2 * hp, 0:T]
                chain(dve.scalar_tensor_tensor(oT, pair(1), vecT[:, 12:13], gate[:, hs, 0:T], ALU.mult, ALU.mult))
                dve.wait_ge(s["o_r"], hp + 1)
                dve.tensor_tensor(oT, oT, khT.rearrange("p (h t) -> p h t", h=2), ALU.mult).then_inc(s["o_done"], 1)
            for n in range(NB):
                dve.wait_ge(s["vb_out"], n + 1)
                dve.wait_ge(s["s0_dec"], NH * (n + 1))
                st = Dbuf[(n // 2) % 2][:, 512 * (n % 2):512 * (n % 2) + 512]
                for h in range(NH):
                    dve.scalar_tensor_tensor(st[:, h * P:(h + 1) * P], ps[:, n % 2, h * P:(h + 1) * P],
                                             kS[:, h, n:n + 1], st[:, h * P:(h + 1) * P], ALU.mult, ALU.add
                                             ).then_inc(s["s_new"], 1)
            dve.wait_ge(s["so_sq"], 1)
            oS = actT[:, 4:8, T:NT]
            chain(dve.scalar_tensor_tensor(oS, so_ps.rearrange("p (h b) -> p h b", h=NH), vecT[:, 12:13],
                                           gate[:, :, T:NT], ALU.mult, ALU.mult))
            dve.wait_ge(s["so_r"], 1)
            chain(dve.tensor_tensor(oS, oS, tmpS[:, 64:96].rearrange("p (h b) -> p h b", h=NH), ALU.mult))
            dve.sem_inc(s["so_done"], 1)
            dve.sem_inc(s["mixer_read"], 1)
            dve.wait_ge(s["ada_saved"], 12)
            dve.wait_ge(s["gvec_in"], 48)
            chain(dve.tensor_scalar(mm[0:N1, 2, :], mm[0:N1, 2, :], 1.0, None, ALU.add))
            for n, g in ((0, 0), (2, 1), (3, 2)):
                dve.tensor_tensor(mm[0:N1, n, :], mm[0:N1, n, :], gvec[0:N1, g, :], ALU.mult).then_inc(s["modrow_ready"], 1)
            dve.wait_ge(s["modrow_ready"], 3)
            dve.memset(ybuf[:, 0, :], 0.0).then_inc(s["modrow_ready"], 1)
            dve.wait_ge(s["modrow_ready"], 4)
            dve.sem_inc(s["zeros_ready"], 1)
            dve.wait_ge(s["modb_ready"], 4)
            dve.wait_ge(s["zero_rows"], 16)
            for j in range(TT):
                R = ROWS[j]
                row = [modb[:, n, :] if j < PT else mm[0:R, n, :] for n in range(4)]
                dve.wait_ge(s["mix_sq"], j + 1)
                dve.tensor_scalar(ss[0:R, j:j + 1], ss[0:R, j:j + 1], 1.0 / D, EPS, ALU.mult, ALU.add
                                  ).then_inc(s["mix_sqrt"], 1)
                dve.wait_ge(s["mix_rstd"], j + 1)
                chain(dve.reciprocal(rstd[0:R, j:j + 1], rstd[0:R, j:j + 1]))
                mixed = ybuf[0:R, 0, :]
                chain(dve.scalar_tensor_tensor(mixed.rearrange("p (a n) -> p a n", a=2), pair(j % 2)[0:R],
                                               rstd[0:R, j:j + 1], row[0].rearrange("p (a n) -> p a n", a=2),
                                               ALU.mult, ALU.mult))
                dve.tensor_tensor(xrows(j), xrows(j), mixed, ALU.add).then_inc(s["x1_ready"], 1)
                dve.wait_ge(s["x1_sq"], j + 1)
                dve.tensor_scalar(ss[0:R, j:j + 1], ss[0:R, j:j + 1], 1.0 / D, EPS, ALU.mult, ALU.add
                                  ).then_inc(s["mix_sqrt"], 1)
                dve.wait_ge(s["x1_rstd"], j + 1)
                chain(dve.reciprocal(rstd[0:R, j:j + 1], rstd[0:R, j:j + 1]))
                if j >= 2:
                    dve.wait_ge(s["h2_stored"], 16 * (j - 1))
                    dve.wait_ge(s["h2_turned"], j - 1)
                h2 = xg[0:R, j % 2, :]
                chain(dve.scalar_tensor_tensor(h2, xrows(j), rstd[0:R, j:j + 1], row[2], ALU.mult, ALU.mult))
                dve.tensor_tensor(h2, h2, row[1], ALU.add).then_inc(s["h2_ready"], 1)
                dve.wait_ge(s["h2_turned"], j + 1)
                dve.tensor_copy(actT[:, 4:8, j * P:j * P + R],
                                ps[:, 5, :].rearrange("p (k n) -> p k n", k=4)[:, :, 0:R]).then_inc(s["h2T_d"], 1)
            def pick(e, posm_at, offset=None):
                for j in range(TT):
                    if offset is None:
                        last = dve.tensor_scalar(onehot[:, j, :], iota[:, :], posm_at(j), None, ALU.is_equal)
                    else:
                        last = dve.tensor_scalar(onehot[:, j, :], iota[:, :], offset, posm_at(j), ALU.add, ALU.is_equal)
                last.then_inc(s["onehot_ready"], 1)

            def index(e, r4):
                dve.wait_ge(s["disp_out"], e + 1)
                dve.tensor_copy(wslot[:, r4:r4 + 1], ps[:, 7, 1:2])
                chain(dve.tensor_scalar(idx_f[:, 0:1], ps[:, 7, 0:1], 0.0, None, ALU.is_equal))
                chain(dve.scalar_tensor_tensor(idx_f[:, 1:2], idx_f[:, 0:1], trash1, ps[:, 7, 0:1], ALU.mult, ALU.add))
                dve.tensor_scalar(idx_i[:, r4:r4 + 1], idx_f[:, 1:2], -1.0, None, ALU.add).then_inc(s["idx_ready"], 1)

            def posm_static(e):
                return lambda j: posm[:, e, j:j + 1]

            def posm_dyn(e):
                return lambda j: posm[:, bass.ds(e, 1), j:j + 1].rearrange("p e n -> p (e n)")

            def glu(n, par, weight, R=P):
                dve.wait_ge(s["silu_done"], n + 1)
                dve.scalar_tensor_tensor(hh[0:R, par, :], sg[0:R, par, :], weight, ps[0:R, 4 + par, FE:2 * FE],
                                         ALU.mult, ALU.mult).then_inc(s["glu_done"], 1)

            def xT_half(e, par):
                dve.wait_ge(s["x_turned2"], e + 1)
                dve.tensor_copy(xT[:, par, 4:8, :], ps[:, 1, :].rearrange("p (k n) -> p k n", k=4)
                                ).then_inc(s["xT_d"], 1)

            def y_half(n, par, R=P):
                dve.wait_ge(s["down_done"], n + 1)
                dve.tensor_copy(ybuf[0:R, par, 512:1024], ps[0:R, 3, :]).then_inc(s["y_d"], 1)

            dve.wait_ge(s["h2_ready"], TT)
            chain(dve.memset(scores, 1.0))
            dve.memset(tabrows, 0.0).then_inc(s["zeros_ready"], 1)
            dve.wait_ge(s["score_ready"], 1)
            chain(dve.tensor_tensor(sel, scores, rbias[:, :].unsqueeze(1).to_broadcast([P, TT, NE]), ALU.add))
            for j in range(TT):
                for g in range(8):
                    last = dve.max(sorted8[:, j, g, :], sel[:, j, 8 * g:8 * g + 8])
            chain(last)
            chain(dve.tensor_tensor(gsc, sorted8[:, :, :, 0], sorted8[:, :, :, 1], ALU.add))
            other = gsc.unsqueeze(2).to_broadcast([P, TT, 8, 8])
            this = gsc.unsqueeze(3).to_broadcast([P, TT, 8, 8])
            dve.tensor_tensor(cmp1.rearrange("p j (a b) -> p j a b", a=8), other, this, ALU.is_gt)
            chain(dve.tensor_tensor(cmp2.rearrange("p j (a b) -> p j a b", a=8), other, this, ALU.is_equal))
            chain(dve.tensor_tensor(cmp2, cmp2, lower8.unsqueeze(1).to_broadcast([P, TT, NE]), ALU.mult))
            chain(dve.tensor_tensor(cmp1, cmp1, cmp2, ALU.add))
            chain(dve.tensor_reduce(grank, cmp1.rearrange("p j (a b) -> p j a b", a=8), AX.X, ALU.add))
            chain(dve.tensor_scalar(gmask, grank, 3.5, None, ALU.is_lt))
            chain(dve.tensor_scalar(gpen, gmask, 1e30, -1e30, ALU.mult, ALU.add))
            g4 = sel.rearrange("p j (a b) -> p j a b", a=8)
            chain(dve.tensor_tensor(g4, g4, gmask.unsqueeze(3).to_broadcast([P, TT, 8, 8]), ALU.mult))
            chain(dve.tensor_tensor(g4, g4, gpen.unsqueeze(3).to_broadcast([P, TT, 8, 8]), ALU.add))
            for j in range(TT):
                last = dve.max(top8[:, j, :], sel[:, j, :])
            chain(last)
            v8 = top8[:, :, 7:8].to_broadcast([P, TT, NE])
            dve.tensor_tensor(cmp1, sel, v8, ALU.is_gt)
            chain(dve.tensor_tensor(cmp2, sel, v8, ALU.is_equal))
            for j in range(TT):
                last = dve.tensor_tensor_scan(route_mask[:, j, :], ones[:, 0:NE], cmp2[:, j, :], 0.0, ALU.mult, ALU.add)
            chain(last)
            chain(dve.tensor_reduce(grank[:, :, 0], cmp1, AX.X, ALU.add))
            chain(dve.tensor_scalar(grank[:, :, 0], grank[:, :, 0], -1.0, TOP_K + 0.5, ALU.mult, ALU.add))
            chain(dve.tensor_tensor(route_mask, route_mask, grank[:, :, 0:1].to_broadcast([P, TT, NE]), ALU.is_lt))
            chain(dve.tensor_tensor(route_mask, route_mask, cmp2, ALU.mult))
            chain(dve.tensor_tensor(route_mask, route_mask, cmp1, ALU.add))
            chain(dve.tensor_tensor(scores, scores, route_mask, ALU.mult))
            chain(dve.tensor_scalar(route_mask[:, PT, :], route_mask[:, PT, :], valid, None, ALU.mult))
            dve.sem_inc(s["route_m"], 1)
            chain(dve.tensor_reduce(grank[:, :, 1], scores, AX.X, ALU.add))
            chain(dve.reciprocal(grank[:, :, 1], grank[:, :, 1]))
            chain(dve.tensor_scalar(grank[:, :, 1], grank[:, :, 1], ROUTED_SCALE, None, ALU.mult))
            chain(dve.tensor_tensor(tokw[:, :, :, 1].rearrange("p e j -> p j e"), scores,
                                    grank[:, :, 1:2].to_broadcast([P, TT, NE]), ALU.mult))
            glu(0, 0, 1.0)
            dve.wait_ge(s["pos_out"], 1)
            pos = ps[:, 7, 0:TT * NE].rearrange("p (j e) -> p j e", j=TT)
            chain(dve.scalar_tensor_tensor(sel, pos, 1.0, route_mask, ALU.add, ALU.mult))
            chain(dve.tensor_scalar(posm[:, :, :].rearrange("p e j -> p j e"), sel, -1.0, None, ALU.add))
            cnt = ps[0:NE, 7, 320:321]
            for j in range(4):
                last = dve.tensor_scalar(tabi[:, j:j + 1], cnt, float(P * (j + 1)), None, ALU.is_gt)
            chain(last)
            chain(dve.tensor_reduce(tabn, tabi, AX.X, ALU.add))
            dve.sem_inc(s["cnt_out"], 1)
            dve.wait_ge(s["table_in"], 1)
            chain(dve.tensor_scalar(tabd[:, 0:1], ps[0:NE, 7, 328:329], 0.0, None, ALU.add))
            chain(dve.tensor_copy(tabd[:, 1:2], trash1[0:NE, :]))
            chain(dve.tensor_scalar(tabd[:, 1:2], tabd[:, 1:2], -float(TRASH + 1), None, ALU.add))
            for j in range(4):
                chain(dve.tensor_scalar(tab1, iota[0:NE, 0:32], tabd[:, 0:1], tabi[:, j:j + 1], ALU.is_equal, ALU.mult))
                chain(dve.scalar_tensor_tensor(tabrows[0:NE, 0:32], tab1, tabd[:, 1:2], tabrows[0:NE, 0:32], ALU.mult, ALU.add))
                chain(dve.scalar_tensor_tensor(tabrows[0:NE, 32:64], tab1, NEVER - P * (j + 1), tabrows[0:NE, 32:64],
                                               ALU.mult, ALU.add))
                chain(dve.tensor_scalar(tabd[:, 0:1], tabd[:, 0:1], 1.0, None, ALU.add))
            dve.sem_inc(s["cnt_out"], 1)
            dve.wait_ge(s["table_out"], 1)
            dve.tensor_copy(table_i[:, 0:32], ps[:, 7, 352:384])
            dve.tensor_copy(tabq, ps[:, 7, 384:416])
            chain(dve.tensor_scalar(table_i[:, 32:33], ps[:, 7, 336:337], 1.0, None, ALU.max))

            dve.wait_ge(s["h2_turned"], TT)
            dve.wait_ge(s["h2_stored"], 16 * TT)
            chain(dve.memset(xg[:, :, :], 0.0))
            dve.sem_inc(s["table_ready"], 1)
            pick(0, posm_static(0))
            glu(1, 1, 1.0)
            y_half(0, 0)
            glu(2, 0, 1.0)
            y_half(1, 1)
            index(0, 0)
            pick(1, posm_static(1))
            glu(3, 1, 1.0)
            dve.wait_ge(s["ff_init0"], 16)
            y_half(2, 0)
            index(1, 1)
            pick(2, posm_static(2))
            glu(4, 0, 1.0, NB)
            dve.wait_ge(s["ff_init1"], 16)
            y_half(3, 1)
            xT_half(0, 0)

            LINKS = 2

            def step(e, r, tail=0, first=False, posm_of=posm_static):
                n = e + TT
                if tail < 3:
                    xT_half(e + 1, (r + 1) % 2)
                glu(n, (r + 1) % 2, wslot[:, r:r + 1])
                if tail < 2:
                    if not isinstance(e, int) or e >= 2:
                        dve.wait_ge(s["scattered"], (e - 1) * 16)
                    index(e + 2, (r + 2) % 4)
                if tail < 1:
                    pick(e + 3, posm_of(e + 3))
                y_half(n - 1, r % 2, NB if first else P)

            dve.wait_ge(s["ff_init0"], 16 * 2)
            step(0, 0, first=True)
            dve.wait_ge(s["ff_init1"], 16 * 2)
            step(1, 1)
            dve.wait_ge(s["ff_init0"], 16 * 3)
            step(2, 2)
            step(3, 3)
            before = chain.count
            with dve.Fori(1, NE // 4 - 1) as i:
                for r in range(4):
                    e = i * 4 + r
                    chain.base, chain.count = (i - 1) * (4 * LINKS) + before, LINKS * r
                    step(e, r, posm_of=posm_dyn)
            chain.base, chain.count = 0, before + LINKS * (NE - 8)
            for r in range(4):
                dve.wait_ge(s["scattered"], 16 * (NE - 4 + r - 2))
                step(NE - 4 + r, r, tail=r)
            dve.wait_ge(s["scattered"], 16 * (NE - 2))
            y_half(TT + NE - 1, 0)
            before = chain.count
            extra = dve.value_load(table_i[0:1, 32:33], min_val=1, max_val=MAX_EXTRA)
            with dve.Fori(0, extra) as i:
                e = dve.value_load(table_i[0:1, bass.ds(i, 1)], min_val=0, max_val=NE - 1)
                chain.base, chain.count = i * (1 + LINKS) + before, 0
                chain(dve.tensor_scalar(qneg, tabq[:, bass.ds(i, 1)], -1.0, NEVER, ALU.mult, ALU.add))
                pick(i + NE, posm_dyn(e), offset=qneg)
                dve.wait_ge(s["onehot_ready"], i + (NE + 1))
                dve.wait_ge(s["scattered"], i * 16 + 16 * NE)
                index(i + NE, 0)
                xT_half(i + NE, 0)
                glu(i + (TT + NE), 0, wslot[:, 0:1])
                y_half(i + (TT + NE), 0)
            for j in range(TT):
                R = ROWS[j]
                g2 = modb[:, 3, :] if j < PT else mm[0:R, 3, :]
                dve.wait_ge(s["ff_sq"], j + 1)
                dve.tensor_scalar(fin_ss[0:R, 0:1], fin_ss[0:R, 0:1], 1.0 / D, EPS, ALU.mult, ALU.add
                                  ).then_inc(s["ff_sqrt"], 1)
                dve.wait_ge(s["ff_rstd"], j + 1)
                if j == 0:
                    chain.base, chain.count = extra * (1 + LINKS) + before, 0
                chain(dve.reciprocal(fin_r[0:R, 1:2], fin_r[0:R, 0:1]))
                if j >= 2:
                    dve.wait_ge(s[f"out_sent{j % 2}"], 16 * (j // 2))
                out = ybuf[0:R, j % 2, :]
                chain(dve.scalar_tensor_tensor(out, xg[0:R, j % 2, :], fin_r[0:R, 1:2], g2, ALU.mult, ALU.mult))
                dve.tensor_tensor(out, out, xrows(j), ALU.add).then_inc(s["out_ready"], 1)


_INS = ["x_prompt", "x_sample", "c_prompt", "c_sample", "state_pool", "state_hgrn", "w_ada", "b_ada", "g_pre_mix",
        "g_post_mix", "w_in", "w_pool", "pool_scale", "lb_logits", "g_out_norm", "w_out", "g_pre_ffn", "g_post_ffn",
        "w_router", "router_bias", "w_exp_gate", "w_exp_up", "w_exp_down", "w_sh_gate", "w_sh_up", "w_sh_down"]
_OUTS = [(1, 512, 1024), (8, 1, 1024), (1, 1, 15, 512), (1, 1, 4, 128, 128), (1, 8, 15, 512), (1, 8, 4, 128, 128)]


def kernel(**inputs):
    import numpy as np
    import concourse.bacc as bacc
    from concourse.bass_utils import run_bass_kernel_spmd

    nc = bacc.Bacc("TRN2", target_bir_lowering=False, num_devices=1)
    arrays, args = {}, []
    for name in _INS:
        a = np.ascontiguousarray(inputs[name])
        arrays[f"in_{name}"] = a
        args.append(nc.dram_tensor(f"in_{name}", a.shape, mybir.dt.from_np(a.dtype), kind="ExternalInput").ap())
    for n, shape in enumerate(_OUTS):
        args.append(nc.dram_tensor(f"out_{n}", shape, F32, kind="ExternalOutput").ap())
    args.append(nc.dram_tensor("h2_rows", (520, 1024), F32).ap())
    args.append(nc.dram_tensor("ff_rows", (520 + 128, 1024), F32).ap())
    build(nc, *args)
    r = run_bass_kernel_spmd(nc, [arrays], core_ids=[0])
    return tuple(r.results[0][f"out_{n}"] for n in range(len(_OUTS)))
```

```python
from contextlib import ExitStack

import concourse.bass as bass
from concourse import mybir

F32 = mybir.dt.float32
I32 = mybir.dt.int32
I8 = mybir.dt.int8
BF16 = mybir.dt.bfloat16
ALU = mybir.AluOpType
ACT = mybir.ActivationFunctionType
AX = mybir.AxisListType

P = 128
EPS = 1e-6
WINDOWS = (2, 4, 8, 16)
HIST = 15
TOP_K = 8
ROUTED_SCALE = 2.5
NEVER = 1024.0
LEVELS = (64, 32, 16, 8, 4, 2, 1)


class Chain:

    def __init__(self, engine, sem):
        self.engine, self.sem, self.count, self.base = engine, sem, 0, 0

    def __call__(self, instruction):
        instruction.then_inc(self.sem, 1)
        self.count += 1
        self.engine.wait_ge(self.sem, self.base + self.count)


def build(nc, x_prompt, x_sample, c_prompt, c_sample, state_pool, state_hgrn, w_ada, b_ada, g_pre_mix, g_post_mix,
          w_in, w_pool, pool_scale, lb_logits, g_out_norm, w_out, g_pre_ffn, g_post_ffn, w_router, router_bias,
          w_exp_gate, w_exp_up, w_exp_down, w_sh_gate, w_sh_up, w_sh_down,
          y_prompt, y_sample, pool_prompt, hgrn_prompt, pool_sample, hgrn_sample, h2_rows, ff_rows):
    D = x_prompt.shape[2]
    T = x_prompt.shape[1]
    NB = x_sample.shape[0]
    NT = T + NB
    KC = D // P
    PT = T // P
    TT = PT + 1
    NE = w_exp_gate.shape[1]
    NH = state_hgrn.shape[2]
    FE = w_exp_gate.shape[3]
    HALF = NT // 2
    N1 = NB + 1
    TRASH = NT
    ROWS = [P] * PT + [NB]
    MAX_EXTRA = NT * TOP_K // P
    MAX_TURNS = MAX_EXTRA // 4
    TAB = MAX_EXTRA + 8
    assert (D, T, NB, NE, NH, FE) == (1024, 512, 8, 64, 4, 256)

    ctx = ExitStack()
    with ctx:
        def sb(name, shape, dt=F32):
            return ctx.enter_context(nc.sbuf_tensor(name, shape, dt))

        def sem(name):
            return ctx.enter_context(nc.semaphore(name))

        ringA = sb("ringA", [P, 4, 4096])
        ringB = sb("ringB", [P, 4, 2048])
        late = sb("late", [P, 7680])
        bc = sb("bc", [P, 4096])
        mm = sb("mm", [P, 4, D])
        xt = sb("xt", [P, TT, D])
        actT = sb("actT", [P, KC, NT])
        ident = sb("ident", [P, P])
        ones = sb("ones", [P, P])
        tri = sb("tri", [P, P])
        iota = sb("iota", [P, P])
        masks = sb("masks", [P, 8, P], I8)
        tokw = sb("tokw", [P, NE, TT, 6], BF16)
        posm = sb("posm", [P, NE, TT])
        onehot = sb("onehot", [P, TT, P], BF16)
        wrt = sb("wrt", [P, KC, NE])
        rbias = sb("rbias", [P, NE])
        small = sb("small", [P, 448])
        gidx = sb("gidx", [P, 4], I32)
        sidx = sb("sidx", [P, 4], I32)
        table_i = sb("table_i", [P, TAB + 1], I32)

        iB = ringB[:, :, :].rearrange("p a b -> p (a b)")
        q = iB[:, 0:NH * NT].rearrange("p (h t) -> p h t", h=NH)
        f = iB[:, 2080:4160].rearrange("p (h t) -> p h t", h=NH)
        UW = HIST + NT
        u = iB[:, 4160:4160 + 4 * UW].rearrange("p (g t) -> p g t", g=4)
        b = iB[:, 6300:7324]
        wpool = iB[:, 7324:7836].rearrange("p (g d) -> p g d", g=4)
        m1 = iB[:, 0:2048]
        gate = late[:, 0:2080].rearrange("p (h t) -> p h t", h=NH)
        v = late[:, 2080:4640].rearrange("p (j c) -> p j c", j=TT)
        diffs = late[:, 4640:6720].rearrange("p (g t) -> p g t", g=4)
        kk = late[:, 4640:5680].rearrange("p (h t) -> p h t", h=2)
        att = late[:, 5680:6704].rearrange("p (c i) -> p c i", i=P)
        tmpS = late[:, 6720:7680]
        Dbuf = [bc[:, 0:1024], bc[:, 1024:2048], bc[:, 2048:3072]]
        khT = bc[:, 2048:3072]
        Sb = bc[:, 3072:4096].rearrange("p (h c v) -> p h c v", h=2, c=4)
        xn = [bc[:, 0:1024], bc[:, 1024:2048]]
        junk = bc[:, 2048:3072]
        hraw = bc[:, 3072:3584]
        histT = bc[:, 3584:4064].rearrange("p (g b r) -> p g b r", g=4, b=NB)
        cs = late[:, 0:1024]
        spent = actT[:, 0:4, :].rearrange("p k n -> p (k n)")
        gains = [spent[:, 0:1024], spent[:, 1024:2048], spent[:, 0:1024]]
        h2buf = late[:, 0:4096].rearrange("p (a n) -> p a n", a=4)
        modb = bc[:, :].rearrange("p (a n) -> p a n", a=4)
        xg = late[:, 0:2048].rearrange("p (a n) -> p a n", a=2)
        xT = late[:, 2048:4096].rearrange("p (a k n) -> p a k n", a=2, k=KC)
        ybuf = late[:, 4096:6144].rearrange("p (a n) -> p a n", a=2)
        sg = late[:, 6144:6656].rearrange("p (a n) -> p a n", a=2)
        hh = late[:, 6656:7168].rearrange("p (a n) -> p a n", a=2)
        hhT = late[:, 7168:7680].rearrange("p (a k n) -> p a k n", a=2, k=2)

        at = [0]

        def cut(n):
            at[0] += n
            return small[:, at[0] - n:at[0]]

        ss = cut(TT)
        rstd = cut(TT)
        cT = cut(KC * N1).rearrange("p (k r) -> p k r", k=KC)
        a1T = cut(KC * N1).rearrange("p (k r) -> p k r", k=KC)
        b1T = cut(KC * N1).rearrange("p (k r) -> p k r", k=KC)
        gpre = cut(KC)
        vecT = cut(13)
        lb = cut(NH)
        oml = cut(NH)
        lbt = cut(3 * NH)
        eps_c = cut(1)
        icnt = cut(16)
        dl = cut(8)
        kS = cut(NH * NB).rearrange("p (h b) -> p h b", h=NH)
        trash1 = cut(1)
        valid = cut(1)
        slot_sums = cut(8).rearrange("p (r a) -> p r a", a=2)
        idx_f = cut(2)
        qneg = cut(1)
        lower8 = cut(64)
        u_rows = tmpS[:, 448:960]
        zero_tile = ybuf[:, 0, :]
        fin = late[:, 0:5 * D].rearrange("p (j n) -> p j n", j=TT)
        fin_junk = late[:, 5 * D:6 * D]
        rt = [0]

        def routed(n):
            rt[0] += n
            return bc[:, rt[0] - n:rt[0]]

        def per_expert():
            return routed(TT * NE).rearrange("p (j e) -> p j e", j=TT)

        scores, sel, cmp1, cmp2, route_mask = (per_expert() for _ in range(5))
        sorted8 = routed(TT * 64).rearrange("p (j g r) -> p j g r", j=TT, g=8)
        gsc, grank, gmask, gpen, top8 = (routed(TT * 8).rearrange("p (j g) -> p j g", j=TT) for _ in range(5))
        tabrows = routed(2 * TAB)
        tabq = routed(TAB)
        tabi = routed(4)[0:NE]
        tabn = routed(1)[0:NE]
        tabd = routed(2)[0:NE]
        tab1 = routed(TAB)[0:NE]
        wpart = per_expert()
        turns8 = routed(8)
        assert rt[0] <= 3072

        ps = ctx.enter_context(nc.psum_tensor("ps", [P, 8, 512], F32))

        names = """in_small in_c in_x ringA_in0 ringA_in1 ringA_in2 ringA_in3 ringB_in0 ringB_in1 ringB_in2 ringB_in3
        consts_pool consts_dve pe_cT c_silu cT_ready ms_ready sq_ready rms_sqrt rstd_ready xn_ready x_turned x_evac_a x_evac_d
        ada_out ada_saved m1_turned m1T_ready mod_a mod_d lb_diff lb_exp lb_ready
        proj_out proj_a proj_d f_ready
        hist_in hist_turned hist_ready u_ready rows_turned rows_saved pool_d pool_y pool_saved rows_out hist_copy
        ln_done kk_ready b_ready diff_ready exp_done x_level level_out level_used qd_exp qd_ready kh_diff kh_exp kh_ready
        kh_turned khT_ready upd_out s_ready o_out o_sq o_ms o_r o_done hstate_out d_last
        s0_in s0_dec vb_out s_new so_out s_out so_sq so_ms so_r so_done
        gvec_in modrow_ready mod_out modb_ready mix_out mix_sq mix_sqrt mix_rstd x1_ready x1_sq x1_sqrt x1_rstd h2_ready h2_stored
        h2_turned h2T_a h2T_d logit_out score_ready route_m pos_out pos_read cnt_out table_in table_out table_ready
        up_done silu_done glu_done hh_turned hhT_ready down_done y_a y_d ff_init0 ff_init1 scattered zero_rows zeros_ready
        onehot_ready disp_out idx_ready gathered0 gathered1 x_turned2 xT_a xT_d
        ff_ready ff_in0 ff_in1 ff_in2 ff_in3 ff_in4 ff_sq ff_sqrt ff_rstd out_ready out_sent dve_chain act_chain pool_chain pool_passed""".split()
        s = {n: sem(n) for n in names}

        ypool_ps = ps[:, 4:6, 0:HALF]
        so_ps = ps[:, 6, 0:NH * NB]
        sms_ps = ps[:, 7, 0:NH * NB]
        logit_ps = ps[:, 7, 0:TT * NE].rearrange("p (j e) -> p j e", j=TT)

        def pair(i):
            return ps[:, 2 * i:2 * i + 2, :]

        def mix_ps(j):
            return pair((2, 1, 0, 1, 0)[j])

        def spread_ps(n):
            return pair(3 * (1 - n % 2))

        def ringA_k(slot):
            return ringA[:, slot, :].rearrange("p (k n) -> p k n", k=KC)

        def ringA_gu(slot):
            return ringA[:, slot, :].rearrange("p (a k n) -> p a k n", a=2, k=KC)

        def ringB_k(slot):
            return ringB[:, slot, :].rearrange("p (k n) -> p k n", k=2)

        pieces = [("ada", 512 * i) for i in range(4)]
        pieces += [("in", 0), ("in", 1024), ("in", 512), ("in", 1536), ("in", 2048)]
        pieces += [("ada", 2048 + 512 * i) for i in range(8)]
        pieces += [("out", 0), ("out", 512), ("shared", 0)]
        NPIECE = len(pieces)
        A_OUT, A_SHARED = 17, 19

        def used(p):
            if p < 4:
                return s["ada_out"], p + 1
            if p < 9:
                return s["proj_out"], (4, 8, 12, 12 + TT, 16 + TT)[p - 4]
            if p < A_OUT:
                return s["ada_out"], p - 4
            return (s["up_done"], TT) if p == A_SHARED else (s["mix_out"], TT)

        def piece_source(kind, col, half):
            if kind == "out":
                return w_out[0].rearrange("(k p) n -> p k n", p=P)[:, 4 * half:4 * half + 4, col:col + 512]
            w = {"ada": w_ada, "in": w_in}[kind]
            return w[0].rearrange("(p k) n -> p k n", k=KC)[:, 4 * half:4 * half + 4, col:col + 512]

        def arrived_a(eng, p):
            eng.wait_ge(s[f"ringA_in{p % 4}"], 32 * (p // 4 + 1))

        def state_slot(n):
            return Dbuf[(n // 2) % 2][:, 512 * (n % 2):512 * (n % 2) + 512].rearrange("p (h v) -> p h v", h=NH)

        def xrows(j):
            return xt[0:ROWS[j], j, :]

        block = ctx.enter_context(nc.Block())

        @block.sync
        def _(sp):
            sp.dma_start(cs[0:NB, :], c_sample).then_inc(s["in_c"], 16)
            sp.dma_start(cs[NB:N1, :], c_prompt).then_inc(s["in_c"], 16)
            sp.dma_start(xt[:, 0:PT, :], x_prompt[0].rearrange("(j p) d -> p j d", p=P)).then_inc(s["in_x"], 16)
            sp.dma_start(xt[0:NB, PT, :], x_sample[:, 0, :]).then_inc(s["in_x"], 16)

            def load_piece(p):
                kind, col = pieces[p]
                if p >= 4:
                    sp.wait_ge(*used(p - 4))
                for half in range(2):
                    if kind == "shared":
                        src = (w_sh_gate, w_sh_up)[half][0].rearrange("(p k) n -> p k n", k=KC)
                        dst = ringA_gu(p % 4)[:, half, :, :]
                    else:
                        src = piece_source(kind, col, half)
                        dst = ringA_k(p % 4)[:, 4 * half:4 * half + 4, :]
                    sp.dma_start(dst, src).then_inc(s[f"ringA_in{p % 4}"], 16)

            for p in range(NPIECE):
                load_piece(p)

            sp.wait_ge(s["o_done"], 2)
            sp.dma_start(ringB_k(0), w_sh_down[0].rearrange("(p k) n -> p k n", k=2)).then_inc(s["ringB_in0"], 16)

            def load_a(e, slot, e_dram):
                for half, w in enumerate((w_exp_gate, w_exp_up)):
                    sp.dma_start(ringA_gu(slot)[:, half, :, :],
                                 w[0, e_dram].rearrange("e (p k) n -> p (e k) n", k=KC)
                                 if not isinstance(e_dram, int) else w[0, e_dram].rearrange("(p k) n -> p k n", k=KC)
                                 ).then_inc(s[f"ringA_in{slot}"], 16)

            def load_b(e, slot, e_dram):
                src = w_exp_down[0, e_dram]
                src = (src.rearrange("(p k) n -> p k n", k=2) if isinstance(e_dram, int)
                       else src.rearrange("e (p k) n -> p (e k) n", k=2))
                sp.dma_start(ringB_k(slot), src).then_inc(s[f"ringB_in{slot}"], 16)

            for e in range(4):
                sp.wait_ge(*used(NPIECE - 4 + e))
                load_a(e, e, e)
                if e in (1, 2):
                    sp.wait_ge(s["mix_out"], TT)
                if e == 3:
                    sp.wait_ge(s["down_done"], TT)
                load_b(e, (1 + e) % 4, e)
            with sp.Fori(1, NE // 4) as i:
                for r in range(4):
                    e = i * 4 + r
                    sp.wait_ge(s["up_done"], e + 2)
                    load_a(e, r, bass.ds(e, 1))
                    sp.wait_ge(s["down_done"], e + 2)
                    load_b(e, (1 + r) % 4, bass.ds(e, 1))
            sp.wait_ge(s["table_ready"], 1)
            turns = sp.value_load(table_i[0:1, TAB:TAB + 1], min_val=1, max_val=MAX_TURNS)
            with sp.Fori(0, turns) as i:
                for r in range(4):
                    e = sp.value_load(table_i[0:1, bass.ds(i * 4 + r, 1)], min_val=0, max_val=NE - 1)
                    sp.wait_ge(s["up_done"], i * 4 + (NE + r + 2))
                    load_a(e, r, bass.ds(e, 1))
                    sp.wait_ge(s["down_done"], i * 4 + (NE + r + 2))
                    load_b(e, (1 + r) % 4, bass.ds(e, 1))

            for j in range(TT):
                sp.wait_ge(s["out_ready"], j + 1)
                dst = y_prompt[0, j * P:(j + 1) * P, :] if j < PT else y_sample[:, 0, :]
                sp.dma_start(dst, fin[0:ROWS[j], j, :]).then_inc(s["out_sent"], 16)
            sp.wait_ge(s["out_sent"], 16 * TT)
            sp.wait_ge(s["rows_out"], 48)
            sp.wait_ge(s["hstate_out"], 32)
            sp.wait_ge(s["s_out"], 16 * NB)

        @block.gpsimd
        def _(pool):
            chain = Chain(pool, s["pool_chain"])
            def small_in(dst, src):
                pool.dma_start(dst, src).then_inc(s["in_small"], 16)
            small_in(tmpS[0:8, 0:P], lb_logits.rearrange("a (h p) -> (a h) p", p=P))
            small_in(tmpS[8:12, 0:P], pool_scale[0].rearrange("(h p) -> h p", p=P))
            small_in(tmpS[12:13, 0:P], g_out_norm)
            small_in(gpre, g_pre_mix[0].rearrange("(p k) -> p k", k=KC))
            small_in(m1[0:N1, :], b_ada[0, 0:2048].partition_broadcast(N1))
            small_in(mm[0:N1, :, :].rearrange("r a n -> r (a n)"),
                     b_ada[0, 2048:6144].partition_broadcast(N1))
            small_in(rbias[:, :], router_bias[0, :].partition_broadcast(P))
            small_in(wrt[:, :, :], w_router[0].rearrange("(p k) e -> p k e", k=KC))
            small_in(wpool, w_pool[0].rearrange("g c d -> c g d"))
            small_in(hraw[0:NB * HIST, :], state_pool[0].rearrange("b r c -> (b r) c"))
            chain(pool.memset(ident[:, :], 0.0))
            chain(pool.affine_select(out=ident[:, :], in_=ident[:, :], compare_op=ALU.not_equal, fill=1.0, base=0,
                                     pattern=[[-1, P]], channel_multiplier=1))
            chain(pool.memset(tri[:, :], 0.0))
            chain(pool.affine_select(out=tri[:, :], in_=tri[:, :], compare_op=ALU.is_ge, fill=1.0, base=0,
                                     pattern=[[-1, P]], channel_multiplier=1))
            pool.iota(iota[:, :], pattern=[[1, P]], base=0, channel_multiplier=0,
                      allow_small_or_imprecise_dtypes=True)
            pool.iota(icnt, pattern=[[1, 16]], base=1, channel_multiplier=0, allow_small_or_imprecise_dtypes=True)
            pool.iota(trash1, pattern=[[0, 1]], base=TRASH + 1, channel_multiplier=1,
                      allow_small_or_imprecise_dtypes=True)
            pool.memset(tokw[:, :, :, 2], 0.0)
            pool.iota(tokw[:, :, :, 0], pattern=[[0, NE], [P, TT]], base=0, channel_multiplier=0,
                      allow_small_or_imprecise_dtypes=True)
            pool.iota(tokw[:, :, :, 1], pattern=[[0, NE], [0, TT]], base=1, channel_multiplier=1,
                      allow_small_or_imprecise_dtypes=True).then_inc(s["consts_pool"], 1)
            chain(pool.memset(lower8, 1.0))
            chain(pool.affine_select(out=lower8, in_=lower8, compare_op=ALU.is_gt, fill=0.0, base=0,
                                     pattern=[[1, 8], [-1, 8]], channel_multiplier=0))
            ones_u = masks[:, :, :]
            chain(pool.memset(ones_u, 0.0))
            m0 = masks[:, 0, :]
            chain(pool.affine_select(out=m0, in_=m0, compare_op=ALU.not_equal, fill=1.0, base=0,
                                     pattern=[[-1, P]], channel_multiplier=1))
            for n, half in enumerate(LEVELS):
                right = masks[:, n + 1, :].rearrange("p (b h r) -> p b h r", h=2, r=half)[:, :, 1, :]
                chain(pool.memset(right, 1.0))
                nb = P // (2 * half)
                chain(pool.affine_select(out=right, in_=right, compare_op=ALU.is_ge, fill=0.0, base=0,
                                         pattern=[[-2 * half, nb], [0, half]], channel_multiplier=1))
                last = pool.affine_select(out=right, in_=right, compare_op=ALU.is_ge, fill=0.0, base=half - 1,
                                          pattern=[[2 * half, nb], [0, half]], channel_multiplier=-1)
                if half > 1:
                    chain(last)
            last.then_inc(s["consts_pool"], 1)

            pool.wait_ge(s["u_ready"], 4)
            for g, w in enumerate(WINDOWS):
                src = u[:, g, 0:HIST + T]
                step = 1
                while step < w:
                    dst = (Dbuf[0] if src.offset != Dbuf[0].offset else Dbuf[1])[:, 0:HIST + T]
                    chain(pool.tensor_tensor(dst[:, 2 * step - 1:], src[:, 2 * step - 1:], src[:, step - 1:HIST + T - step], ALU.add))
                    src = dst
                    step *= 2
                diff = diffs[:, g, :]
                mean = src[:, HIST:]
                hs = tmpS[:, 0:NB]
                if g == 0:
                    pool.wait_ge(s["hist_ready"], 1)
                    pool.wait_ge(s["consts_dve"], 1)
                chain(pool.tensor_tensor(mean[:, 0:w - 1], mean[:, 0:w - 1], icnt[:, 0:w - 1], ALU.mult))
                chain(pool.tensor_scalar(mean[:, w - 1:], mean[:, w - 1:], 1.0 / w, None, ALU.mult))
                chain(pool.tensor_tensor(diff[:, 0:T], mean, u[:, g, HIST:HIST + T], ALU.subtract))
                hsum = tmpS[:, 256 + NB * g:256 + NB * g + NB]
                chain(pool.tensor_tensor(hs, hsum, u[:, g, HIST + T:UW], ALU.add))
                chain(pool.tensor_scalar(hs, hs, 1.0 / w, None, ALU.mult))
                pool.tensor_tensor(diff[:, T:NT], hs, u[:, g, HIST + T:UW], ALU.subtract).then_inc(s["pool_d"], 1)
            pool.dma_start(pool_sample[0, :, 0:HIST - 1, :], state_pool[0, :, 1:HIST, :]).then_inc(s["rows_out"], 16)
            def s0_load(n):
                pool.dma_start(state_slot(n),
                               state_hgrn[0, n].rearrange("h k v -> k h v")).then_inc(s["s0_in"], 16)
            pool.wait_ge(s["pool_d"], 4)
            for n in range(4):
                s0_load(n)
            pool.wait_ge(s["rows_saved"], 1)
            pool.dma_start(pool_prompt[0, 0, :, :], u_rows[0:HIST, :]).then_inc(s["rows_out"], 16)
            pool.dma_start(pool_sample[0, :, HIST - 1, :], u_rows[HIST:HIST + NB, :]).then_inc(s["rows_out"], 16)
            for n in range(NB):
                pool.wait_ge(s["s_new"], NH * (n + 1))
                pool.dma_start(hgrn_sample[0, n].rearrange("h k v -> k h v"),
                               Dbuf[(n // 2) % 2][:, 512 * (n % 2):512 * (n % 2) + 512].rearrange("p (h v) -> p h v", h=NH)
                               ).then_inc(s["s_out"], 16)
                if n + 4 < NB:
                    pool.wait_ge(s["s_out"], 16 * (n + 1))
                    pool.wait_ge(s["so_out"], n + 1)
                    s0_load(n + 4)
            def gain_in(n, g):
                pool.dma_start(gains[n][0:N1, :], g[0, :].partition_broadcast(N1)).then_inc(s["gvec_in"], 16)

            pool.wait_ge(s["proj_out"], 16 + TT)
            gain_in(0, g_post_mix)
            gain_in(1, g_pre_ffn)
            for hp in range(2):
                if hp == 1:
                    pool.wait_ge(s["modrow_ready"], 1)
                    gain_in(2, g_post_ffn)
                pool.wait_ge(s["b_ready"], hp + 1)
                for n, half in enumerate(LEVELS):
                    if n == 0:
                        pool.wait_ge(s["s_out"], 16 * NB)
                        pool.wait_ge(s["so_out"], NB)
                        if hp == 1:
                            pool.wait_ge(s["o_done"], 1)
                            pool.wait_ge(s["o_out"], 1)
                    if n >= 3:
                        pool.wait_ge(s["level_out"], 8 * hp + n - 1)
                    b4 = b.rearrange("p (b r) -> p b r", r=2 * half)
                    mid = b4[:, :, half - 1:half].to_broadcast([P, 1024 // (2 * half), 2 * half])
                    pool.tensor_tensor(Dbuf[(n + 1) % 3].rearrange("p (b r) -> p b r", r=2 * half), b4, mid,
                                       ALU.subtract).then_inc(s["diff_ready"], 1)
                pool.wait_ge(s["s_ready"], 8 * (hp + 1))
                pool.dma_start(hgrn_prompt[0, 0, 2 * hp:2 * hp + 2].rearrange("h k v -> k h v"),
                               Sb[:, :, 3, :]).then_inc(s["hstate_out"], 16)
            pool.wait_ge(s["zeros_ready"], 1)
            pool.dma_start(ff_rows[NT:NT + P, :], zero_tile).then_inc(s["zero_rows"], 16)
            for j in range(TT):
                pool.wait_ge(s["h2_ready"], j + 1)
                pool.dma_start(h2_rows[j * P:j * P + ROWS[j], :], h2buf[0:ROWS[j], j % 4, :]).then_inc(s["h2_stored"], 16)
                pool.wait_ge(s["h2_stored"], 16 * (j + 1))
            pool.wait_ge(s["h2_turned"], TT)
            chain(pool.memset(xg[:, :, :], 0.0))

            def waits_stand_alone():
                pool.sem_inc(s["pool_passed"], 1)

            def gather(e, r4, par):
                pool.wait_ge(s["idx_ready"], e + 1)
                waits_stand_alone()
                pool.indirect_dma_start(xg[:, par, :], None, h2_rows,
                                        bass.IndirectOffsetOnAxis(ap=gidx[:, r4:r4 + 1], axis=0),
                                        bounds_check=NT - 1, oob_is_err=False).then_inc(s[f"gathered{par}"], 16)

            def scatter(n, r4, par):
                pool.wait_ge(s["y_a"], n + 1)
                pool.wait_ge(s["y_d"], n + 1)
                waits_stand_alone()
                pool.indirect_dma_start(ff_rows, bass.IndirectOffsetOnAxis(ap=sidx[:, r4:r4 + 1], axis=0),
                                        ybuf[:, par, :], None, compute_op=ALU.add).then_inc(s["scattered"], 16)

            gather(0, 0, 0)
            gather(1, 1, 1)
            pool.wait_ge(s["x_turned2"], 1)
            gather(2, 2, 0)

            def step(e, r, first=False):
                pool.wait_ge(s["x_turned2"], e + 2)
                gather(e + 3, (r + 3) % 4, (r + 1) % 2)
                if not first:
                    if not isinstance(e, int) or e > 1:
                        pool.wait_ge(s["scattered"], (e - 1) * 16)
                    scatter(e + (TT - 1), (r + 3) % 4, r % 2)

            step(0, 0, first=True)
            pool.wait_ge(s["ff_init0"], 16 * 3)
            pool.wait_ge(s["ff_init1"], 16 * 2)
            pool.wait_ge(s["zero_rows"], 16)
            for e in range(1, 4):
                step(e, e)
            with pool.Fori(1, NE // 4) as i:
                for r in range(4):
                    step(i * 4 + r, r)
            turns = pool.value_load(table_i[0:1, TAB:TAB + 1], min_val=1, max_val=MAX_TURNS)
            with pool.Fori(0, turns) as i:
                for r in range(4):
                    step(i * 4 + (NE + r), r)
            pool.wait_ge(s["scattered"], turns * 64 + 16 * (NE - 1))
            scatter(turns * 4 + (TT + NE - 1), 3, 0)
            pool.wait_ge(s["scattered"], turns * 64 + 16 * NE)
            pool.wait_ge(s["gathered0"], turns * 32 + 16 * (NE // 2 + 1))
            pool.wait_ge(s["gathered1"], turns * 32 + 16 * (NE // 2 + 1))
            pool.wait_ge(s["x_turned2"], turns * 4 + NE + 1)
            pool.wait_ge(s["ff_ready"], 1)
            waits_stand_alone()
            for j in range(TT):
                pool.dma_start(fin[0:ROWS[j], j, :], ff_rows[j * P:j * P + ROWS[j], :]).then_inc(s[f"ff_in{j}"], 16)

        @block.scalar
        def _(act):
            act.wait_ge(s["in_c"], 32)
            act.activation(cs[0:N1, :], cs[0:N1, :], ACT.Silu).then_inc(s["c_silu"], 1)
            act.wait_ge(s["in_x"], 32)
            act.wait_ge(s["consts_dve"], 1)
            for j in range(TT):
                if j >= 1:
                    act.wait_ge(s["sq_ready"], j)
                act.activation(junk[0:ROWS[j], :], xrows(j), ACT.Square,
                               accum_out=ss[0:ROWS[j], j:j + 1]).then_inc(s["sq_ready"], 1)
            act.wait_ge(s["ms_ready"], 1)
            act.activation(rstd, ss, ACT.Sqrt).then_inc(s["rms_sqrt"], 1)
            act.wait_ge(s["rstd_ready"], 1)
            def normed(j):
                act.activation(xn[j % 2][0:ROWS[j], :], xrows(j), ACT.Copy,
                               scale=rstd[0:ROWS[j], j:j + 1]).then_inc(s["xn_ready"], 1)

            normed(0)
            normed(1)
            for j in range(TT):
                act.wait_ge(s["x_turned"], j + 1)
                if j + 2 < TT:
                    normed(j + 2)
                act.activation(actT[:, 0:4, j * P:j * P + ROWS[j]],
                               ps[:, 2 * (j % 2), :].rearrange("p (k n) -> p k n", k=4)[:, :, 0:ROWS[j]],
                               ACT.Copy).then_inc(s["x_evac_a"], 1)
            act.wait_ge(s["m1T_ready"], 1)
            act.wait_ge(s["x_evac_a"], TT)
            for k in range(4):
                act.activation(actT[:, k, 0:T], actT[:, k, 0:T], ACT.Identity, scale=a1T[:, k, NB:N1],
                               bias=b1T[:, k, NB:N1]).then_inc(s["mod_a"], 1)

            act.wait_ge(s["lb_diff"], 1)
            act.activation(lbt[:, 0:2 * NH], lbt[:, 0:2 * NH], ACT.Exp).then_inc(s["lb_exp"], 1)

            def two_halves(h):
                return pair(h)[:, :, 0:HALF]

            for n, (dst, func) in enumerate(((f, ACT.Sigmoid), (q, ACT.Silu))):
                for h in range(NH):
                    act.wait_ge(s["proj_out"], 4 + 4 * n + h + 1)
                    act.activation(dst[:, h, :].rearrange("p (a t) -> p a t", a=2), two_halves(h),
                                   func).then_inc(s["proj_a"], 1)
            for j in range(TT):
                act.wait_ge(s["proj_out"], 12 + j + 1)
                act.activation(v[0:ROWS[j], j, :], ps[0:ROWS[j], j, :], ACT.Copy).then_inc(s["proj_a"], 1)
            act.wait_ge(s["f_ready"], NH)
            for h in range(NH):
                for n in (2 * h, 2 * h + 1):
                    act.wait_ge(s["s0_in"], 16 * 4 if n < 4 else 16 * NB if n >= 6 else 16 * 6)
                    st = state_slot(n)
                    for h2 in range(NH):
                        act.activation(st[:, h2, :], st[:, h2, :], ACT.Copy, scale=f[:, h2, T + n:T + n + 1]
                                       ).then_inc(s["s0_dec"], 1)
                act.wait_ge(s["proj_out"], 12 + TT + h + 1)
                act.activation(gate[:, h, :].rearrange("p (a t) -> p a t", a=2), two_halves(h % 2),
                               ACT.Silu).then_inc(s["proj_a"], 1)
            act.wait_ge(s["so_out"], NB)
            act.activation(tmpS[:, 0:32], so_ps, ACT.Square).then_inc(s["so_sq"], 1)
            act.wait_ge(s["so_ms"], 1)
            act.activation(tmpS[:, 32:64], sms_ps, ACT.Ln, bias=eps_c, scale=1.0 / P).then_inc(s["act_chain"], 1)
            act.wait_ge(s["act_chain"], 1)
            act.activation(tmpS[:, 64:96], tmpS[:, 32:64], ACT.Exp, scale=-0.5).then_inc(s["so_r"], 1)

            for g in range(4):
                act.wait_ge(s["pool_y"], g + 1)
                act.activation(u[:, g, 0:NT].rearrange("p (a t) -> p a t", a=2), ypool_ps, ACT.Copy,
                               scale=vecT[:, 8 + g:9 + g]).then_inc(s["pool_saved"], 1)

            for hp in range(2):
                act.wait_ge(s["f_ready"], 4)
                if hp == 0:
                    act.wait_ge(s["s_out"], 16 * NB)
                else:
                    act.wait_ge(s["o_out"], 1)
                act.activation(Dbuf[0].rearrange("p (h t) -> p h t", h=2), f[:, 2 * hp:2 * hp + 2, 0:T],
                               ACT.Ln).then_inc(s["ln_done"], 1)
                for n, half in enumerate(LEVELS):
                    act.wait_ge(s["diff_ready"], 7 * hp + n + 1)
                    d4 = Dbuf[(n + 1) % 3].rearrange("p (b h r) -> p b h r", h=2, r=half)
                    act.activation(d4[:, :, 1, :], d4[:, :, 1, :], ACT.Exp)
                    act.activation(d4[:, :, 0, :], d4[:, :, 0, :], ACT.Exp, scale=-1.0).then_inc(s["exp_done"], 1)
                act.wait_ge(s["level_out"], 8 * hp + 8)
                act.activation(Dbuf[0], b, ACT.Exp).then_inc(s["qd_exp"], 1)
                act.activation(dl, b.rearrange("p (c t) -> p c t", t=P)[:, :, P - 1], ACT.Exp).then_inc(s["d_last"], 1)
                act.wait_ge(s["kh_diff"], hp + 1)
                act.activation(Dbuf[1], Dbuf[1], ACT.Exp).then_inc(s["kh_exp"], 1)
                act.wait_ge(s["kh_turned"], hp + 1)
                act.activation(khT.rearrange("p (a n) -> p a n", a=2), pair(3), ACT.Copy).then_inc(s["khT_ready"], 1)
                act.wait_ge(s["o_out"], hp + 1)
                act.activation(khT.rearrange("p (a n) -> p a n", a=2), pair(1), ACT.Square).then_inc(s["o_sq"], 1)
                act.wait_ge(s["o_ms"], hp + 1)
                act.activation(khT.rearrange("p (a n) -> p a n", a=2), pair(3), ACT.Ln, bias=eps_c, scale=1.0 / P).then_inc(s["act_chain"], 1)
                act.wait_ge(s["act_chain"], hp + 2)
                act.activation(khT, khT, ACT.Exp, scale=-0.5).then_inc(s["o_r"], 1)
            def modb_save(n):
                act.wait_ge(s["mod_out"], n + 1)
                act.activation(modb[:, n, :].rearrange("p (a n) -> p a n", a=2), spread_ps(n), ACT.Copy
                               ).then_inc(s["modb_ready"], 1)

            def squares(j):
                R = ROWS[j]
                act.wait_ge(s["mix_out"], j + 1)
                act.activation(ybuf[0:R, 1, :].rearrange("p (a n) -> p a n", a=2), mix_ps(j)[0:R], ACT.Square,
                               accum_out=ss[0:R, j:j + 1]).then_inc(s["mix_sq"], 1)
                act.wait_ge(s["mix_sqrt"], 2 * j + 1)
                act.activation(rstd[0:R, j:j + 1], ss[0:R, j:j + 1], ACT.Sqrt).then_inc(s["mix_rstd"], 1)
                act.wait_ge(s["x1_ready"], j + 1)
                act.activation(ybuf[0:R, 1, :], xrows(j), ACT.Square, accum_out=ss[0:R, j:j + 1]
                               ).then_inc(s["x1_sq"], 1)
                act.wait_ge(s["mix_sqrt"], 2 * j + 2)
                act.activation(rstd[0:R, j:j + 1], ss[0:R, j:j + 1], ACT.Sqrt).then_inc(s["x1_rstd"], 1)

            def h2T_half(j):
                act.wait_ge(s["h2_turned"], j + 1)
                act.activation(actT[:, 0:4, j * P:j * P + ROWS[j]],
                               ps[:, 5, :].rearrange("p (k n) -> p k n", k=4)[:, :, 0:ROWS[j]], ACT.Copy
                               ).then_inc(s["h2T_a"], 1)

            act.wait_ge(s["hstate_out"], 32)
            for n in range(3):
                modb_save(n)
            squares(0)
            modb_save(3)
            squares(1)
            h2T_half(0)
            squares(2)
            h2T_half(1)
            squares(3)
            h2T_half(2)
            squares(4)
            h2T_half(3)
            h2T_half(4)
            act.wait_ge(s["logit_out"], TT)
            act.wait_ge(s["zeros_ready"], 2)
            act.activation(scores[:, 0:PT, :], logit_ps[:, 0:PT, :], ACT.Sigmoid)
            act.activation(scores[0:NB, PT, :], logit_ps[0:NB, PT, :], ACT.Sigmoid).then_inc(s["score_ready"], 1)

            def silu(n, par, R=P):
                act.wait_ge(s["up_done"], n + 1)
                act.activation(sg[0:R, par, :], ps[0:R, 4 + par, 0:FE], ACT.Silu).then_inc(s["silu_done"], 1)

            def xT_half(e, par):
                act.wait_ge(s["x_turned2"], e + 1)
                act.activation(xT[:, par, 0:4, :], ps[:, 0, :].rearrange("p (k n) -> p k n", k=4), ACT.Copy
                               ).then_inc(s["xT_a"], 1)

            def y_half(n, par, R=P):
                act.wait_ge(s["down_done"], n + 1)
                act.activation(ybuf[0:R, par, 0:512], ps[0:R, 2, :], ACT.Copy).then_inc(s["y_a"], 1)

            def hhT_all(n, par, R=P):
                act.wait_ge(s["hh_turned"], n + 1)
                act.activation(hhT[:, par, :, 0:R], ps[:, 6, 0:256].rearrange("p (k n) -> p k n", k=2)[:, :, 0:R],
                               ACT.Copy).then_inc(s["hhT_ready"], 1)

            for n in range(TT):
                silu(n, n % 2, ROWS[n])
                if n >= 1:
                    if n >= 3:
                        act.wait_ge(s[f"ff_init{(n - 1) % 2}"], 16 * ((n - 1) // 2))
                    y_half(n - 1, (n - 1) % 2, ROWS[n - 1])
                    act.wait_ge(s["y_a"], n)
                    act.wait_ge(s["y_d"], n)
                    act.dma_start(ff_rows[(n - 1) * P:n * P, :], ybuf[:, (n - 1) % 2, :]
                                  ).then_inc(s[f"ff_init{(n - 1) % 2}"], 16)
                if n == TT - 1:
                    xT_half(0, 0)
                hhT_all(n, n % 2, ROWS[n])

            def step(e, r, first=False):
                n = e + TT
                silu(n, (r + 1) % 2)
                xT_half(e + 1, (r + 1) % 2)
                y_half(n - 1, r % 2, NB if first else P)
                if first:
                    act.wait_ge(s["y_a"], TT)
                    act.wait_ge(s["y_d"], TT)
                    act.dma_start(ff_rows[PT * P:NT, :], ybuf[0:NB, r % 2, :]).then_inc(s["ff_init0"], 16)
                hhT_all(n, (r + 1) % 2)

            act.wait_ge(s["ff_init0"], 16 * 2)
            step(0, 0, first=True)
            act.wait_ge(s["ff_init1"], 16 * 2)
            step(1, 1)
            act.wait_ge(s["ff_init0"], 16 * 3)
            step(2, 2)
            act.wait_ge(s["scattered"], 16)
            step(3, 3)
            with act.Fori(1, NE // 4) as i:
                for r in range(4):
                    e = i * 4 + r
                    act.wait_ge(s["scattered"], (e - 2) * 16)
                    step(e, r)
            turns = act.value_load(table_i[0:1, TAB:TAB + 1], min_val=1, max_val=MAX_TURNS)
            with act.Fori(0, turns) as i:
                for r in range(4):
                    e = i * 4 + (NE + r)
                    act.wait_ge(s["scattered"], (e - 2) * 16)
                    step(e, r)
            act.wait_ge(s["scattered"], turns * 64 + 16 * (NE - 2))
            y_half(turns * 4 + (TT + NE - 1), 0)
            for j in range(TT):
                R = ROWS[j]
                act.wait_ge(s[f"ff_in{j}"], 16)
                if j >= 1:
                    act.wait_ge(s["ff_sq"], j)
                act.activation(fin_junk[0:R, :], fin[0:R, j, :], ACT.Square, accum_out=ss[0:R, j:j + 1]
                               ).then_inc(s["ff_sq"], 1)
                act.wait_ge(s["ff_sqrt"], j + 1)
                act.activation(rstd[0:R, j:j + 1], ss[0:R, j:j + 1], ACT.Sqrt).then_inc(s["ff_rstd"], 1)

        @block.tensor
        def _(pe):
            pe.wait_ge(s["consts_pool"], 1)
            pe.wait_ge(s["c_silu"], 1)
            for k in range(KC):
                mt = pe.transpose(ps[:, 7, k * N1:(k + 1) * N1], cs[0:N1, k::KC], ident[0:N1, 0:N1])
            mt.then_inc(s["pe_cT"], 1)
            def ada(n, p):
                arrived_a(pe, p)
                if n >= 2:
                    pe.wait_ge(s["ada_saved"], n - 1)
                for k in range(KC):
                    mt = pe.matmul(ps[0:N1, 4 + n % 2, :], cT[:, k, :], ringA_k(p % 4)[:, k, :],
                                   start=k == 0, stop=k == KC - 1)
                mt.then_inc(s["ada_out"], 1)

            pe.wait_ge(s["cT_ready"], 1)
            ada(0, 0)
            ada(1, 1)
            for j in range(TT):
                pe.wait_ge(s["xn_ready"], j + 1)
                if j >= 2:
                    pe.wait_ge(s["x_evac_a"], j - 1)
                    pe.wait_ge(s["x_evac_d"], j - 1)
                for k in range(KC):
                    R = ROWS[j]
                    mt = pe.transpose(ps[:, 2 * (j % 2) + k // 4, (k % 4) * P:(k % 4) * P + R],
                                      xn[j % 2][0:R, k::KC], ident[0:R, 0:R])
                mt.then_inc(s["x_turned"], 1)
            ada(2, 2)
            ada(3, 3)
            pe.wait_ge(s["in_small"], 160)
            pe.transpose(ps[:, 6, 480:493], tmpS[0:13, 0:P], ident[0:13, 0:13])
            for g in range(4):
                mt = pe.transpose(ps[:, 6, NB * HIST * g:NB * HIST * (g + 1)], hraw[0:NB * HIST, g * P:(g + 1) * P],
                                  ident[0:NB * HIST, 0:NB * HIST])
            mt.then_inc(s["hist_turned"], 1)

            pe.wait_ge(s["ada_saved"], 4)
            for n in range(2):
                for k in range(KC):
                    mt = pe.transpose(ps[:, 7, 144 + (n * KC + k) * N1:144 + (n * KC + k + 1) * N1],
                                      m1[0:N1, n * D + k:(n + 1) * D:KC], ident[0:N1, 0:N1])
            mt.then_inc(s["m1_turned"], 1)

            pe.wait_ge(s["mod_a"], 4)
            pe.wait_ge(s["mod_d"], 1)
            def spread_v(n):
                if n == 0:
                    pe.wait_ge(s["proj_a"], 8 + TT)
                if n == 1:
                    pe.wait_ge(s["rows_saved"], 1)
                if n >= 2:
                    pe.wait_ge(s["s_new"], NH * (n - 1))
                pe.matmul(ps[:, 4 + n % 2, :], ident[0:NB, n:n + 1].to_broadcast([NB, P]), v[0:NB, PT, :],
                          start=True, stop=True).then_inc(s["vb_out"], 1)

            def read_state(n):
                pe.wait_ge(s["s_new"], NH * (n + 1))
                for h in range(NH):
                    mt = pe.matmul(ps[:, 6, h * NB + n:h * NB + n + 1], state_slot(n)[:, h, :],
                                   q[:, h, T + n:T + n + 1], start=True, stop=True)
                mt.then_inc(s["so_out"], 1)

            for n in range(5):
                p = 4 + n
                if n == 4:
                    pe.wait_ge(s["proj_a"], 8)
                    for g in range(4):
                        mt = pe.transpose(ps[0:HIST + NB, 5, g * P:(g + 1) * P], u[:, g, T:UW], ident[:, :])
                    mt.then_inc(s["rows_turned"], 1)
                arrived_a(pe, p)
                w = ringA_k(p % 4)
                if n == 3:
                    for j in range(TT):
                        if j % 2 == 0:
                            pe.wait_ge(s["proj_a"], 4 + j // 2 + 1)
                        for k in range(KC):
                            mt = pe.matmul(ps[0:ROWS[j], j, :], actT[:, k, j * P:j * P + ROWS[j]], w[:, k, :],
                                           start=k == 0, stop=k == KC - 1)
                        mt.then_inc(s["proj_out"], 1)
                else:
                    for h in range(NH):
                        if n == 0 and h == 0:
                            pe.wait_ge(s["x_evac_a"], TT)
                            pe.wait_ge(s["x_evac_d"], TT)
                        if n == 0 and h == 3:
                            pe.wait_ge(s["hist_ready"], 1)
                            pe.wait_ge(s["m1T_ready"], 1)
                        if n == 1:
                            pe.wait_ge(s["u_ready"], h + 1)
                        if n == 2:
                            pe.wait_ge(s["proj_a"], h + 1)
                        bank = 2 * h
                        if n == 4:
                            bank = 2 * (h % 2)
                            pe.wait_ge(s["proj_a"], 8 + (2, 4, TT + 1, TT + 2)[h])
                            spread_v(2 * h)
                            spread_v(2 * h + 1)
                        for half in range(2):
                            for k in range(KC):
                                mt = pe.matmul(ps[:, bank + half, 0:HALF], w[:, k, h * P:(h + 1) * P],
                                               actT[:, k, half * HALF:(half + 1) * HALF],
                                               start=k == 0, stop=k == KC - 1)
                        mt.then_inc(s["proj_out"], 1)
                        if n == 4:
                            read_state(2 * h)
                            read_state(2 * h + 1)
            pe.wait_ge(s["so_sq"], 1)
            pe.matmul(ps[:, 7, 0:32], ones[:, :], tmpS[:, 0:32], start=True, stop=True).then_inc(s["so_ms"], 1)
            pe.wait_ge(s["proj_a"], 8 + TT + 4)

            for g in range(4):
                pe.wait_ge(s["pool_d"], g + 1)
                if g >= 1:
                    pe.wait_ge(s["pool_saved"], g)
                diff = diffs[:, g, :]
                for half in range(2):
                    mt = pe.matmul(ps[:, 4 + half, 0:HALF], wpool[:, g, :], diff[:, half * HALF:(half + 1) * HALF],
                                   start=True, stop=True)
                mt.then_inc(s["pool_y"], 1)

            ada_n = [4]

            def more_ada():
                if ada_n[0] < 12:
                    ada(ada_n[0], ada_n[0] + 5)
                    ada_n[0] += 1

            pe.wait_ge(s["pool_saved"], 4)
            for hp in range(2):
                for n in range(8):
                    g = 8 * hp + n
                    if g == 0:
                        pe.wait_ge(s["kk_ready"], 1)
                    if n == 0 and hp == 1:
                        pe.wait_ge(s["kk_ready"], 2)
                        pe.wait_ge(s["o_done"], 1)
                    if n >= 1:
                        pe.wait_ge(s["x_level"], 7 * hp + n)
                    if g >= 2:
                        pe.wait_ge(s["level_used"], g - 1)
                    for h in range(2):
                        for c in range(PT):
                            if n == 0:
                                left = kk[:, h, c * P:(c + 1) * P]
                                right = q[:, 2 * hp + h, c * P:(c + 1) * P]
                            else:
                                left = right = Dbuf[n % 3][:, h * T + c * P:h * T + (c + 1) * P]
                            mt = pe.matmul(ps[:, 2 * (n % 2) + h, c * P:(c + 1) * P], left, right, start=True, stop=True)
                    mt.then_inc(s["level_out"], 1)
                    if n % 2 == 1:
                        more_ada()
                pe.wait_ge(s["kh_ready"], hp + 1)
                if hp == 0:
                    pe.wait_ge(s["so_done"], 1)
                for hc in range(8):
                    mt = pe.transpose(ps[:, 6 + hc // 4, (hc % 4) * P:(hc % 4 + 1) * P], Dbuf[1][:, hc * P:(hc + 1) * P],
                                      ident[:, :])
                mt.then_inc(s["kh_turned"], 1)
                pe.wait_ge(s["khT_ready"], hp + 1)
                pe.wait_ge(s["level_used"], 8 * hp + 8)
                for h in range(2):
                    for c in range(PT):
                        mt = pe.matmul(ps[:, h, c * P:(c + 1) * P], khT[:, (4 * h + c) * P:(4 * h + c + 1) * P],
                                       v[:, c, (2 * hp + h) * P:(2 * hp + h + 1) * P], start=True, stop=True)
                mt.then_inc(s["upd_out"], 1)
                pe.wait_ge(s["qd_ready"], hp + 1)
                pe.wait_ge(s["s_ready"], 8 * (hp + 1))
                for h in range(2):
                    for c in range(PT):
                        out = ps[:, 2 + h, c * P:(c + 1) * P]
                        mt = pe.matmul(out, v[:, c, (2 * hp + h) * P:(2 * hp + h + 1) * P], att[:, 4 * h + c, :],
                                       start=True, stop=c == 0)
                        if c >= 1:
                            mt = pe.matmul(out, Sb[:, h, c - 1, :], Dbuf[0][:, (4 * h + c) * P:(4 * h + c + 1) * P],
                                           start=False, stop=True)
                mt.then_inc(s["o_out"], 1)
                pe.wait_ge(s["o_sq"], hp + 1)
                for h in range(2):
                    mt = pe.matmul(ps[:, 6 + h, :], ones[:, :], khT[:, h * T:(h + 1) * T], start=True, stop=True)
                mt.then_inc(s["o_ms"], 1)
            while ada_n[0] < 12:
                more_ada()
            def spread_mod(n):
                if n >= 2:
                    pe.wait_ge(s["modb_ready"], n - 1)
                for half in range(2):
                    mt = pe.matmul(spread_ps(n)[:, half, :], ident[0:N1, NB:N1].to_broadcast([N1, P]),
                                   mm[0:N1, n, half * 512:(half + 1) * 512], start=True, stop=True)
                mt.then_inc(s["mod_out"], 1)

            def project_half(j, half, ks):
                for k in ks:
                    left = (u if k < 4 else actT)[:, k, j * P:j * P + ROWS[j]]
                    mt = pe.matmul(mix_ps(j)[0:ROWS[j], half, :], left, ringA_k((A_OUT + half) % 4)[:, k, :],
                                   start=k == 0, stop=k == KC - 1)
                return mt

            def project_out(j):
                if j == 2:
                    pe.wait_ge(s["modb_ready"], 4)
                if j >= 3:
                    pe.wait_ge(s["x1_ready"], j - 1)
                for half in range(2):
                    mt = project_half(j, half, range(KC))
                mt.then_inc(s["mix_out"], 1)

            def turn_h2(j):
                R = ROWS[j]
                if j == 0:
                    pe.wait_ge(s["x1_ready"], 1)
                pe.wait_ge(s["h2_ready"], j + 1)
                if j >= 1:
                    pe.wait_ge(s["h2T_a"], j)
                    pe.wait_ge(s["h2T_d"], j)
                for k in range(KC):
                    mt = pe.transpose(ps[:, 5 + k // 4, (k % 4) * P:(k % 4) * P + R], h2buf[0:R, j % 4, k::KC],
                                      ident[0:R, 0:R])
                mt.then_inc(s["h2_turned"], 1)

            def route(j):
                R = ROWS[j]
                pe.wait_ge(s["h2T_a"], j + 1)
                pe.wait_ge(s["h2T_d"], j + 1)
                for k in range(KC):
                    mt = pe.matmul(ps[0:R, 7, j * NE:(j + 1) * NE], actT[:, k, j * P:j * P + R], wrt[:, k, :],
                                   start=k == 0, stop=k == KC - 1)
                mt.then_inc(s["logit_out"], 1)

            def up(n, par, left, slot, R=P):
                if n_static(n, 2):
                    pe.wait_ge(s["glu_done"], n - 1)
                for k in range(KC):
                    mt = pe.matmul(ps[0:R, 4 + par, :].rearrange("p (a n) -> p a n", a=2), left(k),
                                   ringA_gu(slot)[:, :, k, :], start=k == 0, stop=k == KC - 1)
                mt.then_inc(s["up_done"], 1)

            def n_static(n, least):
                return not isinstance(n, int) or n >= least

            def down(n, par, slot, R=P):
                pe.wait_ge(s["hhT_ready"], n + 1)
                if n_static(n, 1):
                    pe.wait_ge(s["y_a"], n)
                    pe.wait_ge(s["y_d"], n)
                for half in range(2):
                    for k in range(2):
                        mt = pe.matmul(ps[0:R, 2 + half, :], hhT[:, par, k, 0:R],
                                       ringB_k(slot)[:, k, half * 512:(half + 1) * 512], start=k == 0, stop=k == 1)
                mt.then_inc(s["down_done"], 1)

            def turn_hh(n, par, R=P):
                pe.wait_ge(s["glu_done"], n + 1)
                if n_static(n, 1):
                    pe.wait_ge(s["hhT_ready"], n)
                for k in range(2):
                    mt = pe.transpose(ps[:, 6, k * P:k * P + R], hh[0:R, par, k::2], ident[0:R, 0:R])
                mt.then_inc(s["hh_turned"], 1)

            def turn_x(e, par, gathers):
                pe.wait_ge(s[f"gathered{par}"], gathers)
                if n_static(e, 1):
                    pe.wait_ge(s["xT_a"], e)
                    pe.wait_ge(s["xT_d"], e)
                for k in range(KC):
                    mt = pe.transpose(ps[:, k // 4, (k % 4) * P:(k % 4 + 1) * P], xg[:, par, k::KC], ident[:, :])
                mt.then_inc(s["x_turned2"], 1)

            def dispatch(e, tok):
                pe.wait_ge(s["onehot_ready"], e + 1)
                if n_static(e, 1):
                    pe.wait_ge(s["idx_ready"], e)
                for j in range(TT):
                    mt = pe.matmul(ps[:, 7, 0:6], onehot[:, j, :], tok(j), start=j == 0, stop=j == TT - 1)
                mt.then_inc(s["disp_out"], 1)

            def tok_static(e):
                return lambda j: tokw[:, e, j, :]

            def shared_up(n):
                if n == 0:
                    arrived_a(pe, A_SHARED)
                up(n, n % 2, lambda k: actT[:, k, n * P:n * P + ROWS[n]], A_SHARED % 4, ROWS[n])

            arrived_a(pe, A_OUT)
            arrived_a(pe, A_OUT + 1)
            pe.wait_ge(s["ada_saved"], 12)
            for half in range(2):
                project_half(0, half, range(4))
            pe.wait_ge(s["o_done"], 2)
            for half in range(2):
                mt = project_half(0, half, range(4, KC))
            mt.then_inc(s["mix_out"], 1)
            pe.wait_ge(s["modrow_ready"], 3)
            spread_mod(0)
            spread_mod(1)
            spread_mod(2)
            project_out(1)
            spread_mod(3)
            project_out(2)
            turn_h2(0)
            project_out(3)
            turn_h2(1)
            route(0)
            project_out(4)
            turn_h2(2)
            route(1)
            turn_h2(3)
            route(2)
            shared_up(0)
            turn_h2(4)
            route(3)
            route(4)
            pe.wait_ge(s["h2T_a"], TT)
            shared_up(1)
            pe.wait_ge(s["route_m"], 1)
            for j in range(TT):
                for j2 in range(j + 1):
                    mt = pe.matmul(ps[:, 7, j * NE:(j + 1) * NE], tri[:, :] if j2 == j else ones[:, :],
                                   route_mask[:, j2, :], start=j2 == 0, stop=j2 == j)
            for j in range(TT):
                mt = pe.matmul(ps[0:NE, 7, 320:321], route_mask[:, j, :], ones[:, 0:1], start=j == 0, stop=j == TT - 1)
            mt.then_inc(s["pos_out"], 1)
            turn_hh(0, 0)
            pe.wait_ge(s["ringB_in0"], 16)
            down(0, 0, 0)
            turn_hh(1, 1)
            for n in range(2, TT):
                shared_up(n)
                down(n - 1, (n - 1) % 2, 0)
                if n == 2:
                    pe.wait_ge(s["cnt_out"], 1)
                    pe.matmul(ps[0:NE, 0, 328:329], tri[0:NE, 0:NE], tabn, start=True, stop=True)
                    pe.matmul(ps[:, 0, 336:337], ones[0:NE, :], tabn, start=True, stop=True).then_inc(s["table_in"], 1)
                if n == 3:
                    pe.wait_ge(s["cnt_out"], 2)
                    pe.matmul(ps[:, 0, 352:352 + 2 * TAB], ones[0:NE, :], tabrows[0:NE, :], start=True, stop=True
                              ).then_inc(s["table_out"], 1)
                if n == TT - 1:
                    pe.wait_ge(s["table_ready"], 1)
                    turn_x(0, 0, 16)
                dispatch(n - 2, tok_static(n - 2))
                turn_hh(n, n % 2, ROWS[n])

            def tok_at(e):
                return lambda j: tokw[:, bass.ds(e, 1), j, :].rearrange("p e n -> p (e n)")

            def step(e, r, g, nxt, first=False):
                n = e + TT
                pe.wait_ge(s["xT_a"], e + 1)
                pe.wait_ge(s["xT_d"], e + 1)
                in_a(r, g)
                up(n, (r + 1) % 2, lambda k: xT[:, r % 2, k, :], r)
                turn_x(e + 1, (r + 1) % 2, g * 32 + 16 * ((r + 1) // 2 + 1))
                dispatch(e + 3, tok_static(nxt) if isinstance(nxt, int) else tok_at(nxt))
                in_b(r, g)
                down(n - 1, r % 2, r % 4, NB if first else P)
                turn_hh(n, (r + 1) % 2)

            def in_a(r, g):
                pe.wait_ge(s[f"ringA_in{r}"], g * 32 + 32 * 6)

            def in_b(r, g):
                pe.wait_ge(s[f"ringB_in{r}"], g * 16 + 16)

            def extra_expert(n):
                return pe.value_load(table_i[0:1, n:n + 1] if isinstance(n, int) else table_i[0:1, bass.ds(n, 1)],
                                     min_val=0, max_val=NE - 1)

            for r in range(4):
                step(r, r, 0, r + 3, first=r == 0)
            with pe.Fori(1, NE // 4 - 1) as i:
                for r in range(4):
                    step(i * 4 + r, r, i, i * 4 + (r + 3))
            for r in range(4):
                step(NE - 4 + r, r, NE // 4 - 1, NE - 1 if r == 0 else extra_expert(r - 1))
            turns = pe.value_load(table_i[0:1, TAB:TAB + 1], min_val=1, max_val=MAX_TURNS)
            with pe.Fori(0, turns) as i:
                for r in range(4):
                    nxt = extra_expert(i * 4 + (r + 3))
                    step(i * 4 + (NE + r), r, i + NE // 4, nxt)
            in_b(0, turns + NE // 4)
            down(turns * 4 + (TT + NE - 1), 0, 0)

        @block.vector
        def _(dve):
            chain = Chain(dve, s["dve_chain"])
            dve.memset(ones[:, :], 1.0)
            dve.memset(eps_c, EPS)
            dve.wait_ge(s["consts_pool"], 1)
            chain(dve.memset(ss, 1.0))
            chain(dve.tensor_scalar(valid, trash1, float(TRASH + 1 + NB), None, ALU.is_lt))
            dve.reciprocal(icnt, icnt).then_inc(s["consts_dve"], 1)
            dve.wait_ge(s["pe_cT"], 1)
            dve.tensor_copy(cT, ps[:, 7, 0:KC * N1].rearrange("p (k r) -> p k r", k=KC)).then_inc(s["cT_ready"], 1)
            dve.wait_ge(s["sq_ready"], TT)
            dve.tensor_scalar(ss, ss, 1.0 / D, EPS, ALU.mult, ALU.add).then_inc(s["ms_ready"], 1)
            dve.wait_ge(s["rms_sqrt"], 1)
            dve.reciprocal(rstd, rstd).then_inc(s["rstd_ready"], 1)
            for j in range(TT):
                dve.wait_ge(s["x_turned"], j + 1)
                dve.tensor_copy(actT[:, 4:8, j * P:j * P + ROWS[j]],
                                ps[:, 2 * (j % 2) + 1, :].rearrange("p (k n) -> p k n", k=4)[:, :, 0:ROWS[j]]
                                ).then_inc(s["x_evac_d"], 1)
            def ada_save(n, p, dst):
                dve.wait_ge(s["ada_out"], n + 1)
                dve.tensor_tensor(dst, ps[0:N1, 4 + n % 2, :], dst, ALU.add).then_inc(s["ada_saved"], 1)

            dve.wait_ge(s["in_small"], 160)
            for n in range(4):
                ada_save(n, n, m1[0:N1, 512 * n:512 * n + 512])
            dve.wait_ge(s["m1_turned"], 1)
            m1T = ps[:, 7, 144:144 + 2 * KC * N1].rearrange("p (a k r) -> p a k r", a=2, k=KC)
            dve.tensor_copy(b1T, m1T[:, 0])
            chain(dve.tensor_scalar(a1T, m1T[:, 1], 1.0, None, ALU.add))
            chain(dve.tensor_tensor(a1T, a1T, gpre.unsqueeze(2).to_broadcast([P, KC, N1]), ALU.mult))
            dve.sem_inc(s["m1T_ready"], 1)
            dve.wait_ge(s["x_evac_d"], TT)
            for k in range(4, KC):
                dve.tensor_scalar(actT[:, k, 0:T], actT[:, k, 0:T], a1T[:, k, NB:N1], b1T[:, k, NB:N1], ALU.mult, ALU.add)
            dve.wait_ge(s["x_evac_a"], TT)
            chain(dve.tensor_tensor(actT[:, :, T:NT], actT[:, :, T:NT], a1T[:, :, 0:NB], ALU.mult))
            dve.tensor_tensor(actT[:, :, T:NT], actT[:, :, T:NT], b1T[:, :, 0:NB], ALU.add).then_inc(s["mod_d"], 1)
            dve.wait_ge(s["hist_turned"], 1)
            dve.tensor_copy(vecT, ps[:, 6, 480:493])
            chain(dve.tensor_copy(histT, ps[:, 6, 0:4 * NB * HIST].rearrange("p (g b r) -> p g b r", g=4, b=NB)))
            for g, w in enumerate(WINDOWS):
                last = dve.tensor_reduce(tmpS[:, 256 + NB * g:256 + NB * g + NB], histT[:, g, :, HIST - (w - 1):HIST],
                                         AX.X, ALU.add)
            last.then_inc(s["hist_ready"], 1)
            chain(dve.tensor_tensor(lbt[:, 8:12], vecT[:, 0:4], vecT[:, 4:8], ALU.max))
            dve.tensor_tensor(lbt[:, 0:4], vecT[:, 0:4], lbt[:, 8:12], ALU.subtract)
            dve.tensor_tensor(lbt[:, 4:8], vecT[:, 4:8], lbt[:, 8:12], ALU.subtract).then_inc(s["lb_diff"], 1)
            dve.wait_ge(s["lb_exp"], 1)
            chain(dve.tensor_tensor(lbt[:, 8:12], lbt[:, 0:4], lbt[:, 4:8], ALU.add))
            chain(dve.reciprocal(lbt[:, 8:12], lbt[:, 8:12]))
            chain(dve.tensor_tensor(lb, lbt[:, 0:4], lbt[:, 8:12], ALU.mult))
            chain(dve.tensor_scalar(oml, lb, -1.0, 1.0, ALU.mult, ALU.add))

            for g in range(4):
                if g == 0:
                    dve.memset(u[:, :, 0:HIST], 0.0)
                dve.wait_ge(s["proj_out"], g + 1)
                dve.tensor_copy(u[:, g, HIST:UW].rearrange("p (a t) -> p a t", a=2), pair(g)[:, :, 0:HALF]
                                ).then_inc(s["u_ready"], 1)
            for h in range(NH):
                dve.wait_ge(s["proj_a"], h + 1)
                dve.tensor_scalar(f[:, h, :], f[:, h, :], oml[:, h:h + 1], lb[:, h:h + 1], ALU.mult, ALU.add
                                  ).then_inc(s["f_ready"], 1)
            dve.wait_ge(s["f_ready"], 4)
            chain(dve.tensor_scalar(kS, f[:, :, T:NT], -1.0, 1.0, ALU.mult, ALU.add))
            dve.wait_ge(s["rows_turned"], 1)
            dve.tensor_copy(u_rows[0:HIST + NB, :], ps[0:HIST + NB, 5, :]).then_inc(s["rows_saved"], 1)
            for n in range(NB):
                dve.wait_ge(s["vb_out"], n + 1)
                dve.wait_ge(s["s0_dec"], NH * (n + 1))
                st = state_slot(n)
                for h in range(NH):
                    dve.scalar_tensor_tensor(st[:, h, :], ps[:, 4 + n % 2, h * P:(h + 1) * P], kS[:, h, n:n + 1],
                                             st[:, h, :], ALU.mult, ALU.add).then_inc(s["s_new"], 1)
            dve.wait_ge(s["so_sq"], 1)
            dve.wait_ge(s["proj_a"], 12 + TT)
            oS = actT[:, 4:8, T:NT]
            chain(dve.scalar_tensor_tensor(oS, so_ps.rearrange("p (h b) -> p h b", h=NH), vecT[:, 12:13],
                                           gate[:, :, T:NT], ALU.mult, ALU.mult))
            dve.wait_ge(s["so_r"], 1)
            chain(dve.tensor_tensor(oS, oS, tmpS[:, 64:96].rearrange("p (h b) -> p h b", h=NH), ALU.mult))
            dve.sem_inc(s["so_done"], 1)

            ada_n = [4]

            def more_ada():
                n = ada_n[0]
                if n < 12:
                    ada_save(n, n + 5, mm[0:N1, (n - 4) // 2, 512 * (n % 2):512 * (n % 2) + 512])
                    ada_n[0] += 1

            dve.wait_ge(s["pool_y"], 4)
            for hp in range(2):
                hs = slice(2 * hp, 2 * hp + 2)
                dve.tensor_scalar(kk, f[:, hs, :], -1.0, 1.0, ALU.mult, ALU.add).then_inc(s["kk_ready"], 1)
                dve.wait_ge(s["kk_ready"], hp + 1)
                chain(dve.memset(att, 0.0))
                dve.wait_ge(s["ln_done"], hp + 1)
                for c in range(8):
                    last = dve.tensor_tensor_scan(b[:, c * P:(c + 1) * P], ones[:, :], Dbuf[0][:, c * P:(c + 1) * P],
                                                  0.0, ALU.mult, ALU.add)
                last.then_inc(s["b_ready"], 1)
                dve.wait_ge(s["b_ready"], hp + 1)

                def times(n):
                    half = LEVELS[n]
                    dve.wait_ge(s["exp_done"], 7 * hp + n + 1)
                    for side, src in ((1, q[:, hs, 0:T]), (0, kk[:, :, 0:T])):
                        d4 = Dbuf[(n + 1) % 3].rearrange("p (x h r) -> p x h r", h=2, r=half)[:, :, side, :]
                        s4 = src.rearrange("p a (x h r) -> p a x h r", h=2, r=half)[:, :, :, side, :]
                        last = dve.tensor_tensor(d4.rearrange("p (a x) r -> p a x r", a=2), d4.rearrange("p (a x) r -> p a x r", a=2),
                                                 s4, ALU.mult)
                    last.then_inc(s["x_level"], 1)

                def keep(n):
                    dve.wait_ge(s["level_out"], 8 * hp + n + 1)
                    if n >= 1:
                        dve.wait_ge(s["level_used"], 8 * hp + n)
                    dve.copy_predicated(att, masks[:, n, :].unsqueeze(1).to_broadcast([P, 8, P]),
                                        pair(n % 2).rearrange("p a (c i) -> p (a c) i", i=P)
                                        ).then_inc(s["level_used"], 1)

                dve.wait_ge(s["consts_pool"], 2)
                for n in range(7):
                    times(n)
                    keep(n)
                    if n in (2, 4, 6):
                        more_ada()
                keep(7)
                more_ada()
                last_b = b.rearrange("p (c t) -> p c t", t=P)[:, :, P - 1:P].to_broadcast([P, 8, P])
                dve.tensor_tensor(Dbuf[1].rearrange("p (c t) -> p c t", t=P), last_b,
                                  b.rearrange("p (c t) -> p c t", t=P), ALU.subtract).then_inc(s["kh_diff"], 1)
                dve.wait_ge(s["qd_exp"], hp + 1)
                dve.tensor_tensor(Dbuf[0].rearrange("p (h t) -> p h t", h=2), Dbuf[0].rearrange("p (h t) -> p h t", h=2),
                                  q[:, hs, 0:T], ALU.mult).then_inc(s["qd_ready"], 1)
                dve.wait_ge(s["kh_exp"], hp + 1)
                dve.tensor_tensor(Dbuf[1].rearrange("p (h t) -> p h t", h=2), Dbuf[1].rearrange("p (h t) -> p h t", h=2),
                                  kk[:, :, 0:T], ALU.mult).then_inc(s["kh_ready"], 1)
                dve.wait_ge(s["gvec_in"], 32 + 16 * hp)
                if hp == 0:
                    dve.wait_ge(s["ada_saved"], 6)
                    dve.tensor_tensor(mm[0:N1, 0, :], mm[0:N1, 0, :], gains[0][0:N1, :], ALU.mult).then_inc(s["modrow_ready"], 1)
                else:
                    dve.wait_ge(s["ada_saved"], 12)
                    chain(dve.tensor_scalar(mm[0:N1, 2, :], mm[0:N1, 2, :], 1.0, None, ALU.add))
                    for n, g in ((2, 1), (3, 2)):
                        dve.tensor_tensor(mm[0:N1, n, :], mm[0:N1, n, :], gains[g][0:N1, :], ALU.mult
                                          ).then_inc(s["modrow_ready"], 1)
                dve.wait_ge(s["upd_out"], hp + 1)
                dve.wait_ge(s["d_last"], hp + 1)
                if hp == 1:
                    dve.wait_ge(s["hstate_out"], 16)
                for c in range(PT):
                    for h in range(2):
                        upd = ps[:, h, c * P:(c + 1) * P]
                        if c == 0:
                            dve.tensor_copy(Sb[:, h, 0, :], upd).then_inc(s["s_ready"], 1)
                        else:
                            dve.wait_ge(s["s_ready"], 8 * hp + 2 * c - 1 + h)
                            dve.scalar_tensor_tensor(Sb[:, h, c, :], Sb[:, h, c - 1, :], dl[:, 4 * h + c:4 * h + c + 1], upd,
                                                     ALU.mult, ALU.add).then_inc(s["s_ready"], 1)
                dve.wait_ge(s["o_sq"], hp + 1)
                oT = actT[:, 4 + 2 * hp:6 + 2 * hp, 0:T]
                chain(dve.scalar_tensor_tensor(oT, pair(1), vecT[:, 12:13], gate[:, hs, 0:T], ALU.mult, ALU.mult))
                dve.wait_ge(s["o_r"], hp + 1)
                dve.tensor_tensor(oT, oT, khT.rearrange("p (h t) -> p h t", h=2), ALU.mult).then_inc(s["o_done"], 1)
            dve.memset(ybuf[:, 0, :], 0.0).then_inc(s["zeros_ready"], 1)
            dve.wait_ge(s["zero_rows"], 16)

            def rows_of(j):
                return [modb[:, n, :] if j < PT else mm[0:ROWS[j], n, :] for n in range(4)]

            def residual(j):
                R = ROWS[j]
                dve.wait_ge(s["mix_sq"], j + 1)
                dve.tensor_scalar(ss[0:R, j:j + 1], ss[0:R, j:j + 1], 1.0 / D, EPS, ALU.mult, ALU.add
                                  ).then_inc(s["mix_sqrt"], 1)
                dve.wait_ge(s["mix_rstd"], j + 1)
                chain(dve.reciprocal(rstd[0:R, j:j + 1], rstd[0:R, j:j + 1]))
                if j == 0:
                    dve.wait_ge(s["modb_ready"], 1)
                mixed = ybuf[0:R, 0, :]
                chain(dve.scalar_tensor_tensor(mixed.rearrange("p (a n) -> p a n", a=2), mix_ps(j)[0:R],
                                               rstd[0:R, j:j + 1], rows_of(j)[0].rearrange("p (a n) -> p a n", a=2),
                                               ALU.mult, ALU.mult))
                dve.tensor_tensor(xrows(j), xrows(j), mixed, ALU.add).then_inc(s["x1_ready"], 1)

            def normed2(j):
                R = ROWS[j]
                dve.wait_ge(s["x1_sq"], j + 1)
                dve.tensor_scalar(ss[0:R, j:j + 1], ss[0:R, j:j + 1], 1.0 / D, EPS, ALU.mult, ALU.add
                                  ).then_inc(s["mix_sqrt"], 1)
                dve.wait_ge(s["x1_rstd"], j + 1)
                chain(dve.reciprocal(rstd[0:R, j:j + 1], rstd[0:R, j:j + 1]))
                if j == 0:
                    dve.wait_ge(s["modb_ready"], 3)
                if j >= 4:
                    dve.wait_ge(s["h2_stored"], 16 * (j - 3))
                    dve.wait_ge(s["h2_turned"], j - 3)
                h2 = h2buf[0:R, j % 4, :]
                chain(dve.scalar_tensor_tensor(h2, xrows(j), rstd[0:R, j:j + 1], rows_of(j)[2], ALU.mult, ALU.mult))
                dve.tensor_tensor(h2, h2, rows_of(j)[1], ALU.add).then_inc(s["h2_ready"], 1)

            def h2T_half(j):
                dve.wait_ge(s["h2_turned"], j + 1)
                dve.tensor_copy(actT[:, 4:8, j * P:j * P + ROWS[j]],
                                ps[:, 6, :].rearrange("p (k n) -> p k n", k=4)[:, :, 0:ROWS[j]]).then_inc(s["h2T_d"], 1)

            for j in range(TT):
                residual(j)
                normed2(j)
                if 1 <= j < 4:
                    h2T_half(j - 1)
            h2T_half(3)
            h2T_half(4)

            def pick(e, posm_at, offset=None):
                for j in range(TT):
                    if offset is None:
                        last = dve.tensor_scalar(onehot[:, j, :], iota[:, :], posm_at(j), None, ALU.is_equal)
                    else:
                        last = dve.tensor_scalar(onehot[:, j, :], iota[:, :], offset, posm_at(j), ALU.add, ALU.is_equal)
                last.then_inc(s["onehot_ready"], 1)

            def index(e, r4):
                dve.wait_ge(s["disp_out"], e + 1)
                sums = slot_sums[:, r4, :]
                chain(dve.tensor_reduce(sums, ps[:, 7, 0:6].rearrange("p (a n) -> p a n", a=2), AX.X, ALU.add))
                chain(dve.tensor_scalar(idx_f[:, 0:1], sums[:, 0:1], 0.0, None, ALU.is_equal))
                chain(dve.scalar_tensor_tensor(idx_f[:, 1:2], idx_f[:, 0:1], trash1, sums[:, 0:1], ALU.mult, ALU.add))
                dve.tensor_scalar(gidx[:, r4:r4 + 1], idx_f[:, 1:2], -1.0, None, ALU.add).then_inc(s["idx_ready"], 1)

            def posm_static(e):
                return lambda j: posm[:, e, j:j + 1]

            def posm_dyn(e):
                return lambda j: posm[:, bass.ds(e, 1), j:j + 1].rearrange("p e n -> p (e n)")

            def glu(n, par, weight, R=P):
                dve.wait_ge(s["silu_done"], n + 1)
                dve.scalar_tensor_tensor(hh[0:R, par, :], sg[0:R, par, :], weight, ps[0:R, 4 + par, FE:2 * FE],
                                         ALU.mult, ALU.mult).then_inc(s["glu_done"], 1)

            def xT_half(e, par):
                dve.wait_ge(s["x_turned2"], e + 1)
                dve.tensor_copy(xT[:, par, 4:8, :], ps[:, 1, :].rearrange("p (k n) -> p k n", k=4)
                                ).then_inc(s["xT_d"], 1)

            def y_half(n, par, R=P):
                dve.wait_ge(s["down_done"], n + 1)
                dve.tensor_copy(ybuf[0:R, par, 512:1024], ps[0:R, 3, :]).then_inc(s["y_d"], 1)

            dve.wait_ge(s["h2_ready"], TT)
            chain(dve.memset(scores, 1.0))
            dve.memset(tabrows, 0.0).then_inc(s["zeros_ready"], 1)
            dve.wait_ge(s["score_ready"], 1)
            chain(dve.tensor_tensor(sel, scores, rbias[:, :].unsqueeze(1).to_broadcast([P, TT, NE]), ALU.add))
            for j in range(TT):
                for g in range(8):
                    last = dve.max(sorted8[:, j, g, :], sel[:, j, 8 * g:8 * g + 8])
            chain(last)
            chain(dve.tensor_tensor(gsc, sorted8[:, :, :, 0], sorted8[:, :, :, 1], ALU.add))
            other = gsc.unsqueeze(2).to_broadcast([P, TT, 8, 8])
            this = gsc.unsqueeze(3).to_broadcast([P, TT, 8, 8])
            dve.tensor_tensor(cmp1.rearrange("p j (a b) -> p j a b", a=8), other, this, ALU.is_gt)
            chain(dve.tensor_tensor(cmp2.rearrange("p j (a b) -> p j a b", a=8), other, this, ALU.is_equal))
            chain(dve.tensor_tensor(cmp2, cmp2, lower8.unsqueeze(1).to_broadcast([P, TT, NE]), ALU.mult))
            chain(dve.tensor_tensor(cmp1, cmp1, cmp2, ALU.add))
            chain(dve.tensor_reduce(grank, cmp1.rearrange("p j (a b) -> p j a b", a=8), AX.X, ALU.add))
            chain(dve.tensor_scalar(gmask, grank, 3.5, None, ALU.is_lt))
            chain(dve.tensor_scalar(gpen, gmask, 1e30, -1e30, ALU.mult, ALU.add))
            g4 = sel.rearrange("p j (a b) -> p j a b", a=8)
            chain(dve.tensor_tensor(g4, g4, gmask.unsqueeze(3).to_broadcast([P, TT, 8, 8]), ALU.mult))
            chain(dve.tensor_tensor(g4, g4, gpen.unsqueeze(3).to_broadcast([P, TT, 8, 8]), ALU.add))
            for j in range(TT):
                last = dve.max(top8[:, j, :], sel[:, j, :])
            chain(last)
            v8 = top8[:, :, 7:8].to_broadcast([P, TT, NE])
            dve.tensor_tensor(cmp1, sel, v8, ALU.is_gt)
            chain(dve.tensor_tensor(cmp2, sel, v8, ALU.is_equal))
            for j in range(TT):
                last = dve.tensor_tensor_scan(route_mask[:, j, :], ones[:, 0:NE], cmp2[:, j, :], 0.0, ALU.mult, ALU.add)
            chain(last)
            chain(dve.tensor_reduce(grank[:, :, 0], cmp1, AX.X, ALU.add))
            chain(dve.tensor_scalar(grank[:, :, 0], grank[:, :, 0], -1.0, TOP_K + 0.5, ALU.mult, ALU.add))
            chain(dve.tensor_tensor(route_mask, route_mask, grank[:, :, 0:1].to_broadcast([P, TT, NE]), ALU.is_lt))
            chain(dve.tensor_tensor(route_mask, route_mask, cmp2, ALU.mult))
            chain(dve.tensor_tensor(route_mask, route_mask, cmp1, ALU.add))
            chain(dve.tensor_tensor(scores, scores, route_mask, ALU.mult))
            chain(dve.tensor_scalar(route_mask[:, PT, :], route_mask[:, PT, :], valid, None, ALU.mult))
            dve.sem_inc(s["route_m"], 1)
            glu(0, 0, 1.0)
            chain(dve.tensor_reduce(grank[:, :, 1], scores, AX.X, ALU.add))
            chain(dve.reciprocal(grank[:, :, 1], grank[:, :, 1]))
            chain(dve.tensor_scalar(grank[:, :, 1], grank[:, :, 1], ROUTED_SCALE, None, ALU.mult))
            chain(dve.tensor_tensor(scores, scores, grank[:, :, 1:2].to_broadcast([P, TT, NE]), ALU.mult))
            for n in range(3):
                part = tokw[:, :, :, 3 + n].rearrange("p e j -> p j e")
                chain(dve.tensor_copy(part, scores))
                if n < 2:
                    chain(dve.tensor_tensor(scores, scores, part, ALU.subtract))
            dve.wait_ge(s["pos_out"], 1)
            pos = ps[:, 7, 0:TT * NE].rearrange("p (j e) -> p j e", j=TT)
            chain(dve.scalar_tensor_tensor(sel, pos, 1.0, route_mask, ALU.add, ALU.mult))
            chain(dve.tensor_scalar(posm[:, :, :].rearrange("p e j -> p j e"), sel, -1.0, None, ALU.add))
            cnt = ps[0:NE, 7, 320:321]
            for j in range(4):
                last = dve.tensor_scalar(tabi[:, j:j + 1], cnt, float(P * (j + 1)), None, ALU.is_gt)
            chain(last)
            chain(dve.tensor_reduce(tabn, tabi, AX.X, ALU.add))
            dve.sem_inc(s["cnt_out"], 1)
            pick(0, posm_static(0))
            glu(1, 1, 1.0)
            y_half(0, 0)
            glu(2, 0, 1.0)
            y_half(1, 1)
            dve.wait_ge(s["table_in"], 1)
            chain(dve.tensor_scalar(tabd[:, 0:1], ps[0:NE, 0, 328:329], 0.0, None, ALU.add))
            chain(dve.tensor_copy(tabd[:, 1:2], trash1[0:NE, :]))
            chain(dve.tensor_scalar(tabd[:, 1:2], tabd[:, 1:2], -float(TRASH + 1), None, ALU.add))
            for j in range(4):
                chain(dve.tensor_scalar(tab1, iota[0:NE, 0:TAB], tabd[:, 0:1], tabi[:, j:j + 1], ALU.is_equal, ALU.mult))
                chain(dve.scalar_tensor_tensor(tabrows[0:NE, 0:TAB], tab1, tabd[:, 1:2], tabrows[0:NE, 0:TAB], ALU.mult, ALU.add))
                chain(dve.scalar_tensor_tensor(tabrows[0:NE, TAB:2 * TAB], tab1, NEVER - P * (j + 1), tabrows[0:NE, TAB:2 * TAB],
                                               ALU.mult, ALU.add))
                chain(dve.tensor_scalar(tabd[:, 0:1], tabd[:, 0:1], 1.0, None, ALU.add))
            dve.sem_inc(s["cnt_out"], 1)
            index(0, 0)
            pick(1, posm_static(1))
            glu(3, 1, 1.0)
            dve.wait_ge(s["ff_init0"], 16)
            y_half(2, 0)
            dve.wait_ge(s["table_out"], 1)
            dve.tensor_copy(table_i[:, 0:TAB], ps[:, 0, 352:352 + TAB])
            dve.tensor_scalar(tabq, ps[:, 0, 352 + TAB:352 + 2 * TAB], -1.0, NEVER, ALU.mult, ALU.add)
            chain(dve.tensor_scalar(turns8, iota[:, 0:8], 4.0, None, ALU.mult))
            chain(dve.tensor_scalar(turns8, turns8, ps[:, 0, 336:337], None, ALU.is_lt))
            chain(dve.tensor_reduce(qneg, turns8, AX.X, ALU.add))
            chain(dve.tensor_scalar(table_i[:, TAB:TAB + 1], qneg, 1.0, None, ALU.max))
            dve.sem_inc(s["table_ready"], 1)
            index(1, 1)
            pick(2, posm_static(2))
            glu(4, 0, 1.0, NB)
            dve.wait_ge(s["ff_init1"], 16)
            y_half(3, 1)
            xT_half(0, 0)
            index(2, 2)
            pick(3, posm_static(3))

            LINKS = 3

            def extra_block(n):
                at = slice(n, n + 1) if isinstance(n, int) else bass.ds(n, 1)
                e = dve.value_load(table_i[0:1, at], min_val=0, max_val=NE - 1)
                pick(e, posm_dyn(e), offset=tabq[:, at])

            def step(e, r, nxt, first=False):
                n = e + TT
                xT_half(e + 1, (r + 1) % 2)
                glu(n, (r + 1) % 2, slot_sums[:, r, 1:2])
                dve.tensor_copy(sidx[:, r:r + 1], gidx[:, r:r + 1])
                index(e + 3, (r + 3) % 4)
                nxt()
                if not isinstance(e, int) or e > 2:
                    dve.wait_ge(s["scattered"], (e - 2) * 16)
                y_half(n - 1, r % 2, NB if first else P)

            def expert(e):
                return lambda: pick(e, posm_static(e) if isinstance(e, int) else posm_dyn(e))

            dve.wait_ge(s["ff_init0"], 16 * 2)
            step(0, 0, expert(4), first=True)
            dve.wait_ge(s["ff_init1"], 16 * 2)
            step(1, 1, expert(5))
            dve.wait_ge(s["ff_init0"], 16 * 3)
            step(2, 2, expert(6))
            step(3, 3, expert(7))
            before = chain.count
            with dve.Fori(1, NE // 4 - 1) as i:
                for r in range(4):
                    chain.base, chain.count = (i - 1) * (4 * LINKS) + before, LINKS * r
                    step(i * 4 + r, r, expert(i * 4 + (r + 4)))
            chain.base, chain.count = 0, before + LINKS * (NE - 8)
            for r in range(4):
                step(NE - 4 + r, r, lambda: extra_block(r))
            before = chain.count
            turns = dve.value_load(table_i[0:1, TAB:TAB + 1], min_val=1, max_val=MAX_TURNS)
            with dve.Fori(0, turns) as i:
                for r in range(4):
                    chain.base, chain.count = i * (4 * LINKS) + before, LINKS * r
                    step(i * 4 + (NE + r), r, lambda: extra_block(i * 4 + (r + 4)))
            dve.wait_ge(s["scattered"], turns * 64 + 16 * (NE - 2))
            y_half(turns * 4 + (TT + NE - 1), 0)
            dve.wait_ge(s["xT_d"], turns * 4 + (NE + 1))
            dve.sem_inc(s["ff_ready"], 1)
            for j in range(TT):
                R = ROWS[j]
                g2 = modb[:, 3, :] if j < PT else mm[0:R, 3, :]
                dve.wait_ge(s["ff_sq"], j + 1)
                dve.tensor_scalar(ss[0:R, j:j + 1], ss[0:R, j:j + 1], 1.0 / D, EPS, ALU.mult, ALU.add
                                  ).then_inc(s["ff_sqrt"], 1)
                dve.wait_ge(s["ff_rstd"], j + 1)
                if j == 0:
                    chain.base, chain.count = turns * (4 * LINKS) + before, 0
                chain(dve.reciprocal(rstd[0:R, j:j + 1], rstd[0:R, j:j + 1]))
                out = fin[0:R, j, :]
                chain(dve.scalar_tensor_tensor(out, out, rstd[0:R, j:j + 1], g2, ALU.mult, ALU.mult))
                dve.tensor_tensor(out, out, xrows(j), ALU.add).then_inc(s["out_ready"], 1)


_INS = ["x_prompt", "x_sample", "c_prompt", "c_sample", "state_pool", "state_hgrn", "w_ada", "b_ada", "g_pre_mix",
        "g_post_mix", "w_in", "w_pool", "pool_scale", "lb_logits", "g_out_norm", "w_out", "g_pre_ffn", "g_post_ffn",
        "w_router", "router_bias", "w_exp_gate", "w_exp_up", "w_exp_down", "w_sh_gate", "w_sh_up", "w_sh_down"]
_OUTS = [(1, 512, 1024), (8, 1, 1024), (1, 1, 15, 512), (1, 1, 4, 128, 128), (1, 8, 15, 512), (1, 8, 4, 128, 128)]


def kernel(**inputs):
    import numpy as np
    import concourse.bacc as bacc
    from concourse.bass_utils import run_bass_kernel_spmd

    nc = bacc.Bacc("TRN2", target_bir_lowering=False, num_devices=1)
    arrays, args = {}, []
    for name in _INS:
        a = np.ascontiguousarray(inputs[name])
        arrays[f"in_{name}"] = a
        args.append(nc.dram_tensor(f"in_{name}", a.shape, mybir.dt.from_np(a.dtype), kind="ExternalInput").ap())
    for n, shape in enumerate(_OUTS):
        args.append(nc.dram_tensor(f"out_{n}", shape, F32, kind="ExternalOutput").ap())
    args.append(nc.dram_tensor("h2_rows", (520, 1024), F32).ap())
    args.append(nc.dram_tensor("ff_rows", (520 + 128, 1024), F32).ap())
    build(nc, *args)
    r = run_bass_kernel_spmd(nc, [arrays], core_ids=[0])
    return tuple(r.results[0][f"out_{n}"] for n in range(len(_OUTS)))
```

```python
from contextlib import ExitStack

import concourse.bass as bass
from concourse import mybir

F32 = mybir.dt.float32
I32 = mybir.dt.int32
I8 = mybir.dt.int8
BF16 = mybir.dt.bfloat16
ALU = mybir.AluOpType
ACT = mybir.ActivationFunctionType
AX = mybir.AxisListType

P = 128
EPS = 1e-6
WINDOWS = (2, 4, 8, 16)
HIST = 15
TOP_K = 8
ROUTED_SCALE = 2.5
NEVER = 1024.0
LEVELS = (64, 32, 16, 8, 4, 2, 1)


class Chain:

    def __init__(self, engine, sem):
        self.engine, self.sem, self.count, self.base = engine, sem, 0, 0

    def __call__(self, instruction):
        instruction.then_inc(self.sem, 1)
        self.count += 1
        self.engine.wait_ge(self.sem, self.base + self.count)


def build(nc, x_prompt, x_sample, c_prompt, c_sample, state_pool, state_hgrn, w_ada, b_ada, g_pre_mix, g_post_mix,
          w_in, w_pool, pool_scale, lb_logits, g_out_norm, w_out, g_pre_ffn, g_post_ffn, w_router, router_bias,
          w_exp_gate, w_exp_up, w_exp_down, w_sh_gate, w_sh_up, w_sh_down,
          y_prompt, y_sample, pool_prompt, hgrn_prompt, pool_sample, hgrn_sample, h2_rows, ff_rows, mod_rows):
    D = x_prompt.shape[2]
    T = x_prompt.shape[1]
    NB = x_sample.shape[0]
    NT = T + NB
    KC = D // P
    PT = T // P
    TT = PT + 1
    NE = w_exp_gate.shape[1]
    NH = state_hgrn.shape[2]
    FE = w_exp_gate.shape[3]
    HALF = NT // 2
    N1 = NB + 1
    TRASH = NT
    ROWS = [P] * PT + [NB]
    MAX_EXTRA = NT * TOP_K // P
    MAX_TURNS = MAX_EXTRA // 4
    TAB = MAX_EXTRA + 8
    assert (D, T, NB, NE, NH, FE) == (1024, 512, 8, 64, 4, 256)

    ctx = ExitStack()
    with ctx:
        def sb(name, shape, dt=F32):
            return ctx.enter_context(nc.sbuf_tensor(name, shape, dt))

        def sem(name):
            return ctx.enter_context(nc.semaphore(name))

        ringA = sb("ringA", [P, 4, 4096])
        ringB = sb("ringB", [P, 4, 2048])
        late = sb("late", [P, 7680])
        bc = sb("bc", [P, 4096])
        mm = sb("mm", [P, 4, D])
        xt = sb("xt", [P, TT, D])
        actT = sb("actT", [P, KC, NT])
        ident = sb("ident", [P, P])
        ones = sb("ones", [P, P])
        tri = sb("tri", [P, P])
        iota = sb("iota", [P, P])
        masks = sb("masks", [P, 8, P], I8)
        tokw = sb("tokw", [P, NE, TT, 6], BF16)
        posm = sb("posm", [P, NE, TT])
        onehot = sb("onehot", [P, TT, P], BF16)
        wrt = sb("wrt", [P, KC, NE])
        rbias = sb("rbias", [P, NE])
        small = sb("small", [P, 448])
        gidx = sb("gidx", [P, 4], I32)
        sidx = sb("sidx", [P, 4], I32)
        table_i = sb("table_i", [P, TAB + 1], I32)

        iB = ringB[:, :, :].rearrange("p a b -> p (a b)")
        q = iB[:, 0:NH * NT].rearrange("p (h t) -> p h t", h=NH)
        f = iB[:, 2080:4160].rearrange("p (h t) -> p h t", h=NH)
        UW = HIST + NT
        u = iB[:, 4160:4160 + 4 * UW].rearrange("p (g t) -> p g t", g=4)
        b = iB[:, 6300:7324]
        wpool = iB[:, 7324:7836].rearrange("p (g d) -> p g d", g=4)
        m1 = iB[:, 0:2048]
        gate = late[:, 0:2080].rearrange("p (h t) -> p h t", h=NH)
        v = late[:, 2080:4640].rearrange("p (j c) -> p j c", j=TT)
        diffs = late[:, 4640:6720].rearrange("p (g t) -> p g t", g=4)
        kk = late[:, 4640:5680].rearrange("p (h t) -> p h t", h=2)
        att = late[:, 5680:6704].rearrange("p (c i) -> p c i", i=P)
        tmpS = late[:, 6720:7680]
        Dbuf = [bc[:, 0:1024], bc[:, 1024:2048], bc[:, 2048:3072]]
        khT = bc[:, 2048:3072]
        Sb = bc[:, 3072:4096].rearrange("p (h c v) -> p h c v", h=2, c=4)
        xn = [bc[:, 0:1024], bc[:, 1024:2048]]
        junk = bc[:, 2048:3072]
        hraw = bc[:, 3072:3584]
        histT = bc[:, 3584:4064].rearrange("p (g b r) -> p g b r", g=4, b=NB)
        cs = late[:, 0:1024]
        spent = actT[:, 0:4, :].rearrange("p k n -> p (k n)")
        gains = [spent[:, 0:1024], spent[:, 1024:2048], spent[:, 0:1024]]
        h2buf = late[:, 0:4096].rearrange("p (a n) -> p a n", a=4)
        modb = bc[:, :].rearrange("p (a n) -> p a n", a=4)
        xg = late[:, 0:2048].rearrange("p (a n) -> p a n", a=2)
        xT = late[:, 2048:4096].rearrange("p (a k n) -> p a k n", a=2, k=KC)
        ybuf = late[:, 4096:6144].rearrange("p (a n) -> p a n", a=2)
        sg = late[:, 6144:6656].rearrange("p (a n) -> p a n", a=2)
        hh = late[:, 6656:7168].rearrange("p (a n) -> p a n", a=2)
        hhT = late[:, 7168:7680].rearrange("p (a k n) -> p a k n", a=2, k=2)

        at = [0]

        def cut(n):
            at[0] += n
            return small[:, at[0] - n:at[0]]

        ss = cut(TT)
        rstd = cut(TT)
        cT = cut(KC * N1).rearrange("p (k r) -> p k r", k=KC)
        a1T = cut(KC * N1).rearrange("p (k r) -> p k r", k=KC)
        b1T = cut(KC * N1).rearrange("p (k r) -> p k r", k=KC)
        gpre = cut(KC)
        vecT = cut(13)
        lb = cut(NH)
        oml = cut(NH)
        lbt = cut(3 * NH)
        eps_c = cut(1)
        icnt = cut(16)
        dl = cut(8)
        kS = cut(NH * NB).rearrange("p (h b) -> p h b", h=NH)
        trash1 = cut(1)
        valid = cut(1)
        slot_sums = cut(8).rearrange("p (r a) -> p r a", a=2)
        idx_f = cut(2)
        qneg = cut(1)
        lower8 = cut(64)
        u_rows = tmpS[:, 448:960]
        fin = late[:, 0:5 * D].rearrange("p (j n) -> p j n", j=TT)
        fin_junk = late[:, 5 * D:6 * D]
        rt = [0]

        def routed(n):
            rt[0] += n
            return bc[:, rt[0] - n:rt[0]]

        def per_expert():
            return routed(TT * NE).rearrange("p (j e) -> p j e", j=TT)

        scores, sel, cmp1, cmp2, route_mask = (per_expert() for _ in range(5))
        sorted8 = routed(TT * 64).rearrange("p (j g r) -> p j g r", j=TT, g=8)
        gsc, grank, gmask, gpen, top8 = (routed(TT * 8).rearrange("p (j g) -> p j g", j=TT) for _ in range(5))
        tabrows = routed(2 * TAB)
        tabq = routed(TAB)
        tabi = routed(4)[0:NE]
        tabn = routed(1)[0:NE]
        tabd = routed(2)[0:NE]
        tab1 = routed(TAB)[0:NE]
        turns8 = routed(8)
        assert rt[0] <= 3072

        ps = ctx.enter_context(nc.psum_tensor("ps", [P, 8, 512], F32))

        names = """in_small in_c in_x ringA_in0 ringA_in1 ringA_in2 ringA_in3 ringB_in0 ringB_in1 ringB_in2 ringB_in3
        consts_pool consts_dve pe_cT c_silu cT_ready ms_ready sq_ready rms_sqrt rstd_ready xn_ready x_turned x_evac_a x_evac_d
        ada_out ada_saved m1_turned m1T_ready mod_a mod_d lb_diff lb_exp
        proj_out proj_a f_ready
        hist_turned hist_ready u_ready rows_turned rows_saved pool_d pool_y pool_saved rows_out
        ln_done kk_ready b_ready diff_ready exp_done x_level level_out level_used qd_exp qd_ready kh_diff kh_exp kh_ready
        kh_turned khT_ready upd_out s_ready o_out o_sq o_ms o_r o_done hstate_out d_last
        s0_in s0_dec vb_out s_new so_out s_out so_sq so_ms so_r so_done
        gvec_in modrow_ready mix_out mix_sq mix_sqrt mix_rstd x1_ready x1_sq x1_rstd h2_ready h2_stored
        h2_turned h2T_a h2T_d logit_out score_ready route_m pos_out cnt_out table_in table_out table_ready in_bada adds_done scaled mod_stored modb_in0 modb_in1
        up_done silu_done glu_done hh_turned hhT_ready down_done y_a y_d ff_init0 ff_init1 scattered scores_set mix_saved
        onehot_ready disp_out idx_ready gathered0 gathered1 x_turned2 xT_a xT_d
        ff_ready ff_in0 ff_in1 ff_in2 ff_in3 ff_in4 ff_sq ff_sqrt ff_rstd out_ready out_sent dve_chain act_chain pool_chain pool_passed""".split()
        s = {n: sem(n) for n in names}

        ypool_ps = ps[:, 6:8, 0:HALF]
        so_ps = ps[:, 6, 0:NH * NB]
        sms_ps = ps[:, 7, 0:NH * NB]
        logit_ps = ps[:, 7, 0:TT * NE].rearrange("p (j e) -> p j e", j=TT)

        def pair(i):
            return ps[:, 2 * i:2 * i + 2, :]

        def mix_ps(j):
            return pair((2, 0, 1, 0, 1)[j])

        def quarter(rows, bank, g):
            return ps[32 * g:32 * g + rows, bank, g * P:(g + 1) * P]

        def ada_ps(n, g):
            return quarter(N1, 4 + n % 2, g)

        def down_quarter(g):
            return ps[32 * g:32 * g + NB, 2 + g // 2, 256 * (g % 2):256 * (g % 2 + 1)]

        mix_sample = late[0:NB, 6144:7168].rearrange("p (a n) -> p a n", a=2)

        def mix_in(j):
            return mix_sample if j == PT else mix_ps(j)

        def ringA_k(slot):
            return ringA[:, slot, :].rearrange("p (k n) -> p k n", k=KC)

        def ringA_gu(slot):
            return ringA[:, slot, :].rearrange("p (a k n) -> p a k n", a=2, k=KC)

        def ringB_k(slot):
            return ringB[:, slot, :].rearrange("p (k n) -> p k n", k=2)

        pieces = [("ada", 512 * i) for i in range(4)]
        pieces += [("in", 0), ("in", 1024), ("in", 512), ("in", 1536), ("in", 2048)]
        pieces += [("ada", 2048 + 512 * i) for i in range(8)]
        pieces += [("out", 0), ("out", 512), ("shared", 0)]
        NPIECE = len(pieces)
        A_OUT, A_SHARED = 17, 19

        def used(p):
            if p < 4:
                return s["ada_out"], p + 1
            if p < 9:
                return s["proj_out"], (4, 8, 12, 12 + TT, 16 + TT)[p - 4]
            if p < A_OUT:
                return s["ada_out"], p - 4
            return (s["up_done"], TT) if p == A_SHARED else (s["mix_out"], TT)

        def piece_source(kind, col, half):
            if kind == "out":
                return w_out[0].rearrange("(k p) n -> p k n", p=P)[:, 4 * half:4 * half + 4, col:col + 512]
            w = {"ada": w_ada, "in": w_in}[kind]
            return w[0].rearrange("(p k) n -> p k n", k=KC)[:, 4 * half:4 * half + 4, col:col + 512]

        def arrived_a(eng, p):
            eng.wait_ge(s[f"ringA_in{p % 4}"], 32 * (p // 4 + 1))

        def state_slot(n):
            return mm[:, n % 4, 0:512].rearrange("p (h v) -> p h v", h=NH)

        def xrows(j):
            return xt[0:ROWS[j], j, :]

        FILL = ((16, 0, 0, 0, 0, 0, 0, 16), (8, 2, 2, 2, 2, 0, 0, 0))

        SHARED_BANK = {2: 1}
        FILLED = {(0, 2): (4,), (0, 3): (5,), (1, 0): (8, 9), (1, 2): (10,), (1, 6): (11,)}

        block = ctx.enter_context(nc.Block())

        @block.sync
        def _(sp):
            sp.dma_start(cs[0:NB, :], c_sample).then_inc(s["in_c"], 16)
            sp.dma_start(cs[NB:N1, :], c_prompt).then_inc(s["in_c"], 16)

            def load_piece(p):
                kind, col = pieces[p]
                if p >= 4:
                    sp.wait_ge(*used(p - 4))
                for half in range(2):
                    if kind == "shared":
                        src = (w_sh_gate, w_sh_up)[half][0].rearrange("(p k) n -> p k n", k=KC)
                        dst = ringA_gu(p % 4)[:, half, :, :]
                    else:
                        src = piece_source(kind, col, half)
                        dst = ringA_k(p % 4)[:, 4 * half:4 * half + 4, :]
                    sp.dma_start(dst, src).then_inc(s[f"ringA_in{p % 4}"], 16)

            for p in range(NPIECE):
                if p == 1:
                    sp.dma_start(m1[0:N1, :], b_ada[0, 0:2048].partition_broadcast(N1)).then_inc(s["in_x"], 16)
                    sp.dma_start(xt[:, 0:PT, :], x_prompt[0].rearrange("(j p) d -> p j d", p=P)).then_inc(s["in_x"], 16)
                    sp.dma_start(xt[0:NB, PT, :], x_sample[:, 0, :]).then_inc(s["in_x"], 16)
                load_piece(p)

            sp.wait_ge(s["ada_saved"], 12)
            sp.wait_ge(s["modrow_ready"], 3)
            sp.dma_start(mod_rows.rearrange("(r n) -> r n", r=1), mm[NB:N1, :, :].rearrange("r a n -> r (a n)")
                         ).then_inc(s["mod_stored"], 16)
            sp.wait_ge(s["mod_stored"], 16)
            sp.wait_ge(s["o_done"], 2)
            sp.wait_ge(s["hstate_out"], 32)
            for part, (lo, hi) in enumerate(((0, D), (D, 4 * D))):
                sp.dma_start(bc[:, lo:hi], mod_rows[lo:hi].partition_broadcast(P)).then_inc(s[f"modb_in{part}"], 16)

            sp.wait_ge(s["o_done"], 2)
            sp.dma_start(ringB_k(0), w_sh_down[0].rearrange("(p k) n -> p k n", k=2)).then_inc(s["ringB_in0"], 16)

            def load_a(e, slot, e_dram):
                for half, w in enumerate((w_exp_gate, w_exp_up)):
                    sp.dma_start(ringA_gu(slot)[:, half, :, :],
                                 w[0, e_dram].rearrange("e (p k) n -> p (e k) n", k=KC)
                                 if not isinstance(e_dram, int) else w[0, e_dram].rearrange("(p k) n -> p k n", k=KC)
                                 ).then_inc(s[f"ringA_in{slot}"], 16)

            def load_b(e, slot, e_dram):
                src = w_exp_down[0, e_dram]
                src = (src.rearrange("(p k) n -> p k n", k=2) if isinstance(e_dram, int)
                       else src.rearrange("e (p k) n -> p (e k) n", k=2))
                sp.dma_start(ringB_k(slot), src).then_inc(s[f"ringB_in{slot}"], 16)

            for e in range(4):
                sp.wait_ge(*used(NPIECE - 4 + e))
                load_a(e, e, e)
                if e in (1, 2):
                    sp.wait_ge(s["mix_out"], TT)
                if e == 3:
                    sp.wait_ge(s["down_done"], TT)
                load_b(e, (1 + e) % 4, e)
            with sp.Fori(1, NE // 4) as i:
                for r in range(4):
                    e = i * 4 + r
                    sp.wait_ge(s["up_done"], e + 2)
                    load_a(e, r, bass.ds(e, 1))
                    sp.wait_ge(s["down_done"], e + 2)
                    load_b(e, (1 + r) % 4, bass.ds(e, 1))
            sp.wait_ge(s["table_ready"], 1)
            turns = sp.value_load(table_i[0:1, TAB:TAB + 1], min_val=1, max_val=MAX_TURNS)
            with sp.Fori(0, turns) as i:
                for r in range(4):
                    e = sp.value_load(table_i[0:1, bass.ds(i * 4 + r, 1)], min_val=0, max_val=NE - 1)
                    sp.wait_ge(s["up_done"], i * 4 + (NE + r + 2))
                    load_a(e, r, bass.ds(e, 1))
                    sp.wait_ge(s["down_done"], i * 4 + (NE + r + 2))
                    load_b(e, (1 + r) % 4, bass.ds(e, 1))

            sp.wait_ge(s["adds_done"], 1)
            sp.wait_ge(s["ff_ready"], 1)
            for j in range(TT):
                sp.dma_start(fin[0:ROWS[j], j, :], ff_rows[j * P:j * P + ROWS[j], :]).then_inc(s[f"ff_in{j}"], 16)
            for j in range(TT):
                sp.wait_ge(s["out_ready"], j + 1)
                dst = y_prompt[0, j * P:(j + 1) * P, :] if j < PT else y_sample[:, 0, :]
                sp.dma_start(dst, fin[0:ROWS[j], j, :]).then_inc(s["out_sent"], 16)
            sp.wait_ge(s["out_sent"], 16 * TT)
            sp.wait_ge(s["rows_out"], 48)
            sp.wait_ge(s["hstate_out"], 32)
            sp.wait_ge(s["s_out"], 16 * NB)

        @block.gpsimd
        def _(pool):
            chain = Chain(pool, s["pool_chain"])
            chain(pool.memset(ident[:, :], 0.0))
            pool.affine_select(out=ident[:, :], in_=ident[:, :], compare_op=ALU.not_equal, fill=1.0, base=0,
                               pattern=[[-1, P]], channel_multiplier=1).then_inc(s["consts_pool"], 1)
            def small_in(dst, src):
                pool.dma_start(dst, src).then_inc(s["in_small"], 16)
            small_in(tmpS[0:8, 0:P], lb_logits.rearrange("a (h p) -> (a h) p", p=P))
            small_in(tmpS[8:12, 0:P], pool_scale[0].rearrange("(h p) -> h p", p=P))
            small_in(tmpS[12:13, 0:P], g_out_norm)
            small_in(gpre, g_pre_mix[0].rearrange("(p k) -> p k", k=KC))
            small_in(rbias[:, :], router_bias[0, :].partition_broadcast(P))
            small_in(wrt[:, :, :], w_router[0].rearrange("(p k) e -> p k e", k=KC))
            small_in(wpool, w_pool[0].rearrange("g c d -> c g d"))
            small_in(hraw[0:NB * HIST, :], state_pool[0].rearrange("b r c -> (b r) c"))
            chain(pool.memset(tri[:, :], 0.0))
            chain(pool.affine_select(out=tri[:, :], in_=tri[:, :], compare_op=ALU.is_ge, fill=1.0, base=0,
                                     pattern=[[-1, P]], channel_multiplier=1))
            pool.iota(iota[:, :], pattern=[[1, P]], base=0, channel_multiplier=0,
                      allow_small_or_imprecise_dtypes=True)
            pool.iota(icnt, pattern=[[1, 16]], base=1, channel_multiplier=0, allow_small_or_imprecise_dtypes=True)
            pool.iota(trash1, pattern=[[0, 1]], base=TRASH + 1, channel_multiplier=1,
                      allow_small_or_imprecise_dtypes=True)
            pool.memset(tokw[:, :, :, 2], 0.0)
            pool.iota(tokw[:, :, :, 0], pattern=[[0, NE], [P, TT]], base=0, channel_multiplier=0,
                      allow_small_or_imprecise_dtypes=True)
            pool.iota(tokw[:, :, :, 1], pattern=[[0, NE], [0, TT]], base=1, channel_multiplier=1,
                      allow_small_or_imprecise_dtypes=True).then_inc(s["consts_pool"], 1)
            chain(pool.memset(lower8, 1.0))
            chain(pool.affine_select(out=lower8, in_=lower8, compare_op=ALU.is_gt, fill=0.0, base=0,
                                     pattern=[[1, 8], [-1, 8]], channel_multiplier=0))
            ones_u = masks[:, :, :]
            chain(pool.memset(ones_u, 0.0))
            m0 = masks[:, 0, :]
            chain(pool.affine_select(out=m0, in_=m0, compare_op=ALU.not_equal, fill=1.0, base=0,
                                     pattern=[[-1, P]], channel_multiplier=1))
            for n, half in enumerate(LEVELS):
                right = masks[:, n + 1, :].rearrange("p (b h r) -> p b h r", h=2, r=half)[:, :, 1, :]
                chain(pool.memset(right, 1.0))
                nb = P // (2 * half)
                chain(pool.affine_select(out=right, in_=right, compare_op=ALU.is_ge, fill=0.0, base=0,
                                         pattern=[[-2 * half, nb], [0, half]], channel_multiplier=1))
                last = pool.affine_select(out=right, in_=right, compare_op=ALU.is_ge, fill=0.0, base=half - 1,
                                          pattern=[[2 * half, nb], [0, half]], channel_multiplier=-1)
                if half > 1:
                    chain(last)
            last.then_inc(s["consts_pool"], 1)

            pool.wait_ge(s["u_ready"], 4)
            for g, w in enumerate(WINDOWS):
                src = u[:, g, 0:HIST + T]
                step = 1
                while step < w:
                    dst = (Dbuf[0] if src.offset != Dbuf[0].offset else Dbuf[1])[:, 0:HIST + T]
                    chain(pool.tensor_tensor(dst[:, 2 * step - 1:], src[:, 2 * step - 1:], src[:, step - 1:HIST + T - step], ALU.add))
                    src = dst
                    step *= 2
                diff = diffs[:, g, :]
                mean = src[:, HIST:]
                hs = tmpS[:, 0:NB]
                if g == 0:
                    pool.wait_ge(s["hist_ready"], 1)
                    pool.wait_ge(s["consts_dve"], 2)
                chain(pool.tensor_tensor(mean[:, 0:w - 1], mean[:, 0:w - 1], icnt[:, 0:w - 1], ALU.mult))
                chain(pool.tensor_scalar(mean[:, w - 1:], mean[:, w - 1:], 1.0 / w, None, ALU.mult))
                chain(pool.tensor_tensor(diff[:, 0:T], mean, u[:, g, HIST:HIST + T], ALU.subtract))
                hsum = tmpS[:, 256 + NB * g:256 + NB * g + NB]
                chain(pool.tensor_tensor(hs, hsum, u[:, g, HIST + T:UW], ALU.add))
                chain(pool.tensor_scalar(hs, hs, 1.0 / w, None, ALU.mult))
                pool.tensor_tensor(diff[:, T:NT], hs, u[:, g, HIST + T:UW], ALU.subtract).then_inc(s["pool_d"], 1)
            pool.dma_start(pool_sample[0, :, 0:HIST - 1, :], state_pool[0, :, 1:HIST, :]).then_inc(s["rows_out"], 16)
            def s0_load(n):
                pool.dma_start(state_slot(n),
                               state_hgrn[0, n].rearrange("h k v -> k h v")).then_inc(s["s0_in"], 16)
            pool.wait_ge(s["pool_d"], 4)
            for n in range(4):
                s0_load(n)
            pool.wait_ge(s["rows_saved"], 1)
            pool.dma_start(pool_prompt[0, 0, :, :], u_rows[0:HIST, :]).then_inc(s["rows_out"], 16)
            pool.dma_start(pool_sample[0, :, HIST - 1, :], u_rows[HIST:HIST + NB, :]).then_inc(s["rows_out"], 16)
            def level_diff(hp, n):
                half = LEVELS[n]
                if n >= 3:
                    pool.wait_ge(s["level_out"], 8 * hp + n - 1)
                b4 = b.rearrange("p (b r) -> p b r", r=2 * half)
                mid = b4[:, :, half - 1:half].to_broadcast([P, 1024 // (2 * half), 2 * half])
                pool.tensor_tensor(Dbuf[(n + 1) % 3].rearrange("p (b r) -> p b r", r=2 * half), b4, mid,
                                   ALU.subtract).then_inc(s["diff_ready"], 1)

            for n in range(NB):
                if n == 6:
                    pool.wait_ge(s["b_ready"], 1)
                    for m in range(3):
                        level_diff(0, m)
                pool.wait_ge(s["s_new"], NH * (n + 1))
                pool.dma_start(hgrn_sample[0, n].rearrange("h k v -> k h v"),
                               state_slot(n)).then_inc(s["s_out"], 16)
                if n + 4 < NB:
                    pool.wait_ge(s["s_out"], 16 * (n + 1))
                    pool.wait_ge(s["so_out"], n + 1)
                    s0_load(n + 4)
            def gain_in(n, g):
                pool.dma_start(gains[n][0:N1, :], g[0, :].partition_broadcast(N1)).then_inc(s["gvec_in"], 16)

            pool.wait_ge(s["proj_out"], 16 + TT)
            gain_in(0, g_post_mix)
            gain_in(1, g_pre_ffn)
            pool.wait_ge(s["s_out"], 16 * NB)
            pool.wait_ge(s["so_out"], NB)
            pool.dma_start(mm[0:N1, :, :].rearrange("r a n -> r (a n)"),
                           b_ada[0, 2048:6144].partition_broadcast(N1)).then_inc(s["in_bada"], 16)
            for hp in range(2):
                for n in range(3 if hp == 0 else 0, 7):
                    if hp == 1 and n == 0:
                        pool.wait_ge(s["b_ready"], 2)
                        pool.wait_ge(s["kh_turned"], 1)
                    if hp == 1 and n == 1:
                        pool.wait_ge(s["o_done"], 1)
                        pool.wait_ge(s["o_out"], 1)
                    level_diff(hp, n)
                if hp == 1:
                    pool.wait_ge(s["modrow_ready"], 1)
                    gain_in(2, g_post_ffn)
                pool.wait_ge(s["s_ready"], 8 * (hp + 1))
                pool.dma_start(hgrn_prompt[0, 0, 2 * hp:2 * hp + 2].rearrange("h k v -> k h v"),
                               Sb[:, :, 3, :]).then_inc(s["hstate_out"], 16)
            for j in range(TT):
                pool.wait_ge(s["h2_ready"], j + 1)
                pool.dma_start(h2_rows[j * P:j * P + ROWS[j], :], h2buf[0:ROWS[j], j % 4, :]).then_inc(s["h2_stored"], 16)
                pool.wait_ge(s["h2_stored"], 16 * (j + 1))
            pool.wait_ge(s["h2_turned"], TT)
            chain(pool.memset(xg[:, :, :], 0.0))

            def waits_stand_alone():
                pool.sem_inc(s["pool_passed"], 1)

            def gather(e, r4, par):
                pool.wait_ge(s["idx_ready"], e + 1)
                waits_stand_alone()
                pool.indirect_dma_start(xg[:, par, :], None, h2_rows,
                                        bass.IndirectOffsetOnAxis(ap=gidx[:, r4:r4 + 1], axis=0),
                                        bounds_check=NT - 1, oob_is_err=False).then_inc(s[f"gathered{par}"], 16)

            def scatter(n, r4, par):
                pool.wait_ge(s["y_a"], n + 1)
                pool.wait_ge(s["y_d"], n + 1)
                waits_stand_alone()
                pool.indirect_dma_start(ff_rows, bass.IndirectOffsetOnAxis(ap=sidx[:, r4:r4 + 1], axis=0),
                                        ybuf[:, par, :], None, bounds_check=NT - 1, oob_is_err=False,
                                        compute_op=ALU.add).then_inc(s["scattered"], 16)

            gather(0, 0, 0)
            gather(1, 1, 1)
            pool.wait_ge(s["x_turned2"], 1)
            gather(2, 2, 0)

            def step(e, r, first=False):
                pool.wait_ge(s["x_turned2"], e + 2)
                gather(e + 3, (r + 3) % 4, (r + 1) % 2)
                if not first:
                    if not isinstance(e, int) or e > 1:
                        pool.wait_ge(s["scattered"], (e - 1) * 16)
                    scatter(e + (TT - 1), (r + 3) % 4, r % 2)

            step(0, 0, first=True)
            pool.wait_ge(s["ff_init0"], 16 * 3)
            pool.wait_ge(s["ff_init1"], 16 * 2)
            for e in range(1, 4):
                step(e, e)
            with pool.Fori(1, NE // 4) as i:
                for r in range(4):
                    step(i * 4 + r, r)
            turns = pool.value_load(table_i[0:1, TAB:TAB + 1], min_val=1, max_val=MAX_TURNS)
            with pool.Fori(0, turns) as i:
                for r in range(4):
                    step(i * 4 + (NE + r), r)
            pool.wait_ge(s["scattered"], turns * 64 + 16 * (NE - 1))
            scatter(turns * 4 + (TT + NE - 1), 3, 0)
            pool.wait_ge(s["scattered"], turns * 64 + 16 * NE)
            pool.wait_ge(s["gathered0"], turns * 32 + 16 * (NE // 2 + 1))
            pool.wait_ge(s["gathered1"], turns * 32 + 16 * (NE // 2 + 1))
            pool.wait_ge(s["x_turned2"], turns * 4 + NE + 1)
            pool.sem_inc(s["adds_done"], 1)
            for j in range(TT):
                pool.wait_ge(s["scaled"], j + 1)
                pool.tensor_tensor(fin[0:ROWS[j], j, :], fin[0:ROWS[j], j, :], xrows(j), ALU.add).then_inc(s["out_ready"], 1)

        @block.scalar
        def _(act):
            act.wait_ge(s["in_c"], 32)
            act.activation(cs[0:N1, :], cs[0:N1, :], ACT.Silu).then_inc(s["c_silu"], 1)
            act.wait_ge(s["in_x"], 48)
            act.wait_ge(s["consts_dve"], 1)
            for j in range(TT):
                if j >= 1:
                    act.wait_ge(s["sq_ready"], j)
                act.activation(junk[0:ROWS[j], :], xrows(j), ACT.Square,
                               accum_out=ss[0:ROWS[j], j:j + 1]).then_inc(s["sq_ready"], 1)
            act.wait_ge(s["ms_ready"], 1)
            act.activation(rstd, ss, ACT.Sqrt).then_inc(s["rms_sqrt"], 1)
            act.wait_ge(s["rstd_ready"], 1)
            def normed(j):
                act.activation(xn[j % 2][0:ROWS[j], :], xrows(j), ACT.Copy,
                               scale=rstd[0:ROWS[j], j:j + 1]).then_inc(s["xn_ready"], 1)

            normed(0)
            normed(1)
            for j in range(TT):
                act.wait_ge(s["x_turned"], j + 1)
                if j + 2 < TT:
                    normed(j + 2)
                act.activation(actT[:, 0:4, j * P:j * P + ROWS[j]],
                               ps[:, 2 * (j % 2), :].rearrange("p (k n) -> p k n", k=4)[:, :, 0:ROWS[j]],
                               ACT.Copy).then_inc(s["x_evac_a"], 1)
            act.wait_ge(s["m1T_ready"], 1)
            act.wait_ge(s["x_evac_a"], TT)
            for k in range(2):
                act.activation(actT[:, k, 0:T], actT[:, k, 0:T], ACT.Identity, scale=a1T[:, k, NB:N1],
                               bias=b1T[:, k, NB:N1]).then_inc(s["mod_a"], 1)

            act.wait_ge(s["lb_diff"], 1)
            act.activation(lbt[:, 0:2 * NH], lbt[:, 0:2 * NH], ACT.Exp).then_inc(s["lb_exp"], 1)

            def two_halves(h):
                return pair(h)[:, :, 0:HALF]

            for n, (dst, func) in enumerate(((f, ACT.Sigmoid), (q, ACT.Silu))):
                for h in range(NH):
                    act.wait_ge(s["proj_out"], 4 + 4 * n + h + 1)
                    act.activation(dst[:, h, :].rearrange("p (a t) -> p a t", a=2), two_halves(h),
                                   func).then_inc(s["proj_a"], 1)
            def pool_save(g):
                act.wait_ge(s["pool_y"], g + 1)
                act.activation(u[:, g, 0:NT].rearrange("p (a t) -> p a t", a=2), ypool_ps, ACT.Copy,
                               scale=vecT[:, 8 + g:9 + g]).then_inc(s["pool_saved"], 1)

            for j in range(TT):
                act.wait_ge(s["proj_out"], 12 + j + 1)
                if j == PT:
                    for g in range(4):
                        last = act.activation(v[0:NB, j, g * P:(g + 1) * P], quarter(NB, j, g), ACT.Copy)
                else:
                    last = act.activation(v[:, j, :], ps[:, j, :], ACT.Copy)
                last.then_inc(s["proj_a"], 1)
                if j == 3:
                    pool_save(0)
            pool_save(1)

            def logs(hp):
                if hp == 1:
                    act.wait_ge(s["qd_exp"], 1)
                    act.wait_ge(s["d_last"], 1)
                act.activation(b.rearrange("p (h t) -> p h t", h=2), f[:, 2 * hp:2 * hp + 2, 0:T],
                               ACT.Ln).then_inc(s["ln_done"], 1)

            def level_exp(hp, n):
                act.wait_ge(s["diff_ready"], 7 * hp + n + 1)
                d4 = Dbuf[(n + 1) % 3].rearrange("p (b h r) -> p b h r", h=2, r=LEVELS[n])
                act.activation(d4[:, :, 1, :], d4[:, :, 1, :], ACT.Exp)
                act.activation(d4[:, :, 0, :], d4[:, :, 0, :], ACT.Exp, scale=-1.0).then_inc(s["exp_done"], 1)

            act.wait_ge(s["f_ready"], NH)
            for h in range(NH):
                for n in (2 * h, 2 * h + 1):
                    act.wait_ge(s["s0_in"], 16 * 4 if n < 4 else 16 * NB if n >= 6 else 16 * 6)
                    st = state_slot(n)
                    for h2 in range(NH):
                        act.activation(st[:, h2, :], st[:, h2, :], ACT.Copy, scale=f[:, h2, T + n:T + n + 1]
                                       ).then_inc(s["s0_dec"], 1)
                if h == 0:
                    pool_save(2)
                    pool_save(3)
                if h == 2:
                    logs(0)
                act.wait_ge(s["proj_out"], 12 + TT + h + 1)
                act.activation(gate[:, h, :].rearrange("p (a t) -> p a t", a=2), two_halves(h % 2),
                               ACT.Silu).then_inc(s["proj_a"], 1)
            def sample_norm():
                act.wait_ge(s["so_out"], NB)
                act.activation(tmpS[:, 0:32], so_ps, ACT.Square).then_inc(s["so_sq"], 1)
                act.wait_ge(s["so_ms"], 1)
                act.activation(tmpS[:, 32:64], sms_ps, ACT.Ln, bias=eps_c, scale=1.0 / P).then_inc(s["act_chain"], 1)
                act.wait_ge(s["act_chain"], 1)
                act.activation(tmpS[:, 64:96], tmpS[:, 32:64], ACT.Exp, scale=-0.5).then_inc(s["so_r"], 1)

            for hp in range(2):
                for n in range(hp, 7):
                    level_exp(hp, n)
                    if hp == 0 and n == 0:
                        sample_norm()
                act.wait_ge(s["level_out"], 8 * hp + 8)
                act.activation(Dbuf[0], b, ACT.Exp).then_inc(s["qd_exp"], 1)
                act.activation(dl, b.rearrange("p (c t) -> p c t", t=P)[:, :, P - 1], ACT.Exp).then_inc(s["d_last"], 1)
                act.wait_ge(s["kh_diff"], hp + 1)
                act.activation(Dbuf[1], Dbuf[1], ACT.Exp).then_inc(s["kh_exp"], 1)
                if hp == 0:
                    logs(1)
                act.wait_ge(s["kh_turned"], hp + 1)
                act.activation(khT.rearrange("p (a n) -> p a n", a=2), pair(3), ACT.Copy).then_inc(s["khT_ready"], 1)
                act.wait_ge(s["o_out"], hp + 1)
                act.activation(khT.rearrange("p (a n) -> p a n", a=2), pair(1), ACT.Square).then_inc(s["o_sq"], 1)
                act.wait_ge(s["o_ms"], hp + 1)
                act.activation(khT.rearrange("p (a n) -> p a n", a=2), pair(3), ACT.Ln, bias=eps_c, scale=1.0 / P).then_inc(s["act_chain"], 1)
                act.wait_ge(s["act_chain"], hp + 2)
                act.activation(khT, khT, ACT.Exp, scale=-0.5).then_inc(s["o_r"], 1)
                if hp == 0:
                    level_exp(1, 0)
            def squares(j):
                R = ROWS[j]
                act.wait_ge(s["mix_out"], j + 1)
                if j == PT:
                    for g in range(4):
                        last = act.activation(mix_sample[:, :, g * P:(g + 1) * P],
                                              mix_ps(j)[32 * g:32 * g + NB, :, g * P:(g + 1) * P], ACT.Copy)
                    last.then_inc(s["mix_saved"], 1)
                    act.wait_ge(s["mix_saved"], 1)
                act.activation(ybuf[0:R, 1, :].rearrange("p (a n) -> p a n", a=2), mix_in(j), ACT.Square,
                               accum_out=ss[0:R, j:j + 1]).then_inc(s["mix_sq"], 1)
                act.wait_ge(s["mix_sqrt"], 2 * j + 1)
                act.activation(rstd[0:R, j:j + 1], ss[0:R, j:j + 1], ACT.Sqrt).then_inc(s["mix_rstd"], 1)
                act.wait_ge(s["x1_ready"], j + 1)
                act.activation(ybuf[0:R, 1, :], xrows(j), ACT.Square, accum_out=ss[0:R, j:j + 1]
                               ).then_inc(s["x1_sq"], 1)
                act.wait_ge(s["mix_sqrt"], 2 * j + 2)
                act.activation(rstd[0:R, j:j + 1], ss[0:R, j:j + 1], ACT.Sqrt).then_inc(s["x1_rstd"], 1)

            def h2T_half(j):
                act.wait_ge(s["h2_turned"], j + 1)
                act.activation(actT[:, 0:4, j * P:j * P + ROWS[j]],
                               ps[:, 5, :].rearrange("p (k n) -> p k n", k=4)[:, :, 0:ROWS[j]], ACT.Copy
                               ).then_inc(s["h2T_a"], 1)

            squares(0)
            squares(1)
            h2T_half(0)
            squares(2)
            h2T_half(1)
            squares(3)
            h2T_half(2)
            squares(4)
            h2T_half(3)
            h2T_half(4)
            act.wait_ge(s["logit_out"], TT)
            act.wait_ge(s["scores_set"], 1)
            act.activation(scores[:, 0:PT, :], logit_ps[:, 0:PT, :], ACT.Sigmoid)
            act.activation(scores[0:NB, PT, :], logit_ps[0:NB, PT, :], ACT.Sigmoid).then_inc(s["score_ready"], 1)

            def silu(n, par, R=P, bank=None):
                act.wait_ge(s["up_done"], n + 1)
                if bank is not None:
                    act.wait_ge(s["glu_done"], n - 1)
                if R == NB:
                    for g in range(2):
                        last = act.activation(sg[0:NB, par, g * P:(g + 1) * P], quarter(NB, 4 + par, g), ACT.Silu)
                else:
                    last = act.activation(sg[:, par, :], ps[:, 4 + par if bank is None else bank, 0:FE], ACT.Silu)
                last.then_inc(s["silu_done"], 1)

            def xT_half(e, par):
                act.wait_ge(s["x_turned2"], e + 1)
                act.activation(xT[:, par, 0:4, :], ps[:, 0, :].rearrange("p (k n) -> p k n", k=4), ACT.Copy
                               ).then_inc(s["xT_a"], 1)

            def y_half(n, par, R=P):
                act.wait_ge(s["down_done"], n + 1)
                if R == NB:
                    for g in range(2):
                        last = act.activation(ybuf[0:NB, par, 256 * g:256 * (g + 1)], down_quarter(g), ACT.Copy)
                else:
                    last = act.activation(ybuf[:, par, 0:512], ps[:, 2, :], ACT.Copy)
                last.then_inc(s["y_a"], 1)

            def hhT_all(n, par, R=P):
                act.wait_ge(s["hh_turned"], n + 1)
                act.activation(hhT[:, par, :, 0:R], ps[:, 6, 0:256].rearrange("p (k n) -> p k n", k=2)[:, :, 0:R],
                               ACT.Copy).then_inc(s["hhT_ready"], 1)

            for n in range(TT):
                silu(n, n % 2, ROWS[n], bank=SHARED_BANK.get(n))
                if n >= 1:
                    if n >= 3:
                        act.wait_ge(s[f"ff_init{(n - 1) % 2}"], 16 * ((n - 1) // 2))
                    y_half(n - 1, (n - 1) % 2, ROWS[n - 1])
                    act.wait_ge(s["y_a"], n)
                    act.wait_ge(s["y_d"], n)
                    act.dma_start(ff_rows[(n - 1) * P:n * P, :], ybuf[:, (n - 1) % 2, :]
                                  ).then_inc(s[f"ff_init{(n - 1) % 2}"], 16)
                if n == TT - 1:
                    xT_half(0, 0)
                hhT_all(n, n % 2, ROWS[n])

            def step(e, r, first=False):
                n = e + TT
                silu(n, (r + 1) % 2)
                xT_half(e + 1, (r + 1) % 2)
                y_half(n - 1, r % 2, NB if first else P)
                if first:
                    act.wait_ge(s["y_a"], TT)
                    act.wait_ge(s["y_d"], TT)
                    act.dma_start(ff_rows[PT * P:NT, :], ybuf[0:NB, r % 2, :]).then_inc(s["ff_init0"], 16)
                hhT_all(n, (r + 1) % 2)

            act.wait_ge(s["ff_init0"], 16 * 2)
            step(0, 0, first=True)
            act.wait_ge(s["ff_init1"], 16 * 2)
            step(1, 1)
            act.wait_ge(s["ff_init0"], 16 * 3)
            step(2, 2)
            act.wait_ge(s["scattered"], 16)
            step(3, 3)
            with act.Fori(1, NE // 4) as i:
                for r in range(4):
                    e = i * 4 + r
                    act.wait_ge(s["scattered"], (e - 2) * 16)
                    step(e, r)
            turns = act.value_load(table_i[0:1, TAB:TAB + 1], min_val=1, max_val=MAX_TURNS)
            with act.Fori(0, turns) as i:
                for r in range(4):
                    e = i * 4 + (NE + r)
                    act.wait_ge(s["scattered"], (e - 2) * 16)
                    step(e, r)
            act.wait_ge(s["scattered"], turns * 64 + 16 * (NE - 2))
            y_half(turns * 4 + (TT + NE - 1), 0)
            def ff_square(j):
                R = ROWS[j]
                act.wait_ge(s[f"ff_in{j}"], 16)
                if j >= 1:
                    act.wait_ge(s["ff_sq"], j)
                act.activation(fin_junk[0:R, :], fin[0:R, j, :], ACT.Square, accum_out=ss[0:R, j:j + 1]
                               ).then_inc(s["ff_sq"], 1)

            ff_square(0)
            for j in range(TT):
                R = ROWS[j]
                if 1 <= j < TT - 1:
                    ff_square(j + 1)
                act.wait_ge(s["ff_sqrt"], j + 1)
                act.activation(rstd[0:R, j:j + 1], ss[0:R, j:j + 1], ACT.Sqrt).then_inc(s["ff_rstd"], 1)
                if j == 0:
                    ff_square(1)

        @block.tensor
        def _(pe):
            pe.wait_ge(s["consts_pool"], 1)
            pe.wait_ge(s["c_silu"], 1)
            for k in range(KC):
                mt = pe.transpose(ps[:, 7, k * N1:(k + 1) * N1], cs[0:N1, k::KC], ident[0:N1, 0:N1])
            mt.then_inc(s["pe_cT"], 1)

            def ada_products(n, p, k):
                for j in range(4):
                    mt = pe.matmul(ada_ps(n, j), cT[:, k, :], ringA_k(p % 4)[:, k, j * P:(j + 1) * P],
                                   start=k == 0, stop=k == KC - 1)
                return mt

            def ada(n, p):
                arrived_a(pe, p)
                if n >= 2:
                    pe.wait_ge(s["ada_saved"], n - 1)
                for k in range(KC):
                    mt = ada_products(n, p, k)
                mt.then_inc(s["ada_out"], 1)

            pe.wait_ge(s["cT_ready"], 1)
            ada(0, 0)
            ada(1, 1)
            for j in range(TT):
                pe.wait_ge(s["xn_ready"], j + 1)
                if j >= 2:
                    pe.wait_ge(s["x_evac_a"], j - 1)
                    pe.wait_ge(s["x_evac_d"], j - 1)
                for k in range(KC):
                    R = ROWS[j]
                    mt = pe.transpose(ps[:, 2 * (j % 2) + k // 4, (k % 4) * P:(k % 4) * P + R],
                                      xn[j % 2][0:R, k::KC], ident[0:R, 0:R])
                mt.then_inc(s["x_turned"], 1)
            ada(2, 2)
            for n in range(2):
                if n == 1:
                    ada(3, 3)
                pe.wait_ge(s["ada_saved"], 2 * n + 2)
                for k in range(KC):
                    mt = pe.transpose(ps[:, 7, 144 + (n * KC + k) * N1:144 + (n * KC + k + 1) * N1],
                                      m1[0:N1, n * D + k:(n + 1) * D:KC], ident[0:N1, 0:N1])
                mt.then_inc(s["m1_turned"], 1)
            pe.wait_ge(s["in_small"], 128)
            pe.transpose(ps[:, 6, 480:493], tmpS[0:13, 0:P], ident[0:13, 0:13])
            for g in range(4):
                mt = pe.transpose(ps[:, 6, NB * HIST * g:NB * HIST * (g + 1)], hraw[0:NB * HIST, g * P:(g + 1) * P],
                                  ident[0:NB * HIST, 0:NB * HIST])
            mt.then_inc(s["hist_turned"], 1)

            def spread_v(n):
                if n == 0:
                    pe.wait_ge(s["proj_a"], 8 + TT)
                if n == 1:
                    pe.wait_ge(s["rows_saved"], 1)
                if n >= 2:
                    pe.wait_ge(s["s_new"], NH * (n - 1))
                pe.matmul(ps[:, 4 + n % 2, :], ident[0:NB, n:n + 1].to_broadcast([NB, P]), v[0:NB, PT, :],
                          start=True, stop=True).then_inc(s["vb_out"], 1)

            def read_state(n):
                pe.wait_ge(s["s_new"], NH * (n + 1))
                for h in range(NH):
                    mt = pe.matmul(ps[:, 6, h * NB + n:h * NB + n + 1], state_slot(n)[:, h, :],
                                   q[:, h, T + n:T + n + 1], start=True, stop=True)
                mt.then_inc(s["so_out"], 1)

            def pool_mix(g):
                pe.wait_ge(s["pool_d"], g + 1)
                if g >= 1:
                    pe.wait_ge(s["pool_saved"], g)
                for half in range(2):
                    mt = pe.matmul(ypool_ps[:, half, :], wpool[:, g, :], diffs[:, g, half * HALF:(half + 1) * HALF],
                                   start=True, stop=True)
                mt.then_inc(s["pool_y"], 1)

            for n in range(5):
                p = 4 + n
                arrived_a(pe, p)
                w = ringA_k(p % 4)
                if n == 3:
                    for j in range(TT):
                        if j % 2 == 0:
                            pe.wait_ge(s["proj_a"], 4 + j // 2 + 1)
                        for k in range(KC):
                            if j == PT:
                                for g in range(4):
                                    mt = pe.matmul(quarter(NB, j, g), actT[:, k, T:NT], w[:, k, g * P:(g + 1) * P],
                                                   start=k == 0, stop=k == KC - 1)
                            else:
                                mt = pe.matmul(ps[:, j, :], actT[:, k, j * P:(j + 1) * P], w[:, k, :],
                                               start=k == 0, stop=k == KC - 1)
                        mt.then_inc(s["proj_out"], 1)
                        if j == 3:
                            pe.wait_ge(s["proj_a"], 8)
                            for g in range(4):
                                mt = pe.transpose(ps[0:HIST + NB, 5, g * P:(g + 1) * P], u[:, g, T:UW], ident[:, :])
                            mt.then_inc(s["rows_turned"], 1)
                            pool_mix(0)
                    pool_mix(1)
                else:
                    for h in range(NH):
                        if n == 0 and h == 0:
                            pe.wait_ge(s["x_evac_a"], TT)
                            pe.wait_ge(s["x_evac_d"], TT)
                        if n == 0 and h == 3:
                            pe.wait_ge(s["hist_ready"], 1)
                            pe.wait_ge(s["m1T_ready"], 1)
                        if n == 1:
                            pe.wait_ge(s["u_ready"], h + 1)
                        if n == 2:
                            pe.wait_ge(s["proj_a"], h + 1)
                        bank = 2 * h
                        if n == 4:
                            bank = 2 * (h % 2)
                            pe.wait_ge(s["proj_a"], 8 + (2, 4, TT + 1, TT + 2)[h])
                            spread_v(2 * h)
                            spread_v(2 * h + 1)
                        for half in range(2):
                            for k in range(KC):
                                if (n, h, half) == (0, 0, 0):
                                    k = (2, 3, 0, 4, 5, 1, 6, 7)[k]
                                    if k < 2:
                                        pe.wait_ge(s["mod_a"], k + 1)
                                    else:
                                        pe.wait_ge(s["mod_d"], k - 1)
                                if (n, h, half, k) == (0, 0, 1, 0):
                                    pe.wait_ge(s["mod_d"], KC - 1)
                                mt = pe.matmul(ps[:, bank + half, 0:HALF], w[:, k, h * P:(h + 1) * P],
                                               actT[:, k, half * HALF:(half + 1) * HALF],
                                               start=k == (2 if (n, h, half) == (0, 0, 0) else 0), stop=k == KC - 1)
                            if n == 4 and h == 0:
                                if half == 1:
                                    mt.then_inc(s["proj_out"], 1)
                                pool_mix(2 + half)
                        if n < 4 or h > 0:
                            mt.then_inc(s["proj_out"], 1)
                        if n == 4:
                            if h == 0:
                                pe.wait_ge(s["pool_saved"], 4)
                            read_state(2 * h)
                            read_state(2 * h + 1)
            filled = [0]

            def fill(count):
                for _ in range(count):
                    n, k = 4 + filled[0] // KC, filled[0] % KC
                    if k == 0:
                        arrived_a(pe, n + 5)
                        pe.wait_ge(s["ada_saved"], n - 1)
                    mt = ada_products(n, n + 5, k)
                    if k == KC - 1:
                        mt.then_inc(s["ada_out"], 1)
                    filled[0] += 1

            def project_half(j, half, ks):
                for k in ks:
                    left = (u if k < 4 else actT)[:, k, j * P:j * P + ROWS[j]]
                    if j == PT:
                        for g in range(4):
                            mt = pe.matmul(mix_ps(j)[32 * g:32 * g + NB, half, g * P:(g + 1) * P], left,
                                           ringA_k((A_OUT + half) % 4)[:, k, g * P:(g + 1) * P],
                                           start=k == 0, stop=k == KC - 1)
                        continue
                    mt = pe.matmul(mix_ps(j)[0:ROWS[j], half, :], left, ringA_k((A_OUT + half) % 4)[:, k, :],
                                   start=k == 0, stop=k == KC - 1)
                return mt

            for hp in range(2):
                for n in range(8):
                    g = 8 * hp + n
                    if g == 0:
                        pe.wait_ge(s["kk_ready"], 1)
                        pe.wait_ge(s["proj_a"], 11 + TT)
                    if g == 1:
                        pe.wait_ge(s["proj_a"], 12 + TT)
                    if n == 0 and hp == 1:
                        fill(16)
                        pe.wait_ge(s["kk_ready"], 2)
                    if n == 1 and hp == 1:
                        pe.wait_ge(s["o_done"], 1)
                    if n >= 1:
                        pe.wait_ge(s["x_level"], 7 * hp + n)
                    if g >= 2:
                        pe.wait_ge(s["level_used"], g - 1)
                    for h in range(2):
                        for c in range(PT):
                            if n == 0:
                                left = kk[:, h, c * P:(c + 1) * P]
                                right = q[:, 2 * hp + h, c * P:(c + 1) * P]
                            else:
                                left = right = Dbuf[n % 3][:, h * T + c * P:h * T + (c + 1) * P]
                            mt = pe.matmul(ps[:, 2 * (n % 2) + h, c * P:(c + 1) * P], left, right, start=True, stop=True)
                    mt.then_inc(s["level_out"], 1)
                    if g == 0:
                        pe.wait_ge(s["so_sq"], 1)
                        pe.matmul(ps[:, 7, 0:32], ones[:, :], tmpS[:, 0:32], start=True, stop=True
                                  ).then_inc(s["so_ms"], 1)
                    fill(FILL[hp][n])
                if hp == 1:
                    arrived_a(pe, A_OUT)
                    arrived_a(pe, A_OUT + 1)
                    pe.wait_ge(s["ada_saved"], 12)
                    project_half(0, 0, range(4))
                pe.wait_ge(s["kh_ready"], hp + 1)
                if hp == 0:
                    pe.wait_ge(s["so_done"], 1)
                for hc in range(8):
                    mt = pe.transpose(ps[:, 6 + hc // 4, (hc % 4) * P:(hc % 4 + 1) * P], Dbuf[1][:, hc * P:(hc + 1) * P],
                                      ident[:, :])
                mt.then_inc(s["kh_turned"], 1)
                if hp == 1:
                    project_half(0, 1, range(2))
                pe.wait_ge(s["khT_ready"], hp + 1)
                pe.wait_ge(s["level_used"], 8 * hp + 8)
                for h in range(2):
                    for c in range(PT):
                        mt = pe.matmul(ps[:, h, c * P:(c + 1) * P], khT[:, (4 * h + c) * P:(4 * h + c + 1) * P],
                                       v[:, c, (2 * hp + h) * P:(2 * hp + h + 1) * P], start=True, stop=True)
                mt.then_inc(s["upd_out"], 1)
                if hp == 1:
                    project_half(0, 1, range(2, 4))
                pe.wait_ge(s["qd_ready"], hp + 1)
                pe.wait_ge(s["s_ready"], 8 * (hp + 1))
                for h in range(2):
                    for c in range(PT):
                        out = ps[:, 2 + h, c * P:(c + 1) * P]
                        mt = pe.matmul(out, v[:, c, (2 * hp + h) * P:(2 * hp + h + 1) * P], att[:, 4 * h + c, :],
                                       start=True, stop=c == 0)
                        if c >= 1:
                            mt = pe.matmul(out, Sb[:, h, c - 1, :], Dbuf[0][:, (4 * h + c) * P:(4 * h + c + 1) * P],
                                           start=False, stop=True)
                mt.then_inc(s["o_out"], 1)
                pe.wait_ge(s["o_sq"], hp + 1)
                for h in range(2):
                    mt = pe.matmul(ps[:, 6 + h, :], ones[:, :], khT[:, h * T:(h + 1) * T], start=True, stop=True)
                mt.then_inc(s["o_ms"], 1)
            def project_out(j, first=0):
                if j >= 3:
                    pe.wait_ge(s["x1_ready"], j - 1)
                for half in range(2):
                    mt = project_half(j, half, range(first, KC))
                mt.then_inc(s["mix_out"], 1)

            def turn_h2(j):
                R = ROWS[j]
                if j == 0:
                    pe.wait_ge(s["x1_ready"], 1)
                pe.wait_ge(s["h2_ready"], j + 1)
                if j >= 1:
                    pe.wait_ge(s["h2T_a"], j)
                    pe.wait_ge(s["h2T_d"], j)
                for k in range(KC):
                    mt = pe.transpose(ps[:, 5 + k // 4, (k % 4) * P:(k % 4) * P + R], h2buf[0:R, j % 4, k::KC],
                                      ident[0:R, 0:R])
                mt.then_inc(s["h2_turned"], 1)

            def route(j):
                R = ROWS[j]
                pe.wait_ge(s["h2T_a"], j + 1)
                pe.wait_ge(s["h2T_d"], j + 1)
                for k in range(KC):
                    mt = pe.matmul(ps[0:R, 7, j * NE:(j + 1) * NE], actT[:, k, j * P:j * P + R], wrt[:, k, :],
                                   start=k == 0, stop=k == KC - 1)
                mt.then_inc(s["logit_out"], 1)

            def up(n, par, left, slot, R=P, bank=None):
                if n_static(n, 2) and bank is None:
                    pe.wait_ge(s["glu_done"], n - 1)
                for k in range(KC):
                    if R == NB:
                        for g in range(4):
                            mt = pe.matmul(quarter(NB, 4 + par, g), left(k),
                                           ringA_gu(slot)[:, g // 2, k, (g % 2) * P:(g % 2 + 1) * P],
                                           start=k == 0, stop=k == KC - 1)
                        continue
                    mt = pe.matmul(ps[:, 4 + par if bank is None else bank, :].rearrange("p (a n) -> p a n", a=2), left(k),
                                   ringA_gu(slot)[:, :, k, :], start=k == 0, stop=k == KC - 1)
                mt.then_inc(s["up_done"], 1)

            def n_static(n, least):
                return not isinstance(n, int) or n >= least

            def down(n, par, slot, R=P):
                pe.wait_ge(s["hhT_ready"], n + 1)
                if n_static(n, 1):
                    pe.wait_ge(s["y_a"], n)
                    pe.wait_ge(s["y_d"], n)
                if R == NB:
                    for k in range(2):
                        for g in range(4):
                            mt = pe.matmul(down_quarter(g), hhT[:, par, k, 0:NB], ringB_k(slot)[:, k, 256 * g:256 * (g + 1)],
                                           start=k == 0, stop=k == 1)
                for half in range(2 if R == P else 0):
                    for k in range(2):
                        mt = pe.matmul(ps[:, 2 + half, :], hhT[:, par, k, :],
                                       ringB_k(slot)[:, k, half * 512:(half + 1) * 512], start=k == 0, stop=k == 1)
                mt.then_inc(s["down_done"], 1)

            def turn_hh(n, par, R=P):
                pe.wait_ge(s["glu_done"], n + 1)
                if n_static(n, 1):
                    pe.wait_ge(s["hhT_ready"], n)
                for k in range(2):
                    mt = pe.transpose(ps[:, 6, k * P:k * P + R], hh[0:R, par, k::2], ident[0:R, 0:R])
                mt.then_inc(s["hh_turned"], 1)

            def turn_x(e, par, gathers):
                pe.wait_ge(s[f"gathered{par}"], gathers)
                if n_static(e, 1):
                    pe.wait_ge(s["xT_a"], e)
                    pe.wait_ge(s["xT_d"], e)
                for k in range(KC):
                    mt = pe.transpose(ps[:, k // 4, (k % 4) * P:(k % 4 + 1) * P], xg[:, par, k::KC], ident[:, :])
                mt.then_inc(s["x_turned2"], 1)

            def dispatch(e, tok):
                pe.wait_ge(s["onehot_ready"], e + 1)
                if n_static(e, 1):
                    pe.wait_ge(s["idx_ready"], e)
                for j in range(TT):
                    mt = pe.matmul(ps[:, 7, 0:6], onehot[:, j, :], tok(j), start=j == 0, stop=j == TT - 1)
                mt.then_inc(s["disp_out"], 1)

            def tok_static(e):
                return lambda j: tokw[:, e, j, :]

            def shared_up(n):
                if n == 0:
                    arrived_a(pe, A_SHARED)
                up(n, n % 2, lambda k: actT[:, k, n * P:n * P + ROWS[n]], A_SHARED % 4, ROWS[n],
                   bank=SHARED_BANK.get(n))

            for half in range(2):
                project_half(1, half, range(4))
            pe.wait_ge(s["o_done"], 2)
            project_out(0, first=4)
            project_out(1, first=4)
            project_out(2)
            turn_h2(0)
            project_out(3)
            turn_h2(1)
            route(0)
            project_out(4)
            turn_h2(2)
            route(1)
            turn_h2(3)
            route(2)
            shared_up(0)
            turn_h2(4)
            route(3)
            route(4)
            pe.wait_ge(s["h2T_a"], TT)
            shared_up(1)
            shared_up(2)
            pe.wait_ge(s["route_m"], 1)
            for j in range(TT):
                for j2 in range(j + 1):
                    mt = pe.matmul(ps[:, 7, j * NE:(j + 1) * NE], tri[:, :] if j2 == j else ones[:, :],
                                   route_mask[:, j2, :], start=j2 == 0, stop=j2 == j)
            for j in range(TT):
                mt = pe.matmul(ps[0:NE, 7, 320:321], route_mask[:, j, :], ones[:, 0:1], start=j == 0, stop=j == TT - 1)
            mt.then_inc(s["pos_out"], 1)
            turn_hh(0, 0)
            pe.wait_ge(s["ringB_in0"], 16)
            down(0, 0, 0)
            turn_hh(1, 1)
            for n in range(2, TT):
                if n > 2:
                    shared_up(n)
                down(n - 1, (n - 1) % 2, 0)
                if n == 2:
                    pe.wait_ge(s["cnt_out"], 1)
                    pe.matmul(ps[0:NE, 0, 328:329], tri[0:NE, 0:NE], tabn, start=True, stop=True)
                    pe.matmul(ps[:, 0, 336:337], ones[0:NE, :], tabn, start=True, stop=True).then_inc(s["table_in"], 1)
                if n == 3:
                    pe.wait_ge(s["cnt_out"], 2)
                    pe.matmul(ps[:, 0, 352:352 + 2 * TAB], ones[0:NE, :], tabrows[0:NE, :], start=True, stop=True
                              ).then_inc(s["table_out"], 1)
                if n == TT - 1:
                    pe.wait_ge(s["table_ready"], 1)
                    turn_x(0, 0, 16)
                dispatch(n - 2, tok_static(n - 2))
                turn_hh(n, n % 2, ROWS[n])

            def tok_at(e):
                return lambda j: tokw[:, bass.ds(e, 1), j, :].rearrange("p e n -> p (e n)")

            def step(e, r, g, nxt, first=False):
                n = e + TT
                pe.wait_ge(s["xT_a"], e + 1)
                pe.wait_ge(s["xT_d"], e + 1)
                in_a(r, g)
                up(n, (r + 1) % 2, lambda k: xT[:, r % 2, k, :], r)
                turn_x(e + 1, (r + 1) % 2, g * 32 + 16 * ((r + 1) // 2 + 1))
                dispatch(e + 3, tok_static(nxt) if isinstance(nxt, int) else tok_at(nxt))
                in_b(r, g)
                down(n - 1, r % 2, r % 4, NB if first else P)
                turn_hh(n, (r + 1) % 2)

            def in_a(r, g):
                pe.wait_ge(s[f"ringA_in{r}"], g * 32 + 32 * 6)

            def in_b(r, g):
                pe.wait_ge(s[f"ringB_in{r}"], g * 16 + 16)

            def extra_expert(n):
                return pe.value_load(table_i[0:1, n:n + 1] if isinstance(n, int) else table_i[0:1, bass.ds(n, 1)],
                                     min_val=0, max_val=NE - 1)

            for r in range(4):
                step(r, r, 0, r + 3, first=r == 0)
            with pe.Fori(1, NE // 4 - 1) as i:
                for r in range(4):
                    step(i * 4 + r, r, i, i * 4 + (r + 3))
            for r in range(4):
                step(NE - 4 + r, r, NE // 4 - 1, NE - 1 if r == 0 else extra_expert(r - 1))
            turns = pe.value_load(table_i[0:1, TAB:TAB + 1], min_val=1, max_val=MAX_TURNS)
            with pe.Fori(0, turns) as i:
                for r in range(4):
                    nxt = extra_expert(i * 4 + (r + 3))
                    step(i * 4 + (NE + r), r, i + NE // 4, nxt)
            in_b(0, turns + NE // 4)
            down(turns * 4 + (TT + NE - 1), 0, 0)

        @block.vector
        def _(dve):
            chain = Chain(dve, s["dve_chain"])
            dve.memset(ones[:, :], 1.0)
            dve.memset(eps_c, EPS)
            dve.memset(ss, 1.0).then_inc(s["consts_dve"], 1)
            dve.wait_ge(s["pe_cT"], 1)
            dve.tensor_copy(cT, ps[:, 7, 0:KC * N1].rearrange("p (k r) -> p k r", k=KC)).then_inc(s["cT_ready"], 1)

            def ada_save(n, p, dst):
                dve.wait_ge(s["ada_out"], n + 1)
                for j in range(4):
                    part = dst[:, j * P:(j + 1) * P]
                    last = dve.tensor_tensor(part, ada_ps(n, j), part, ALU.add)
                last.then_inc(s["ada_saved"], 1)

            def first_ada(n):
                ada_save(n, n, m1[0:N1, 512 * n:512 * n + 512])

            dve.wait_ge(s["in_x"], 48)
            first_ada(0)
            dve.wait_ge(s["consts_pool"], 2)
            chain(dve.tensor_scalar(valid, trash1, float(TRASH + 1 + NB), None, ALU.is_lt))
            dve.reciprocal(icnt, icnt).then_inc(s["consts_dve"], 1)
            dve.wait_ge(s["sq_ready"], TT)
            dve.tensor_scalar(ss, ss, 1.0 / D, EPS, ALU.mult, ALU.add).then_inc(s["ms_ready"], 1)
            dve.wait_ge(s["rms_sqrt"], 1)
            dve.reciprocal(rstd, rstd).then_inc(s["rstd_ready"], 1)
            first_ada(1)
            for j in range(TT):
                dve.wait_ge(s["x_turned"], j + 1)
                dve.tensor_copy(actT[:, 4:8, j * P:j * P + ROWS[j]],
                                ps[:, 2 * (j % 2) + 1, :].rearrange("p (k n) -> p k n", k=4)[:, :, 0:ROWS[j]]
                                ).then_inc(s["x_evac_d"], 1)
            first_ada(2)
            m1T = ps[:, 7, 144:144 + 2 * KC * N1].rearrange("p (a k r) -> p a k r", a=2, k=KC)
            dve.wait_ge(s["m1_turned"], 1)
            dve.tensor_copy(b1T, m1T[:, 0])
            first_ada(3)
            dve.wait_ge(s["in_small"], 128)
            dve.wait_ge(s["m1_turned"], 2)
            chain(dve.tensor_scalar(a1T, m1T[:, 1], 1.0, None, ALU.add))
            chain(dve.tensor_tensor(a1T, a1T, gpre.unsqueeze(2).to_broadcast([P, KC, N1]), ALU.mult))
            dve.sem_inc(s["m1T_ready"], 1)
            dve.wait_ge(s["x_evac_d"], TT)
            dve.wait_ge(s["x_evac_a"], TT)
            for k in range(2, KC):
                dve.tensor_scalar(actT[:, k, 0:T], actT[:, k, 0:T], a1T[:, k, NB:N1], b1T[:, k, NB:N1], ALU.mult, ALU.add
                                  ).then_inc(s["mod_d"], 1)
            chain(dve.tensor_tensor(actT[:, :, T:NT], actT[:, :, T:NT], a1T[:, :, 0:NB], ALU.mult))
            dve.tensor_tensor(actT[:, :, T:NT], actT[:, :, T:NT], b1T[:, :, 0:NB], ALU.add).then_inc(s["mod_d"], 1)
            dve.wait_ge(s["hist_turned"], 1)
            dve.tensor_copy(vecT, ps[:, 6, 480:493])
            chain(dve.tensor_copy(histT, ps[:, 6, 0:4 * NB * HIST].rearrange("p (g b r) -> p g b r", g=4, b=NB)))
            for g, w in enumerate(WINDOWS):
                last = dve.tensor_reduce(tmpS[:, 256 + NB * g:256 + NB * g + NB], histT[:, g, :, HIST - (w - 1):HIST],
                                         AX.X, ALU.add)
            last.then_inc(s["hist_ready"], 1)
            chain(dve.tensor_tensor(lbt[:, 8:12], vecT[:, 0:4], vecT[:, 4:8], ALU.max))
            dve.tensor_tensor(lbt[:, 0:4], vecT[:, 0:4], lbt[:, 8:12], ALU.subtract)
            dve.tensor_tensor(lbt[:, 4:8], vecT[:, 4:8], lbt[:, 8:12], ALU.subtract).then_inc(s["lb_diff"], 1)
            dve.wait_ge(s["lb_exp"], 1)
            chain(dve.tensor_tensor(lbt[:, 8:12], lbt[:, 0:4], lbt[:, 4:8], ALU.add))
            chain(dve.reciprocal(lbt[:, 8:12], lbt[:, 8:12]))
            chain(dve.tensor_tensor(lb, lbt[:, 0:4], lbt[:, 8:12], ALU.mult))
            chain(dve.tensor_scalar(oml, lb, -1.0, 1.0, ALU.mult, ALU.add))

            for g in range(4):
                if g == 0:
                    dve.memset(u[:, :, 0:HIST], 0.0)
                dve.wait_ge(s["proj_out"], g + 1)
                dve.tensor_copy(u[:, g, HIST:UW].rearrange("p (a t) -> p a t", a=2), pair(g)[:, :, 0:HALF]
                                ).then_inc(s["u_ready"], 1)
            for h in range(NH):
                dve.wait_ge(s["proj_a"], h + 1)
                dve.tensor_scalar(f[:, h, :], f[:, h, :], oml[:, h:h + 1], lb[:, h:h + 1], ALU.mult, ALU.add
                                  ).then_inc(s["f_ready"], 1)
            dve.wait_ge(s["f_ready"], 4)
            chain(dve.tensor_scalar(kS, f[:, :, T:NT], -1.0, 1.0, ALU.mult, ALU.add))
            dve.wait_ge(s["rows_turned"], 1)
            dve.tensor_copy(u_rows[0:HIST + NB, :], ps[0:HIST + NB, 5, :]).then_inc(s["rows_saved"], 1)
            def keys(hp):
                if hp == 0:
                    dve.wait_ge(s["pool_y"], 4)
                dve.tensor_scalar(kk, f[:, 2 * hp:2 * hp + 2, :], -1.0, 1.0, ALU.mult, ALU.add).then_inc(s["kk_ready"], 1)
                dve.wait_ge(s["kk_ready"], hp + 1)

            def decays(hp):
                dve.wait_ge(s["ln_done"], hp + 1)
                for c in range(8):
                    last = dve.tensor_tensor_scan(b[:, c * P:(c + 1) * P], ones[:, :], b[:, c * P:(c + 1) * P],
                                                  0.0, ALU.mult, ALU.add)
                last.then_inc(s["b_ready"], 1)
                dve.wait_ge(s["b_ready"], hp + 1)

            for n in range(NB):
                if n == 4:
                    keys(0)
                if n == 6:
                    decays(0)
                dve.wait_ge(s["vb_out"], n + 1)
                dve.wait_ge(s["s0_dec"], NH * (n + 1))
                st = state_slot(n)
                for h in range(NH):
                    dve.scalar_tensor_tensor(st[:, h, :], ps[:, 4 + n % 2, h * P:(h + 1) * P], kS[:, h, n:n + 1],
                                             st[:, h, :], ALU.mult, ALU.add).then_inc(s["s_new"], 1)
            def sample_out():
                dve.wait_ge(s["so_sq"], 1)
                dve.wait_ge(s["proj_a"], 12 + TT)
                oS = actT[:, 4:8, T:NT]
                chain(dve.scalar_tensor_tensor(oS, so_ps.rearrange("p (h b) -> p h b", h=NH), vecT[:, 12:13],
                                               gate[:, :, T:NT], ALU.mult, ALU.mult))
                dve.wait_ge(s["so_r"], 1)
                chain(dve.tensor_tensor(oS, oS, tmpS[:, 64:96].rearrange("p (h b) -> p h b", h=NH), ALU.mult))
                dve.sem_inc(s["so_done"], 1)

            def more_ada(n):
                ada_save(n, n + 5, mm[0:N1, (n - 4) // 2, 512 * (n % 2):512 * (n % 2) + 512])

            for hp in range(2):
                hs = slice(2 * hp, 2 * hp + 2)
                chain(dve.memset(att, 0.0))

                def times(n):
                    half = LEVELS[n]
                    dve.wait_ge(s["exp_done"], 7 * hp + n + 1)
                    for side, src in ((1, q[:, hs, 0:T]), (0, kk[:, :, 0:T])):
                        d4 = Dbuf[(n + 1) % 3].rearrange("p (x h r) -> p x h r", h=2, r=half)[:, :, side, :]
                        s4 = src.rearrange("p a (x h r) -> p a x h r", h=2, r=half)[:, :, :, side, :]
                        last = dve.tensor_tensor(d4.rearrange("p (a x) r -> p a x r", a=2), d4.rearrange("p (a x) r -> p a x r", a=2),
                                                 s4, ALU.mult)
                    last.then_inc(s["x_level"], 1)

                def keep(n):
                    dve.wait_ge(s["level_out"], 8 * hp + n + 1)
                    if n >= 1:
                        dve.wait_ge(s["level_used"], 8 * hp + n)
                    dve.copy_predicated(att, masks[:, n, :].unsqueeze(1).to_broadcast([P, 8, P]),
                                        pair(n % 2).rearrange("p a (c i) -> p (a c) i", i=P)
                                        ).then_inc(s["level_used"], 1)

                dve.wait_ge(s["consts_pool"], 3)
                for n in range(7):
                    times(n)
                    if (hp, n) == (0, 0):
                        sample_out()
                        dve.wait_ge(s["in_bada"], 16)
                    for piece in FILLED.get((hp, n), ()):
                        more_ada(piece)
                    keep(n)
                keep(7)
                last_b = b.rearrange("p (c t) -> p c t", t=P)[:, :, P - 1:P].to_broadcast([P, 8, P])
                dve.tensor_tensor(Dbuf[1].rearrange("p (c t) -> p c t", t=P), last_b,
                                  b.rearrange("p (c t) -> p c t", t=P), ALU.subtract).then_inc(s["kh_diff"], 1)
                dve.wait_ge(s["qd_exp"], hp + 1)
                dve.tensor_tensor(Dbuf[0].rearrange("p (h t) -> p h t", h=2), Dbuf[0].rearrange("p (h t) -> p h t", h=2),
                                  q[:, hs, 0:T], ALU.mult).then_inc(s["qd_ready"], 1)
                dve.wait_ge(s["kh_exp"], hp + 1)
                dve.tensor_tensor(Dbuf[1].rearrange("p (h t) -> p h t", h=2), Dbuf[1].rearrange("p (h t) -> p h t", h=2),
                                  kk[:, :, 0:T], ALU.mult).then_inc(s["kh_ready"], 1)
                if hp == 0:
                    dve.wait_ge(s["kh_ready"], 1)
                    dve.wait_ge(s["level_out"], 8)
                    keys(1)
                    decays(1)
                    more_ada(6)
                    more_ada(7)
                dve.wait_ge(s["upd_out"], hp + 1)
                dve.wait_ge(s["d_last"], hp + 1)
                if hp == 1:
                    dve.wait_ge(s["hstate_out"], 16)
                for c in range(PT):
                    for h in range(2):
                        upd = ps[:, h, c * P:(c + 1) * P]
                        if c == 0:
                            dve.tensor_copy(Sb[:, h, 0, :], upd).then_inc(s["s_ready"], 1)
                        else:
                            dve.wait_ge(s["s_ready"], 8 * hp + 2 * c - 1 + h)
                            dve.scalar_tensor_tensor(Sb[:, h, c, :], Sb[:, h, c - 1, :], dl[:, 4 * h + c:4 * h + c + 1], upd,
                                                     ALU.mult, ALU.add).then_inc(s["s_ready"], 1)
                dve.wait_ge(s["gvec_in"], 32 + 16 * hp)
                if hp == 0:
                    dve.wait_ge(s["ada_saved"], 6)
                    dve.tensor_tensor(mm[0:N1, 0, :], mm[0:N1, 0, :], gains[0][0:N1, :], ALU.mult).then_inc(s["modrow_ready"], 1)
                else:
                    dve.wait_ge(s["ada_saved"], 12)
                    chain(dve.tensor_scalar(mm[0:N1, 2, :], mm[0:N1, 2, :], 1.0, None, ALU.add))
                    for n, g in ((2, 1), (3, 2)):
                        dve.tensor_tensor(mm[0:N1, n, :], mm[0:N1, n, :], gains[g][0:N1, :], ALU.mult
                                          ).then_inc(s["modrow_ready"], 1)
                dve.wait_ge(s["o_sq"], hp + 1)
                oT = actT[:, 4 + 2 * hp:6 + 2 * hp, 0:T]
                chain(dve.scalar_tensor_tensor(oT, pair(1), vecT[:, 12:13], gate[:, hs, 0:T], ALU.mult, ALU.mult))
                dve.wait_ge(s["o_r"], hp + 1)
                dve.tensor_tensor(oT, oT, khT.rearrange("p (h t) -> p h t", h=2), ALU.mult).then_inc(s["o_done"], 1)

            def rows_of(j):
                return [modb[:, n, :] if j < PT else mm[0:ROWS[j], n, :] for n in range(4)]

            def residual(j):
                R = ROWS[j]
                dve.wait_ge(s["mix_sq"], j + 1)
                dve.tensor_scalar(ss[0:R, j:j + 1], ss[0:R, j:j + 1], 1.0 / D, EPS, ALU.mult, ALU.add
                                  ).then_inc(s["mix_sqrt"], 1)
                dve.wait_ge(s["mix_rstd"], j + 1)
                chain(dve.reciprocal(rstd[0:R, j:j + 1], rstd[0:R, j:j + 1]))
                if j == 0:
                    dve.wait_ge(s["modb_in0"], 16)
                mixed = ybuf[0:R, 0, :]
                chain(dve.scalar_tensor_tensor(mixed.rearrange("p (a n) -> p a n", a=2), mix_in(j),
                                               rstd[0:R, j:j + 1], rows_of(j)[0].rearrange("p (a n) -> p a n", a=2),
                                               ALU.mult, ALU.mult))
                dve.tensor_tensor(xrows(j), xrows(j), mixed, ALU.add).then_inc(s["x1_ready"], 1)

            def normed2(j):
                R = ROWS[j]
                dve.wait_ge(s["x1_sq"], j + 1)
                dve.tensor_scalar(ss[0:R, j:j + 1], ss[0:R, j:j + 1], 1.0 / D, EPS, ALU.mult, ALU.add
                                  ).then_inc(s["mix_sqrt"], 1)
                dve.wait_ge(s["x1_rstd"], j + 1)
                chain(dve.reciprocal(rstd[0:R, j:j + 1], rstd[0:R, j:j + 1]))
                if j == 0:
                    dve.wait_ge(s["modb_in1"], 16)
                if j >= 4:
                    dve.wait_ge(s["h2_stored"], 16 * (j - 3))
                    dve.wait_ge(s["h2_turned"], j - 3)
                h2 = h2buf[0:R, j % 4, :]
                chain(dve.scalar_tensor_tensor(h2, xrows(j), rstd[0:R, j:j + 1], rows_of(j)[2], ALU.mult, ALU.mult))
                dve.tensor_tensor(h2, h2, rows_of(j)[1], ALU.add).then_inc(s["h2_ready"], 1)

            def h2T_half(j):
                dve.wait_ge(s["h2_turned"], j + 1)
                dve.tensor_copy(actT[:, 4:8, j * P:j * P + ROWS[j]],
                                ps[:, 6, :].rearrange("p (k n) -> p k n", k=4)[:, :, 0:ROWS[j]]).then_inc(s["h2T_d"], 1)

            for j in range(TT):
                residual(j)
                normed2(j)
                if 1 <= j < 4:
                    h2T_half(j - 1)
            h2T_half(3)
            h2T_half(4)

            def pick(e, posm_at, offset=None):
                for j in range(TT):
                    if offset is None:
                        last = dve.tensor_scalar(onehot[:, j, :], iota[:, :], posm_at(j), None, ALU.is_equal)
                    else:
                        last = dve.tensor_scalar(onehot[:, j, :], iota[:, :], offset, posm_at(j), ALU.add, ALU.is_equal)
                last.then_inc(s["onehot_ready"], 1)

            def index(e, r4):
                dve.wait_ge(s["disp_out"], e + 1)
                sums = slot_sums[:, r4, :]
                chain(dve.tensor_reduce(sums, ps[:, 7, 0:6].rearrange("p (a n) -> p a n", a=2), AX.X, ALU.add))
                chain(dve.tensor_scalar(idx_f[:, 0:1], sums[:, 0:1], 0.0, None, ALU.is_equal))
                chain(dve.scalar_tensor_tensor(idx_f[:, 1:2], idx_f[:, 0:1], trash1, sums[:, 0:1], ALU.mult, ALU.add))
                dve.tensor_scalar(gidx[:, r4:r4 + 1], idx_f[:, 1:2], -1.0, None, ALU.add).then_inc(s["idx_ready"], 1)

            def posm_static(e):
                return lambda j: posm[:, e, j:j + 1]

            def posm_dyn(e):
                return lambda j: posm[:, bass.ds(e, 1), j:j + 1].rearrange("p e n -> p (e n)")

            def glu(n, par, weight, R=P, bank=None):
                dve.wait_ge(s["silu_done"], n + 1)
                if bank is not None:
                    dve.wait_ge(s["hh_turned"], n - 1)
                if R == NB:
                    for g in range(2):
                        cols = slice(g * P, (g + 1) * P)
                        last = dve.tensor_tensor(hh[0:NB, par, cols], sg[0:NB, par, cols], quarter(NB, 4 + par, 2 + g),
                                                 ALU.mult)
                else:
                    last = dve.scalar_tensor_tensor(hh[:, par, :], sg[:, par, :], weight,
                                                    ps[:, 4 + par if bank is None else bank, FE:2 * FE],
                                                    ALU.mult, ALU.mult)
                last.then_inc(s["glu_done"], 1)

            def xT_half(e, par):
                dve.wait_ge(s["x_turned2"], e + 1)
                dve.tensor_copy(xT[:, par, 4:8, :], ps[:, 1, :].rearrange("p (k n) -> p k n", k=4)
                                ).then_inc(s["xT_d"], 1)

            def y_half(n, par, R=P):
                dve.wait_ge(s["down_done"], n + 1)
                if R == NB:
                    for g in range(2, 4):
                        last = dve.tensor_copy(ybuf[0:NB, par, 256 * g:256 * (g + 1)], down_quarter(g))
                else:
                    last = dve.tensor_copy(ybuf[:, par, 512:1024], ps[:, 3, :])
                last.then_inc(s["y_d"], 1)

            dve.wait_ge(s["h2_ready"], TT)
            chain(dve.memset(scores, 1.0))
            dve.memset(tabrows, 0.0).then_inc(s["scores_set"], 1)
            dve.wait_ge(s["score_ready"], 1)
            chain(dve.tensor_tensor(sel, scores, rbias[:, :].unsqueeze(1).to_broadcast([P, TT, NE]), ALU.add))
            for j in range(TT):
                for g in range(8):
                    last = dve.max(sorted8[:, j, g, :], sel[:, j, 8 * g:8 * g + 8])
            chain(last)
            chain(dve.tensor_tensor(gsc, sorted8[:, :, :, 0], sorted8[:, :, :, 1], ALU.add))
            other = gsc.unsqueeze(2).to_broadcast([P, TT, 8, 8])
            this = gsc.unsqueeze(3).to_broadcast([P, TT, 8, 8])
            dve.tensor_tensor(cmp1.rearrange("p j (a b) -> p j a b", a=8), other, this, ALU.is_gt)
            chain(dve.tensor_tensor(cmp2.rearrange("p j (a b) -> p j a b", a=8), other, this, ALU.is_equal))
            chain(dve.tensor_tensor(cmp2, cmp2, lower8.unsqueeze(1).to_broadcast([P, TT, NE]), ALU.mult))
            chain(dve.tensor_tensor(cmp1, cmp1, cmp2, ALU.add))
            chain(dve.tensor_reduce(grank, cmp1.rearrange("p j (a b) -> p j a b", a=8), AX.X, ALU.add))
            chain(dve.tensor_scalar(gmask, grank, 3.5, None, ALU.is_lt))
            chain(dve.tensor_scalar(gpen, gmask, 1e30, -1e30, ALU.mult, ALU.add))
            g4 = sel.rearrange("p j (a b) -> p j a b", a=8)
            chain(dve.tensor_tensor(g4, g4, gmask.unsqueeze(3).to_broadcast([P, TT, 8, 8]), ALU.mult))
            chain(dve.tensor_tensor(g4, g4, gpen.unsqueeze(3).to_broadcast([P, TT, 8, 8]), ALU.add))
            for j in range(TT):
                last = dve.max(top8[:, j, :], sel[:, j, :])
            chain(last)
            v8 = top8[:, :, 7:8].to_broadcast([P, TT, NE])
            dve.tensor_tensor(cmp1, sel, v8, ALU.is_gt)
            chain(dve.tensor_tensor(cmp2, sel, v8, ALU.is_equal))
            for j in range(TT):
                last = dve.tensor_tensor_scan(route_mask[:, j, :], ones[:, 0:NE], cmp2[:, j, :], 0.0, ALU.mult, ALU.add)
            chain(last)
            chain(dve.tensor_reduce(grank[:, :, 0], cmp1, AX.X, ALU.add))
            chain(dve.tensor_scalar(grank[:, :, 0], grank[:, :, 0], -1.0, TOP_K + 0.5, ALU.mult, ALU.add))
            chain(dve.tensor_tensor(route_mask, route_mask, grank[:, :, 0:1].to_broadcast([P, TT, NE]), ALU.is_lt))
            chain(dve.tensor_tensor(route_mask, route_mask, cmp2, ALU.mult))
            chain(dve.tensor_tensor(route_mask, route_mask, cmp1, ALU.add))
            chain(dve.tensor_tensor(scores, scores, route_mask, ALU.mult))
            chain(dve.tensor_scalar(route_mask[:, PT, :], route_mask[:, PT, :], valid, None, ALU.mult))
            dve.sem_inc(s["route_m"], 1)
            glu(0, 0, 1.0)
            chain(dve.tensor_reduce(grank[:, :, 1], scores, AX.X, ALU.add))
            chain(dve.reciprocal(grank[:, :, 1], grank[:, :, 1]))
            chain(dve.tensor_scalar(grank[:, :, 1], grank[:, :, 1], ROUTED_SCALE, None, ALU.mult))
            chain(dve.tensor_tensor(scores, scores, grank[:, :, 1:2].to_broadcast([P, TT, NE]), ALU.mult))
            for n in range(3):
                part = tokw[:, :, :, 3 + n].rearrange("p e j -> p j e")
                chain(dve.tensor_copy(part, scores))
                if n < 2:
                    chain(dve.tensor_tensor(scores, scores, part, ALU.subtract))
            dve.wait_ge(s["pos_out"], 1)
            pos = ps[:, 7, 0:TT * NE].rearrange("p (j e) -> p j e", j=TT)
            chain(dve.scalar_tensor_tensor(sel, pos, 1.0, route_mask, ALU.add, ALU.mult))
            chain(dve.tensor_scalar(posm[:, :, :].rearrange("p e j -> p j e"), sel, -1.0, None, ALU.add))
            cnt = ps[0:NE, 7, 320:321]
            for j in range(4):
                last = dve.tensor_scalar(tabi[:, j:j + 1], cnt, float(P * (j + 1)), None, ALU.is_gt)
            chain(last)
            chain(dve.tensor_reduce(tabn, tabi, AX.X, ALU.add))
            dve.sem_inc(s["cnt_out"], 1)
            pick(0, posm_static(0))
            glu(1, 1, 1.0)
            y_half(0, 0)
            glu(2, 0, 1.0, bank=SHARED_BANK[2])
            y_half(1, 1)
            dve.wait_ge(s["table_in"], 1)
            chain(dve.tensor_scalar(tabd[:, 0:1], ps[0:NE, 0, 328:329], 0.0, None, ALU.add))
            chain(dve.tensor_copy(tabd[:, 1:2], trash1[0:NE, :]))
            chain(dve.tensor_scalar(tabd[:, 1:2], tabd[:, 1:2], -float(TRASH + 1), None, ALU.add))
            for j in range(4):
                chain(dve.tensor_scalar(tab1, iota[0:NE, 0:TAB], tabd[:, 0:1], tabi[:, j:j + 1], ALU.is_equal, ALU.mult))
                chain(dve.scalar_tensor_tensor(tabrows[0:NE, 0:TAB], tab1, tabd[:, 1:2], tabrows[0:NE, 0:TAB], ALU.mult, ALU.add))
                chain(dve.scalar_tensor_tensor(tabrows[0:NE, TAB:2 * TAB], tab1, NEVER - P * (j + 1), tabrows[0:NE, TAB:2 * TAB],
                                               ALU.mult, ALU.add))
                chain(dve.tensor_scalar(tabd[:, 0:1], tabd[:, 0:1], 1.0, None, ALU.add))
            dve.sem_inc(s["cnt_out"], 1)
            index(0, 0)
            pick(1, posm_static(1))
            glu(3, 1, 1.0)
            dve.wait_ge(s["ff_init0"], 16)
            y_half(2, 0)
            dve.wait_ge(s["table_out"], 1)
            dve.tensor_copy(table_i[:, 0:TAB], ps[:, 0, 352:352 + TAB])
            dve.tensor_scalar(tabq, ps[:, 0, 352 + TAB:352 + 2 * TAB], -1.0, NEVER, ALU.mult, ALU.add)
            chain(dve.tensor_scalar(turns8, iota[:, 0:8], 4.0, None, ALU.mult))
            chain(dve.tensor_scalar(turns8, turns8, ps[:, 0, 336:337], None, ALU.is_lt))
            chain(dve.tensor_reduce(qneg, turns8, AX.X, ALU.add))
            chain(dve.tensor_scalar(table_i[:, TAB:TAB + 1], qneg, 1.0, None, ALU.max))
            dve.sem_inc(s["table_ready"], 1)
            index(1, 1)
            pick(2, posm_static(2))
            glu(4, 0, 1.0, NB)
            dve.wait_ge(s["ff_init1"], 16)
            y_half(3, 1)
            xT_half(0, 0)
            index(2, 2)
            pick(3, posm_static(3))

            LINKS = 3

            def extra_block(n):
                at = slice(n, n + 1) if isinstance(n, int) else bass.ds(n, 1)
                e = dve.value_load(table_i[0:1, at], min_val=0, max_val=NE - 1)
                pick(e, posm_dyn(e), offset=tabq[:, at])

            def step(e, r, nxt, first=False):
                n = e + TT
                xT_half(e + 1, (r + 1) % 2)
                glu(n, (r + 1) % 2, slot_sums[:, r, 1:2])
                dve.tensor_copy(sidx[:, r:r + 1], gidx[:, r:r + 1])
                index(e + 3, (r + 3) % 4)
                nxt()
                if not isinstance(e, int) or e > 2:
                    dve.wait_ge(s["scattered"], (e - 2) * 16)
                y_half(n - 1, r % 2, NB if first else P)

            def expert(e):
                return lambda: pick(e, posm_static(e) if isinstance(e, int) else posm_dyn(e))

            dve.wait_ge(s["ff_init0"], 16 * 2)
            step(0, 0, expert(4), first=True)
            dve.wait_ge(s["ff_init1"], 16 * 2)
            step(1, 1, expert(5))
            dve.wait_ge(s["ff_init0"], 16 * 3)
            step(2, 2, expert(6))
            step(3, 3, expert(7))
            before = chain.count
            with dve.Fori(1, NE // 4 - 1) as i:
                for r in range(4):
                    chain.base, chain.count = (i - 1) * (4 * LINKS) + before, LINKS * r
                    step(i * 4 + r, r, expert(i * 4 + (r + 4)))
            chain.base, chain.count = 0, before + LINKS * (NE - 8)
            for r in range(4):
                step(NE - 4 + r, r, lambda: extra_block(r))
            before = chain.count
            turns = dve.value_load(table_i[0:1, TAB:TAB + 1], min_val=1, max_val=MAX_TURNS)
            with dve.Fori(0, turns) as i:
                for r in range(4):
                    chain.base, chain.count = i * (4 * LINKS) + before, LINKS * r
                    step(i * 4 + (NE + r), r, lambda: extra_block(i * 4 + (r + 4)))
            dve.wait_ge(s["scattered"], turns * 64 + 16 * (NE - 2))
            y_half(turns * 4 + (TT + NE - 1), 0)
            dve.wait_ge(s["xT_d"], turns * 4 + (NE + 1))
            dve.sem_inc(s["ff_ready"], 1)
            for j in range(TT):
                R = ROWS[j]
                g2 = modb[:, 3, :] if j < PT else mm[0:R, 3, :]
                dve.wait_ge(s["ff_sq"], j + 1)
                dve.tensor_scalar(ss[0:R, j:j + 1], ss[0:R, j:j + 1], 1.0 / D, EPS, ALU.mult, ALU.add
                                  ).then_inc(s["ff_sqrt"], 1)
                dve.wait_ge(s["ff_rstd"], j + 1)
                if j == 0:
                    chain.base, chain.count = turns * (4 * LINKS) + before, 0
                chain(dve.reciprocal(rstd[0:R, j:j + 1], rstd[0:R, j:j + 1]))
                out = fin[0:R, j, :]
                dve.scalar_tensor_tensor(out, out, rstd[0:R, j:j + 1], g2, ALU.mult, ALU.mult).then_inc(s["scaled"], 1)


_INS = ["x_prompt", "x_sample", "c_prompt", "c_sample", "state_pool", "state_hgrn", "w_ada", "b_ada", "g_pre_mix",
        "g_post_mix", "w_in", "w_pool", "pool_scale", "lb_logits", "g_out_norm", "w_out", "g_pre_ffn", "g_post_ffn",
        "w_router", "router_bias", "w_exp_gate", "w_exp_up", "w_exp_down", "w_sh_gate", "w_sh_up", "w_sh_down"]
_OUTS = [(1, 512, 1024), (8, 1, 1024), (1, 1, 15, 512), (1, 1, 4, 128, 128), (1, 8, 15, 512), (1, 8, 4, 128, 128)]


def kernel(**inputs):
    import numpy as np
    import concourse.bacc as bacc
    from concourse.bass_utils import run_bass_kernel_spmd

    nc = bacc.Bacc("TRN2", target_bir_lowering=False, num_devices=1)
    arrays, args = {}, []
    for name in _INS:
        a = np.ascontiguousarray(inputs[name])
        arrays[f"in_{name}"] = a
        args.append(nc.dram_tensor(f"in_{name}", a.shape, mybir.dt.from_np(a.dtype), kind="ExternalInput").ap())
    for n, shape in enumerate(_OUTS):
        args.append(nc.dram_tensor(f"out_{n}", shape, F32, kind="ExternalOutput").ap())
    args.append(nc.dram_tensor("h2_rows", (520, 1024), F32).ap())
    args.append(nc.dram_tensor("ff_rows", (520, 1024), F32).ap())
    args.append(nc.dram_tensor("mod_rows", (4096,), F32).ap())
    build(nc, *args)
    r = run_bass_kernel_spmd(nc, [arrays], core_ids=[0])
    return tuple(r.results[0][f"out_{n}"] for n in range(len(_OUTS)))
```
